# Optimizing a Trainium2 kernel written in Bass

```python
import jax, jax.numpy as jnp
from jax import lax
import numpy as np
import math
import jax
import jax.numpy as jnp

D_MODEL = 1024
BATCH = 1
SEQ = 256
DEPTH = 2

D_MIX = D_MODEL
N_GROUPS = 4
GROUP_WIDTH = D_MIX // N_GROUPS
HEAD_DIM = 64
N_HEADS_GROUP = GROUP_WIDTH // HEAD_DIM
CONF_KERNEL = 31
SHORT_KERNEL = 3
FFN_KERNEL = 3
D_FF = 2816
BLOCK_Q = 128
RET_CHUNK = 128
ROPE_BASE = 10000.0
NORM_EPS = 1e-6
N_IN_SLICES = 12
D_IN = N_IN_SLICES * GROUP_WIDTH


def rms_norm(x, g):
    xf = x.astype(jnp.float32)
    y = xf * lax.rsqrt(jnp.mean(xf * xf, axis=-1, keepdims=True) + NORM_EPS)
    return (y * g.astype(jnp.float32)).astype(x.dtype)

def layer_norm(x, g, b):
    xf = x.astype(jnp.float32)
    mu = jnp.mean(xf, axis=-1, keepdims=True)
    xc = xf - mu
    y = xc * lax.rsqrt(jnp.mean(xc * xc, axis=-1, keepdims=True) + NORM_EPS)
    return (y * g.astype(jnp.float32) + b.astype(jnp.float32)).astype(x.dtype)

def causal_dwconv(x, w):
    k_w, c = w.shape
    return lax.conv_general_dilated(
        x, w[:, None, :].astype(x.dtype), window_strides=(1,), padding=[(k_w - 1, 0)],
        dimension_numbers=('NWC', 'WIO', 'NWC'), feature_group_count=c)

def split_heads(x):
    b, t, _ = x.shape
    return x.reshape(b, t, -1, HEAD_DIM).transpose(0, 2, 1, 3)

def merge_heads(x):
    b, h, t, d = x.shape
    return x.transpose(0, 2, 1, 3).reshape(b, t, h * d)

def rotary(x, pos):
    d = x.shape[-1]
    half = d // 2
    inv_freq = ROPE_BASE ** (-jnp.arange(0, d, 2, dtype=jnp.float32) / d)
    ang = pos.astype(jnp.float32)[:, None] * inv_freq[None, :]
    cos, sin = jnp.cos(ang), jnp.sin(ang)
    xf = x.astype(jnp.float32)
    x1, x2 = xf[..., :half], xf[..., half:]
    return jnp.concatenate([x1 * cos - x2 * sin, x2 * cos + x1 * sin], axis=-1)

def conformer_conv(a, gate, dw_w, dw_b, ln_g, ln_b):
    h = a * jax.nn.sigmoid(gate)
    h = causal_dwconv(h, dw_w) + dw_b.astype(h.dtype)
    return jax.nn.silu(layer_norm(h, ln_g, ln_b))

def stick_breaking_attention(q, k, v):
    b, h, t, d = q.shape
    n_blocks = t // BLOCK_Q
    scale = d ** -0.5
    kf = k.astype(jnp.float32)
    key_pos = jnp.arange(t)
    qb = q.reshape(b, h, n_blocks, BLOCK_Q, d).transpose(2, 0, 1, 3, 4)

    def block(args):
        qi, i = args
        z = jnp.einsum('bhqd,bhkd->bhqk', qi.astype(jnp.float32), kf) * scale
        q_pos = i * BLOCK_Q + jnp.arange(BLOCK_Q)
        mask = key_pos[None, :] < q_pos[:, None]
        log_1m_beta = jnp.where(mask, -jax.nn.softplus(z), 0.0)
        tail = lax.cumsum(log_1m_beta, axis=3, reverse=True) - log_1m_beta
        attn = jnp.where(mask, jnp.exp(jax.nn.log_sigmoid(z) + tail), 0.0)
        return jnp.einsum('bhqk,bhkd->bhqd', attn.astype(v.dtype), v)

    out = lax.map(block, (qb, jnp.arange(n_blocks)))
    return out.transpose(1, 2, 0, 3, 4).reshape(b, h, t, d)

def retention_chunkwise(q, k, v):
    b, h, t, d = q.shape
    n_chunks = t // RET_CHUNK
    log_gamma = jnp.log1p(-jnp.exp2(-5.0 - jnp.arange(h, dtype=jnp.float32)))
    idx = jnp.arange(RET_CHUNK, dtype=jnp.float32)
    diff = idx[:, None] - idx[None, :]
    causal = diff >= 0
    d_intra = jnp.where(causal[None], jnp.exp(jnp.where(causal, diff, 0.0)[None] * log_gamma[:, None, None]), 0.0)
    q_decay = jnp.exp((idx[None, :] + 1.0) * log_gamma[:, None])
    k_decay = jnp.exp((RET_CHUNK - 1.0 - idx[None, :]) * log_gamma[:, None])
    chunk_decay = jnp.exp(RET_CHUNK * log_gamma)
    k = k * (d ** -0.5)

    def to_chunks(z):
        return z.reshape(b, h, n_chunks, RET_CHUNK, d).transpose(2, 0, 1, 3, 4)

    def step(state, inp):
        qc, kc, vc = inp
        inner = jnp.einsum('bhqd,bhkd->bhqk', qc, kc) * d_intra
        o = jnp.einsum('bhqk,bhkd->bhqd', inner, vc) + jnp.einsum('bhqd,bhde->bhqe', qc, state) * q_decay[..., None]
        state = state * chunk_decay[:, None, None] + jnp.einsum('bhkd,bhke->bhde', kc * k_decay[..., None], vc)
        return state, o

    state0 = jnp.zeros((b, h, d, d), jnp.float32)
    _, out = lax.scan(step, state0, (to_chunks(q), to_chunks(k), to_chunks(v)))
    return out.transpose(1, 2, 0, 3, 4).reshape(b, h, t, d)

def retention_mixer(q, k, v, g, norm_g):
    t = q.shape[1]
    pos = jnp.arange(t)
    qh = rotary(split_heads(q), pos)
    kh = rotary(split_heads(k), pos)
    vh = split_heads(v).astype(jnp.float32)
    o = retention_chunkwise(qh, kh, vh)
    mu = jnp.mean(o, axis=-1, keepdims=True)
    oc = o - mu
    o = oc * lax.rsqrt(jnp.mean(oc * oc, axis=-1, keepdims=True) + NORM_EPS)
    y = merge_heads(o) * norm_g.astype(jnp.float32)
    return (jax.nn.silu(g.astype(jnp.float32)) * y).astype(q.dtype)

def short_gated_conv(b_gate, c_gate, h, conv_w):
    return b_gate * causal_dwconv(c_gate * h, conv_w)

def conv_ffn(x, w_up, w_conv, w_down):
    h = causal_dwconv(x @ w_up, w_conv)
    gate, up = jnp.split(h, 2, axis=-1)
    return (jax.nn.silu(gate) * up) @ w_down

def first_inputs(seed: int = 0) -> dict:
    key = jax.random.key(seed)
    ks = jax.random.split(key, 16)
    f32 = jnp.float32

    def nrm(k, shape, scale):
        return jax.random.normal(k, shape, f32) * scale

    def gain(k, shape):
        return 1.0 + 0.05 * jax.random.normal(k, shape, f32)

    return {
        'x': nrm(ks[0], (BATCH, SEQ, D_MODEL), 1.0),
        'norm_mix_pre': gain(ks[1], (DEPTH, D_MODEL)),
        'norm_mix_post': gain(ks[2], (DEPTH, D_MODEL)),
        'norm_ffn_pre': gain(ks[3], (DEPTH, D_MODEL)),
        'norm_ffn_post': gain(ks[4], (DEPTH, D_MODEL)),
        'w_in': nrm(ks[5], (DEPTH, D_MODEL, D_IN), D_MODEL ** -0.5),
        'conf_dw_w': nrm(ks[6], (DEPTH, CONF_KERNEL, GROUP_WIDTH), CONF_KERNEL ** -0.5),
        'conf_dw_b': nrm(ks[7], (DEPTH, GROUP_WIDTH), 0.02),
        'conf_ln_g': gain(ks[8], (DEPTH, GROUP_WIDTH)),
        'conf_ln_b': nrm(ks[9], (DEPTH, GROUP_WIDTH), 0.02),
        'ret_norm_g': gain(ks[10], (DEPTH, GROUP_WIDTH)),
        'sc_conv_w': nrm(ks[11], (DEPTH, SHORT_KERNEL, GROUP_WIDTH), SHORT_KERNEL ** -0.5),
        'w_out': nrm(ks[12], (DEPTH, D_MIX, D_MODEL), D_MIX ** -0.5),
        'ffn_up': nrm(ks[13], (DEPTH, D_MODEL, 2 * D_FF), D_MODEL ** -0.5),
        'ffn_conv_w': nrm(ks[14], (DEPTH, FFN_KERNEL, 2 * D_FF), FFN_KERNEL ** -0.5),
        'ffn_down': nrm(ks[15], (DEPTH, D_FF, D_MODEL), D_FF ** -0.5),
    }

def first_block(x, norm_mix_pre, norm_mix_post, norm_ffn_pre, norm_ffn_post, w_in,
              conf_dw_w, conf_dw_b, conf_ln_g, conf_ln_b, ret_norm_g, sc_conv_w,
              w_out, ffn_up, ffn_conv_w, ffn_down):
    for l in range(DEPTH):
        h = rms_norm(x, norm_mix_pre[l])
        proj = h @ w_in[l]
        (c_a, c_gate, sb_q, sb_k, sb_v, r_q, r_k, r_v, r_g,
         sc_b, sc_c, sc_h) = jnp.split(proj, N_IN_SLICES, axis=-1)
        y_conf = conformer_conv(c_a, c_gate, conf_dw_w[l], conf_dw_b[l], conf_ln_g[l], conf_ln_b[l])
        y_sb = merge_heads(stick_breaking_attention(split_heads(sb_q), split_heads(sb_k), split_heads(sb_v)))
        y_ret = retention_mixer(r_q, r_k, r_v, r_g, ret_norm_g[l])
        y_sc = short_gated_conv(sc_b, sc_c, sc_h, sc_conv_w[l])
        mix = jnp.concatenate([y_conf, y_sb, y_ret, y_sc], axis=-1) @ w_out[l]
        x = x + rms_norm(mix, norm_mix_post[l])
        f = conv_ffn(rms_norm(x, norm_ffn_pre[l]), ffn_up[l], ffn_conv_w[l], ffn_down[l])
        x = x + rms_norm(f, norm_ffn_post[l])
    return x


DEPTH_2 = 1

GRID_W = 64
CTX_LEN = 256
NH_M = 4
DQK_M = D_MODEL // 8
DV_M = D_MODEL // 4
MLSTM_CHUNK = 128
NH_D = 8
DH_D = D_MODEL // 16
Q_BLOCK = 128
N_EXPERTS = 32
TOP_K = 4
D_FF_2 = D_MODEL
SWIGLU_LIMIT = 7.0
SWIGLU_ALPHA = 1.702
EXPERT_BLOCK = 128
SPLIT_SIZES = (NH_M * DQK_M, NH_M * DQK_M, NH_M * DV_M, 4 * NH_M, NH_M * DV_M,
               NH_D * 2 * DH_D, NH_D * 2 * DH_D, NH_D * 2 * DH_D, D_MODEL, D_MODEL)
IN_COLS = sum(SPLIT_SIZES)


def rmsnorm(x, g):
    xf = x.astype(jnp.float32)
    y = xf * lax.rsqrt(jnp.mean(xf * xf, axis=-1, keepdims=True) + NORM_EPS)
    return (y * g.astype(jnp.float32)).astype(x.dtype)

def modulate(u, shift, scale):
    return u * (1 + scale) + shift

def split_proj(u, w_in):
    return jnp.split(u @ w_in, np.cumsum(SPLIT_SIZES)[:-1].tolist(), axis=-1)

def axial_rope_tables(n_tok):
    rows = n_tok // GRID_W
    row = jnp.repeat(jnp.arange(rows, dtype=jnp.float32), GRID_W)
    col = jnp.tile(jnp.arange(GRID_W, dtype=jnp.float32), rows)
    n_freq = DH_D // 4
    inv_freq = ROPE_BASE ** (-jnp.arange(n_freq, dtype=jnp.float32) / n_freq)
    ang_r = (row[:, None] * inv_freq)[:, None, None, :]
    ang_c = (col[:, None] * inv_freq)[:, None, None, :]
    return (jnp.cos(ang_r), jnp.sin(ang_r), jnp.cos(ang_c), jnp.sin(ang_c))

def rotate_pairs(x, cos, sin):
    x1, x2 = jnp.split(x, 2, axis=-1)
    cos = cos.astype(x.dtype)
    sin = sin.astype(x.dtype)
    return jnp.concatenate([x1 * cos - x2 * sin, x2 * cos + x1 * sin], axis=-1)

def apply_axial_rope(x, tables):
    cos_r, sin_r, cos_c, sin_c = tables
    half = DH_D // 2
    return jnp.concatenate([rotate_pairs(x[..., :half], cos_r, sin_r),
                            rotate_pairs(x[..., half:], cos_c, sin_c)], axis=-1)

def mlstm_chunkwise(q, k, v, i_pre, logf, state):
    b_, h_, t_, _ = q.shape
    L = MLSTM_CHUNK
    nc = t_ // L

    def chunks(a):
        return jnp.moveaxis(a.reshape(a.shape[:2] + (nc, L) + a.shape[3:]), 2, 0)

    causal = jnp.tril(jnp.ones((L, L), dtype=bool))

    def step(carry, xs):
        C, n, m = carry
        qc, kc, vc, ic, fc = xs
        bcum = jnp.cumsum(fc, axis=-1)
        log_d = jnp.where(causal, bcum[..., :, None] - bcum[..., None, :] + ic[..., None, :], -jnp.inf)
        inter = bcum + m[..., None]
        m_t = jnp.maximum(inter, jnp.max(log_d, axis=-1))
        s = jnp.einsum('bhtk,bhsk->bhts', qc, kc) * jnp.exp(log_d - m_t[..., None])
        w_inter = jnp.exp(inter - m_t)
        num = w_inter[..., None] * jnp.einsum('bhtk,bhkv->bhtv', qc, C) + jnp.einsum('bhts,bhsv->bhtv', s, vc)
        den = w_inter * jnp.einsum('bhtk,bhk->bht', qc, n) + jnp.sum(s, axis=-1)
        h = num / jnp.maximum(jnp.abs(den), jnp.exp(-m_t))[..., None]
        b_last = bcum[..., -1]
        log_w = b_last[..., None] - bcum + ic
        m_new = jnp.maximum(b_last + m, jnp.max(log_w, axis=-1))
        w = jnp.exp(log_w - m_new[..., None])
        decay = jnp.exp(b_last + m - m_new)
        C_new = decay[..., None, None] * C + jnp.einsum('bhsk,bhsv->bhkv', kc * w[..., None], vc)
        n_new = decay[..., None] * n + jnp.einsum('bhs,bhsk->bhk', w, kc)
        return (C_new, n_new, m_new), h

    state, h = lax.scan(step, state, (chunks(q), chunks(k), chunks(v), chunks(i_pre), chunks(logf)))
    return jnp.moveaxis(h, 0, 2).reshape(b_, h_, t_, v.shape[-1]), state

def mlstm_zero_state(batch):
    return (jnp.zeros((batch, NH_M, DQK_M, DV_M), jnp.float32),
            jnp.zeros((batch, NH_M, DQK_M), jnp.float32),
            jnp.zeros((batch, NH_M), jnp.float32))

def mlstm_prepare(p, gate_b):
    b, t = p[0].shape[:2]

    def heads(a, d):
        return a.reshape(b, t, NH_M, d).transpose(0, 2, 1, 3).astype(jnp.float32)

    q = heads(p[0], DQK_M) * DQK_M ** -0.5
    k = heads(p[1], DQK_M)
    v = heads(p[2], DV_M)
    g = (p[3] + gate_b).astype(jnp.float32).reshape(b, t, 4, NH_M).transpose(2, 0, 3, 1)
    return q, k, v, g

def mlstm_direction(q, k, v, i_pre, f_pre, state, reverse):
    logf = jax.nn.log_sigmoid(f_pre)
    if reverse:
        q, k, v, i_pre, logf = (jnp.flip(a, axis=2) for a in (q, k, v, i_pre, logf))
    h, state = mlstm_chunkwise(q, k, v, i_pre, logf, state)
    if reverse:
        h = jnp.flip(h, axis=2)
    return h, state

def mlstm_output(h, o_raw, g):
    b, t = o_raw.shape[:2]
    hn = rmsnorm(h.transpose(0, 2, 1, 3), g)
    o = jax.nn.sigmoid(o_raw.astype(jnp.float32)).reshape(b, t, NH_M, DV_M)
    return (hn * o).reshape(b, t, NH_M * DV_M).astype(o_raw.dtype)

def diff_prepare(p, tables):
    b, t = p[5].shape[:2]
    q = p[5].reshape(b, t, NH_D, 2, DH_D)
    k = p[6].reshape(b, t, NH_D, 2, DH_D)
    if tables is not None:
        q = apply_axial_rope(q, tables)
        k = apply_axial_rope(k, tables)
    v = p[7].reshape(b, t, NH_D, 2 * DH_D)
    return q.transpose(0, 2, 3, 1, 4), k.transpose(0, 2, 3, 1, 4), v.transpose(0, 2, 1, 3)

def diff_attend(q, k, v, lam):
    s = jnp.einsum('bhmqd,bhmkd->bhmqk', q, k).astype(jnp.float32) * DH_D ** -0.5
    p = jax.nn.softmax(s, axis=-1)
    a = p[:, :, 0] - lam * p[:, :, 1]
    return jnp.einsum('bhqk,bhkd->bhqd', a.astype(v.dtype), v)

def diff_output(o, g, lam_init):
    b, h, t, d = o.shape
    on = rmsnorm(o.transpose(0, 2, 1, 3), g) * (1.0 - lam_init)
    return on.reshape(b, t, h * d)

def merge_branches(p, a_out, b_out, w_a, w_b, w_o):
    y = jax.nn.sigmoid(p[8]) * (a_out @ w_a) + jax.nn.sigmoid(p[9]) * (b_out @ w_b)
    return y @ w_o

def token_mixer(u, uc, tables, w_in, gate_b, m_norm_g, lam_p, d_norm_g, w_a, w_b, w_o, lam_init, need_ctx):
    pl = split_proj(u, w_in)
    pc = split_proj(uc, w_in)
    ql, kl, vl, gl = mlstm_prepare(pl, gate_b)
    qc, kc, vc, gc = mlstm_prepare(pc, gate_b)
    st0 = mlstm_zero_state(uc.shape[0])
    h_cf, st_f = mlstm_direction(qc, kc, vc, gc[0], gc[1], st0, False)
    h_cb, st_b = mlstm_direction(qc, kc, vc, gc[2], gc[3], st0, True)
    h_lf, _ = mlstm_direction(ql, kl, vl, gl[0], gl[1], st_f, False)
    h_lb, _ = mlstm_direction(ql, kl, vl, gl[2], gl[3], st_b, True)
    a_lat = mlstm_output(h_lf + h_lb, pl[4], m_norm_g)
    lp = lam_p.astype(jnp.float32)
    lam = jnp.exp(jnp.sum(lp[0] * lp[1])) - jnp.exp(jnp.sum(lp[2] * lp[3])) + lam_init
    qdl, kdl, vdl = diff_prepare(pl, tables)
    qdc, kdc, vdc = diff_prepare(pc, None)
    k_all = jnp.concatenate([kdc, kdl], axis=3)
    v_all = jnp.concatenate([vdc, vdl], axis=2)
    b, h, _, t, dh = qdl.shape
    n_blk = t // Q_BLOCK
    q_blocks = jnp.moveaxis(qdl.reshape(b, h, 2, n_blk, Q_BLOCK, dh), 3, 0)
    o_blocks = lax.map(lambda qb: diff_attend(qb, k_all, v_all, lam), q_blocks)
    o_lat = jnp.moveaxis(o_blocks, 0, 2).reshape(b, h, t, 2 * dh)
    b_lat = diff_output(o_lat, d_norm_g, lam_init)
    y = merge_branches(pl, a_lat, b_lat, w_a, w_b, w_o)
    if not need_ctx:
        return y, None
    a_ctx = mlstm_output(h_cf + h_cb, pc[4], m_norm_g)
    b_ctx = diff_output(diff_attend(qdc, kdc, vdc, lam), d_norm_g, lam_init)
    return y, merge_branches(pc, a_ctx, b_ctx, w_a, w_b, w_o)

def moe_ffn(u, router_w, router_b, w1, b1, w2, b2):
    b, t, d = u.shape
    n_tok = b * t
    xf = u.reshape(n_tok, d)
    logits = (xf @ router_w + router_b).astype(jnp.float32)
    top_val, top_idx = lax.top_k(logits, TOP_K)
    gate = jax.nn.softmax(top_val, axis=-1).astype(u.dtype)
    n_asg = n_tok * TOP_K
    flat_e = top_idx.reshape(n_asg)
    flat_tok = jnp.arange(n_asg, dtype=jnp.int32) // TOP_K
    order = jnp.argsort(flat_e)
    sorted_e = flat_e[order]
    counts = jnp.bincount(flat_e, length=N_EXPERTS)
    padded = (counts + EXPERT_BLOCK - 1) // EXPERT_BLOCK * EXPERT_BLOCK
    pad_end = jnp.cumsum(padded)
    pad_start = pad_end - padded
    sorted_start = jnp.cumsum(counts) - counts
    dest = pad_start[sorted_e] + jnp.arange(n_asg) - sorted_start[sorted_e]
    n_buf = -(-n_asg // EXPERT_BLOCK) * EXPERT_BLOCK + N_EXPERTS * EXPERT_BLOCK
    buf_tok = jnp.zeros((n_buf,), jnp.int32).at[dest].set(flat_tok[order])
    buf_w = jnp.zeros((n_buf,), u.dtype).at[dest].set(gate.reshape(n_asg)[order])
    n_blk = n_buf // EXPERT_BLOCK
    blk_e = jnp.minimum(jnp.searchsorted(pad_end, jnp.arange(n_blk) * EXPERT_BLOCK, side='right'), N_EXPERTS - 1)

    def expert_block(args):
        tok, e = args
        hcat = xf[tok] @ w1[e] + b1[e]
        h_glu = jnp.minimum(hcat[:, :D_FF_2], SWIGLU_LIMIT)
        h_lin = jnp.clip(hcat[:, D_FF_2:], -SWIGLU_LIMIT, SWIGLU_LIMIT)
        act = h_glu * jax.nn.sigmoid(SWIGLU_ALPHA * h_glu) * (h_lin + 1)
        return act @ w2[e] + b2[e]

    y_buf = lax.map(expert_block, (buf_tok.reshape(n_blk, EXPERT_BLOCK), blk_e))
    y = jax.ops.segment_sum(y_buf.reshape(n_buf, d) * buf_w[:, None], buf_tok, num_segments=n_tok)
    return y.reshape(b, t, d)

def second_inputs(seed: int = 0) -> dict:
    key = jax.random.key(seed)
    ks = jax.random.split(key, 24)

    def nrm(k, shape, scale):
        return jax.random.normal(k, shape, jnp.float32) * scale

    L = DEPTH_2
    gate_base = jnp.array([0.0, 3.0, 0.0, 3.0], jnp.float32)[None, :, None]
    return {
        'x': nrm(ks[0], (BATCH, SEQ, D_MODEL), 1.0),
        'c': nrm(ks[1], (BATCH, D_MODEL), 1.0),
        'ctx': nrm(ks[2], (BATCH, CTX_LEN, D_MODEL), 1.0),
        'c_ctx': nrm(ks[3], (D_MODEL,), 1.0),
        'ada_w': nrm(ks[4], (L, D_MODEL, 6 * D_MODEL), 0.5 * D_MODEL ** -0.5),
        'ada_b': nrm(ks[5], (L, 6 * D_MODEL), 0.02),
        'norm1_g': 1.0 + nrm(ks[6], (L, D_MODEL), 0.02),
        'norm2_g': 1.0 + nrm(ks[7], (L, D_MODEL), 0.02),
        'w_in': nrm(ks[8], (L, D_MODEL, IN_COLS), D_MODEL ** -0.5),
        'mlstm_gate_b': (gate_base + nrm(ks[9], (L, 4, NH_M), 0.1)).reshape(L, 4 * NH_M),
        'mlstm_norm_g': 1.0 + nrm(ks[10], (L, NH_M, DV_M), 0.02),
        'diff_lambda': nrm(ks[11], (L, 4, DH_D), 0.1),
        'diff_norm_g': 1.0 + nrm(ks[12], (L, NH_D, 2 * DH_D), 0.02),
        'w_branch_a': nrm(ks[13], (L, NH_M * DV_M, D_MODEL), (NH_M * DV_M) ** -0.5),
        'w_branch_b': nrm(ks[14], (L, NH_D * 2 * DH_D, D_MODEL), (NH_D * 2 * DH_D) ** -0.5),
        'w_out': nrm(ks[15], (L, D_MODEL, D_MODEL), D_MODEL ** -0.5),
        'router_w': nrm(ks[16], (L, D_MODEL, N_EXPERTS), D_MODEL ** -0.5),
        'router_b': nrm(ks[17], (L, N_EXPERTS), 0.01),
        'exp_w1': nrm(ks[18], (L, N_EXPERTS, D_MODEL, 2 * D_FF_2), D_MODEL ** -0.5),
        'exp_b1': nrm(ks[19], (L, N_EXPERTS, 2 * D_FF_2), 0.01),
        'exp_w2': nrm(ks[20], (L, N_EXPERTS, D_FF_2, D_MODEL), D_FF_2 ** -0.5),
        'exp_b2': nrm(ks[21], (L, N_EXPERTS, D_MODEL), 0.01),
        'final_norm_g': 1.0 + nrm(ks[22], (D_MODEL,), 0.02),
    }

def second_block(x, c, ctx, c_ctx, ada_w, ada_b, norm1_g, norm2_g, w_in, mlstm_gate_b, mlstm_norm_g,
              diff_lambda, diff_norm_g, w_branch_a, w_branch_b, w_out, router_w, router_b,
              exp_w1, exp_b1, exp_w2, exp_b2, final_norm_g):
    tables = axial_rope_tables(x.shape[1])
    xc = ctx
    for l in range(DEPTH_2):
        need_ctx = l < DEPTH_2 - 1
        lam_init = 0.8 - 0.6 * math.exp(-0.3 * l)
        mod = jax.nn.silu(c) @ ada_w[l] + ada_b[l]
        sh1, sc1, g1, sh2, sc2, g2 = jnp.split(mod[:, None, :], 6, axis=-1)
        modc = jax.nn.silu(c_ctx) @ ada_w[l] + ada_b[l]
        sh1c, sc1c, g1c, sh2c, sc2c, g2c = jnp.split(modc, 6, axis=-1)
        u = modulate(rmsnorm(x, norm1_g[l]), sh1, sc1)
        uc = modulate(rmsnorm(xc, norm1_g[l]), sh1c, sc1c)
        y, yc = token_mixer(u, uc, tables, w_in[l], mlstm_gate_b[l], mlstm_norm_g[l], diff_lambda[l],
                            diff_norm_g[l], w_branch_a[l], w_branch_b[l], w_out[l], lam_init, need_ctx)
        x = x + g1 * y
        x = x + g2 * moe_ffn(modulate(rmsnorm(x, norm2_g[l]), sh2, sc2), router_w[l], router_b[l],
                             exp_w1[l], exp_b1[l], exp_w2[l], exp_b2[l])
        if need_ctx:
            xc = xc + g1c * yc
            xc = xc + g2c * moe_ffn(modulate(rmsnorm(xc, norm2_g[l]), sh2c, sc2c), router_w[l], router_b[l],
                                    exp_w1[l], exp_b1[l], exp_w2[l], exp_b2[l])
    return rmsnorm(x, final_norm_g)


def setup_inputs(seed=0):
    out = dict(first_inputs(seed))
    for name, value in second_inputs(seed + 1).items():
        if name != "x":
            out[name + "_2"] = value
    return out


def reference(
    x, norm_mix_pre, norm_mix_post, norm_ffn_pre, norm_ffn_post, w_in, conf_dw_w, conf_dw_b,
    conf_ln_g, conf_ln_b, ret_norm_g, sc_conv_w, w_out, ffn_up, ffn_conv_w, ffn_down, c_2,
    ctx_2, c_ctx_2, ada_w_2, ada_b_2, norm1_g_2, norm2_g_2, w_in_2, mlstm_gate_b_2,
    mlstm_norm_g_2, diff_lambda_2, diff_norm_g_2, w_branch_a_2, w_branch_b_2, w_out_2,
    router_w_2, router_b_2, exp_w1_2, exp_b1_2, exp_w2_2, exp_b2_2, final_norm_g_2,
):
    x = first_block(
        x, norm_mix_pre, norm_mix_post, norm_ffn_pre, norm_ffn_post, w_in, conf_dw_w, conf_dw_b,
        conf_ln_g, conf_ln_b, ret_norm_g, sc_conv_w, w_out, ffn_up, ffn_conv_w, ffn_down,
    )
    return second_block(
        x, c_2, ctx_2, c_ctx_2, ada_w_2, ada_b_2, norm1_g_2, norm2_g_2, w_in_2, mlstm_gate_b_2,
        mlstm_norm_g_2, diff_lambda_2, diff_norm_g_2, w_branch_a_2, w_branch_b_2, w_out_2,
        router_w_2, router_b_2, exp_w1_2, exp_b1_2, exp_w2_2, exp_b2_2, final_norm_g_2,
    )


_drawn_inputs = setup_inputs


def setup_inputs(seed=0):
    import zlib

    import numpy as np

    out = dict(_drawn_inputs(seed))
    spreads = {}
    factors = {'conf_ln_b': 4.476,
     'ctx_2': 2.887,
     'ada_b_2': 4.112,
     'norm1_g_2': 8.0,
     'norm2_g_2': 6.953,
     'mlstm_gate_b_2': 2.72,
     'mlstm_norm_g_2': 8.0,
     'diff_lambda_2': 8.0,
     'diff_norm_g_2': 8.0,
     'router_b_2': 8.0,
     'exp_b1_2': 28.921,
     'exp_b2_2': 64.0,
     'final_norm_g_2': 8.979}
    for name, (base, spread) in spreads.items():
        noise = np.random.default_rng([zlib.crc32(name.encode()), seed]).standard_normal(out[name].shape)
        drawn = base * np.exp(spread * noise) if base else spread * noise
        out[name] = jnp.asarray(drawn.astype(out[name].dtype))
    for name, factor in factors.items():
        out[name] = (out[name] * factor).astype(out[name].dtype)
    return out
```

```python
from contextlib import ExitStack

import numpy as np

import concourse.bass as bass
from concourse import mybir

F32 = mybir.dt.float32
ALU = mybir.AluOpType
ACT = mybir.ActivationFunctionType
AX = mybir.AxisListType.X

P = 128
T = 256
TT = T // P
D = 1024
KC = D // P
DEPTH = 2
GW = 256
HD = 64
NH = GW // HD
CONF_K = 31
SC_K = 3
FFN_K = 3
D_FF = 2816
FFC = D_FF // P
EPS = 1e-6
SCALE = HD ** -0.5

WORK = 21600
XHAT_AT = 2526
CAT_AT = XHAT_AT + 2 * 2048
SLOT = 4096
ACT_STEPS = 5
DVE_STEPS = 123
ROW_SLICES = (4, 5, 6, 7, 8)
RING = 5
DIAG = 384

COL_MIX_PRE = 0
COL_CONF_W = COL_MIX_PRE + KC
COL_CONF_B = COL_CONF_W + 2 * CONF_K
COL_CONF_LG = COL_CONF_B + 2
COL_CONF_LB = COL_CONF_LG + 2
COL_SC_W = COL_CONF_LB + 2
COL_FFN_PRE = COL_SC_W + 2 * SC_K
COL_FFN_W = COL_FFN_PRE + KC
N_COLS = COL_FFN_W + 2 * FFC * FFN_K
N_MIXROW = D + GW

CONSTS = {}
_at = 0
for _name, _n in (("ident", P), ("ones", P), ("suffix", P), ("sb_mask", DIAG), ("sb_neg", DIAG),
                  ("ret_decay", NH * DIAG), ("ret_cos", TT * GW), ("ret_sin", TT * GW)):
    CONSTS[_name] = (_at, _n)
    _at += _n
N_CONST = _at
SPARE = 3 * P


def shape_constants():
    c = np.zeros((P, N_CONST), np.float32)

    def put(name, a):
        at, n = CONSTS[name]
        c[:, at:at + n] = np.asarray(a, np.float32).reshape(P, n)

    i = np.arange(P)
    put("ident", np.eye(P))
    put("ones", np.ones((P, P)))
    put("suffix", i[:, None] >= i[None, :])
    strict = (i[:, None] < i[None, :]).astype(np.float32)
    mask = np.concatenate([strict, np.ones((P, P)), strict], axis=1)
    put("sb_mask", mask)
    put("sb_neg", np.where(mask > 0, 0.0, -1e30))
    log_gamma = np.log1p(-np.exp2(-5.0 - np.arange(NH)))
    diff = i[None, :] - i[:, None]
    decay = []
    for h in range(NH):
        diag = np.where(diff >= 0, np.exp(np.maximum(diff, 0) * log_gamma[h]), 0.0)
        full = np.exp((diff + P) * log_gamma[h])
        decay.append(np.concatenate([diag, full, diag], axis=1) * SCALE)
    put("ret_decay", np.stack(decay, axis=1))
    inv = (np.float32(10000.0) ** (-np.arange(0, HD, 2, dtype=np.float32) / np.float32(HD))).astype(np.float32)
    pos = (i[:, None] + P * np.arange(TT)[None, :]).astype(np.float32)
    ang = (pos[:, :, None] * inv[None, None, :]).astype(np.float32)
    cos, sin = np.cos(ang), np.sin(ang)
    put("ret_cos", np.tile(np.concatenate([cos, cos], -1)[:, :, None, :], (1, 1, NH, 1)))
    put("ret_sin", np.tile(np.concatenate([-sin, sin], -1)[:, :, None, :], (1, 1, NH, 1)))
    return c


LAYER_SLOTS = [("in", s) for s in range(6)] + [("out", s) for s in range(2)]
for _m in range(5):
    LAYER_SLOTS += [("up", g) for g in ((0, 1, 2) if _m == 0 else (2 * _m + 1, 2 * _m + 2))] + [("down", _m)]
LAYER_SLOTS += [("down", 5)]
assert len(LAYER_SLOTS) % RING == 0 and len(LAYER_SLOTS) == 25

LAYER_BANKS = [("T", i, i) for i in range(4)]
LAYER_BANKS += [("s", i, (4 + i) % 8) for i in range(6)]
LAYER_BANKS += [("Z", h, 2 + h) for h in range(4)]
LAYER_BANKS += [("s", 6, 6), ("s", 7, 7), ("RQ", 0, 0), ("RK", 0, 1), ("s", 8, 2), ("s", 9, 3)]
LAYER_BANKS += [("RS", h, 4 + h) for h in range(4)]
LAYER_BANKS += [("s", 10, 0), ("s", 11, 1)]
LAYER_BANKS += [("I", h, 2 + h) for h in range(4)]
LAYER_BANKS += [("RO", 0, 6), ("CM", 0, 7), ("SB", 0, 0), ("SB", 1, 1), ("CV", 0, 2), ("RT", 0, 3)]
LAYER_BANKS += [("M", i, 4 + i) for i in range(4)]
LAYER_BANKS += [("F", i, i) for i in range(4)]
LAYER_BANKS += [("U", g, (2 * (g // 2)) % 4 + g % 2) for g in range(6)]
LAYER_BANKS += [("D", i, 4 + i) for i in range(4)]
LAYER_BANKS += [("U", g, (2 * (g // 2)) % 4 + g % 2) for g in range(6, 22)]


NHM, DQK, DV = 4, 128, 256
ST = 2 * TT
S = ST * P
NHD, DHD = 8, 64
N_EXP, TOP_K = 32, 4
CAP = 64
PAIRS = N_EXP // 2
W_IN2_COLS = dict(mq=0, mk=512, mv=1024, gates=2048, mo=2064, dq=3088, dk=4112, dv=5136, pa=6160, pb=7184)
LAM_INIT = 0.2
LIMIT, ALPHA = 7.0, 1.702

CONSTS2 = {}
_at = 0
for _name, _n in (("rope_cos", T), ("rope_sin", T), ("partner", P), ("prefix", P), ("before", P), ("iota", CAP),
                  ("pick", 2), ("spread", P)):
    CONSTS2[_name] = (_at, _n)
    _at += _n
N_CONST2 = _at


def shape_constants2():
    c = np.zeros((P, N_CONST2), np.float32)

    def put(name, a):
        at, n = CONSTS2[name]
        c[:, at:at + n] = np.asarray(a, np.float32).reshape(P, n)

    i = np.arange(P)
    d = i % DHD
    nf = DHD // 4
    inv = (np.float32(10000.0) ** (-np.arange(nf, dtype=np.float32) / np.float32(nf))).astype(np.float32)
    tok = np.arange(T)
    pos = np.where((d < DHD // 2)[:, None], (tok // 64)[None, :], (tok % 64)[None, :]).astype(np.float32)
    ang = (pos * inv[d % nf][:, None]).astype(np.float32)
    first = (d % (2 * nf)) < nf
    put("rope_cos", np.cos(ang))
    put("rope_sin", np.where(first[:, None], -np.sin(ang), np.sin(ang)))
    partner = np.where(first, i + nf, i - nf)
    put("partner", partner[:, None] == i[None, :])
    put("prefix", i[:, None] <= i[None, :])
    put("before", i[:, None] < i[None, :])
    put("iota", np.tile(np.arange(CAP), (P, 1)))
    put("pick", (i % 32)[:, None] == np.arange(2)[None, :])
    put("spread", np.tile((i % 32 == 0)[:, None], (1, P)))
    return c


B2_SLOTS = [("ada", n) for n in range(12)]
B2_SLOTS += [("mq", 0), ("mk", 0), ("mv", 0), ("mv", 1), ("mo", 0), ("mo", 1)]
B2_SLOTS += [(k, g) for g in (0, 1) for k in ("dv", "dq", "dk")]
B2_SLOTS += [(k, g) for g in (0, 1) for k in ("pa", "pb", "wa", "wb")]
B2_SLOTS += [("wo", 0), ("wo", 1)]

B2_BANKS = []
for _n in range(12):
    B2_BANKS.append(("ada", _n, _n % 2))
    if _n >= 1:
        _m = _n - 1
        B2_BANKS += [("mT", 0, 2)] if _m == 3 else [("mT", 1, 3)] if _m == 9 else []
        B2_BANKS += [("mR", _m, 4 + _m % 2)] if _m in (4, 5, 10) else []
B2_BANKS += [("mR", 11, 5)]
B2_BANKS += [("CT", i, i) for i in range(4)] + [("XT", i, 4 + i) for i in range(4)]
B2_BANKS += [("mq", 0, 0), ("mq", 1, 1)] + [("mk", h, 2 + h) for h in range(4)] + [("mg", 0, 6), ("F", 9, 7)]
B2_BANKS += [("mv", i, i) for i in range(4)]
B2_BANKS += [("GT", 0, 4), ("GT", 1, 5)]
B2_BANKS += [("mv", 4, 6), ("mv", 5, 7), ("mv", 6, 0), ("mv", 7, 1)]
B2_BANKS += [("mo", 0, 2), ("mo", 1, 3), ("mo", 2, 4), ("mo", 3, 5), ("MR", 0, 6)]


def _heads_banks():
    out = []
    for h in range(NHM + 1):
        if h < NHM:
            out += [("MB", h, 7), ("QK", 2 * h, 0), ("QK", 2 * h + 1, 1)]
        if h >= 1:
            out += [("H", 4 * (h - 1) + i, 2 + i) for i in range(4)]
    return out


B2_BANKS += _heads_banks()
B2_BANKS += [("AT", i, 6 + i % 2) for i in range(4)]
for _g in (0, 1):
    B2_BANKS += [("dv", 4 * _g + i, i) for i in range(4)]
    B2_BANKS += [("dq", 4 * _g, 4), ("dk", 4 * _g, 5), ("rot", 4 * _g, 6)]
    for _hh in range(4):
        _h = 4 * _g + _hh
        if _hh < 3:
            B2_BANKS += [("dq", _h + 1, 4), ("dk", _h + 1, 5)]
        B2_BANKS += [("S", 4 * _h + i, i) for i in range(4)]
        if _hh < 3:
            B2_BANKS += [("rot", _h + 1, 6)]
        B2_BANKS += [("PT", 2 * _h, 7), ("PT", 2 * _h + 1, 4), ("O", _h, 5)]
B2_BANKS += [("BT", i, i) for i in range(4)]
for _g in (0, 1):
    B2_BANKS += [("pa", 2 * _g, 4), ("pa", 2 * _g + 1, 5), ("pb", 2 * _g, 6), ("pb", 2 * _g + 1, 7)]
    B2_BANKS += [("wa", 2 * _g, 0), ("wa", 2 * _g + 1, 1), ("wb", 2 * _g, 2), ("wb", 2 * _g + 1, 3)]
B2_BANKS += [("Y", i, 4 + i) for i in range(4)]
B2_BANKS += [("R", i, i) for i in range(4)]
B2_BANKS += [("L", 0, 4), ("PC", 0, 5), ("CN", 0, 6), ("gT", 0, 7)]
B2_BANKS += [("YM", i, i) for i in range(4)]
MOE_BANKS = [("G", 0, 4), ("G", 1, 5), ("GLU", 0, 6), ("LIN", 0, 7), ("GLU", 1, 4), ("LIN", 1, 5),
             ("ST", 0, 6), ("AT2", 0, 7), ("OUT", 0, 4), ("OUT", 1, 5), ("AT2", 1, 6)]
PAIR_SLOTS = [("w1", x, q) for q in range(4) for x in (0, 1)] + [("w2", x, q) for q in range(2) for x in (0, 1)]
PAIR_RING = (4, 0, 1, 2, 3, 5)


def bank_rounds(items):
    used, where = [0] * 8, {}
    for kind, i, b in items:
        where[kind, i] = (b, used[b])
        used[b] += 1
    return where, used


LAYER_WHERE, LAYER_FILLS = bank_rounds(LAYER_BANKS)
B2_WHERE, B2_FILLS = bank_rounds(B2_BANKS)
MOE_WHERE, MOE_FILLS = bank_rounds(MOE_BANKS)


def earlier_fills(key, l):
    if key in MOE_WHERE:
        b, n = MOE_WHERE[key]
        return b, l * MOE_FILLS[b] + (DEPTH * LAYER_FILLS[b] + B2_FILLS[b] + n)
    if key in B2_WHERE:
        b, n = B2_WHERE[key]
        return b, DEPTH * LAYER_FILLS[b] + n
    b, n = LAYER_WHERE[key]
    return b, l * LAYER_FILLS[b] + n


def build_program(nc, w, out):
    with ExitStack() as ctx:
        def sb(name, n, p=P):
            return ctx.enter_context(nc.sbuf_tensor(name, [p, n], F32))

        def sem(name):
            return ctx.enter_context(nc.semaphore(name))

        psum = ctx.enter_context(nc.psum_tensor("psum", [P, 8, 512], F32))
        ring = sb("ring", 6 * SLOT)
        const = sb("const", N_CONST)
        x_row = sb("x_row", TT * D)
        stats = sb("stats", 64)
        work = sb("work", WORK)
        offset = [0]

        def part(n, *shape):
            at = offset[0]
            offset[0] += n
            assert offset[0] <= WORK, offset
            v = work[:, at:at + n]
            if shape:
                names = "abcd"[:len(shape)]
                v = v.rearrange(f"p ({' '.join(names)}) -> p {' '.join(names)}", **dict(zip(names, shape)))
            return v

        def cst(name):
            at, n = CONSTS[name]
            return const[:, at:at + n]

        ident, ones, suffix = cst("ident"), cst("ones"), cst("suffix")
        sb_mask4 = cst("sb_mask").unsqueeze(1).broadcast_to([P, NH, DIAG])
        sb_neg4 = cst("sb_neg").unsqueeze(1).broadcast_to([P, NH, DIAG])
        ret_decay = cst("ret_decay").rearrange("p (h n) -> p h n", h=NH)
        x = x_row[:, :].rearrange("p (t d) -> p t d", t=TT)
        sumsq, rms, rinv = stats[:, 0:2], stats[:, 2:4], stats[:, 4:6]
        ret_mu, ret_var, ret_std, ret_rinv = (stats[:, 8 + 8 * i:16 + 8 * i] for i in range(4))

        cols = part(N_COLS + N_COLS % 2)
        mix_row = part(N_MIXROW)
        ffn_row = part(D)
        assert offset[0] == XHAT_AT
        xhat = part(TT * D, TT, D)
        hT = part(KC * T, KC, T)
        assert offset[0] == CAT_AT
        catT = part(KC * T, KC, T)
        q_z = part(NH * T, NH, T)
        rq_z = part(NH * T, NH, T)
        conf_pad = part(2 * (T + 30), 2, T + 30)
        sc_pad = part(2 * (T + 2), 2, T + 2)
        branch_at = offset[0]
        kT = part(2 * T, 2, T)
        v_sb = part(TT * GW, TT, GW)
        z = part(NH * DIAG, NH, DIAG)
        soft = part(NH * DIAG, NH, DIAG)
        rq = part(TT * GW, TT, GW)
        rk = part(TT * GW, TT, GW)
        swapped = part(TT * GW)
        rkT = part(2 * T, 2, T)
        rv = part(TT * GW, TT, GW)
        rg = part(TT * GW, TT, GW)
        conf_gate = part(2 * T, 2, T)
        conf = part(2 * T, 2, T)
        conf_sq = part(2 * T, 2, T)
        sc_b = part(2 * T, 2, T)
        sc_c = part(2 * T, 2, T)
        r_scores = xhat.rearrange("p t d -> p (t d)")[:, 0:NH * DIAG].rearrange("p (h n) -> p h n", h=NH)
        ret = conf_sq
        offset[0] = branch_at
        ffT = part(FFC * T, FFC, T)
        taps = part(2 * 4 * T, 2, 4, T)

        extra_at = [5 * SLOT]

        def extra(n, *shape):
            at = extra_at[0]
            extra_at[0] += n
            assert extra_at[0] <= 6 * SLOT
            return shaped(ring[:, at:at + n], shape)

        def shaped(v, shape):
            if not shape:
                return v
            names = "abcd"[:len(shape)]
            return v.rearrange(f"p ({' '.join(names)}) -> p {' '.join(names)}", **dict(zip(names, shape)))

        def at(start, n, *shape):
            assert start + n <= WORK
            return shaped(work[:, start:start + n], shape)

        ctx_row = extra(TT * D, TT, D)
        const2 = extra(N_CONST2)
        cols2 = extra(2 * KC + 4 * KC)
        cT = extra(2 * KC, KC, 2)
        siluc = extra(KC * 32, KC, 32)
        gate_w = extra(KC * 16, KC, 16)
        gate_b = extra(16)
        lam_row = extra(4 * DHD, 4, DHD)
        router_b = extra(N_EXP)

        def cst2(name):
            a, n = CONSTS2[name]
            return const2[:, a:a + n]

        flatten = lambda v: v.rearrange("p a b -> p (a b)")
        low, mid = 0, XHAT_AT + TT * D
        ada_rows = at(CAT_AT, 1024, 2, 512)
        uT = at(CAT_AT + 1024, KC * S, KC, S)
        high = CAT_AT + 1024 + KC * S
        g_rows = at(WORK - 2048, 2048, 2, D)
        top = WORK - 2048
        m_v = at(high, ST * NHM * 258, ST, NHM, 258)
        m_kT = at(high + 4128, NHM * S, NHM, S)
        m_qT = at(high + 6176, NHM * T, NHM, T)
        cummax = [[const[0:NHM, SPARE + 384 * (2 * d + i):SPARE + 384 * (2 * d + i + 1)] for i in (0, 1)] for d in (0, 1)]
        assert high + 7200 <= top and high + 7680 <= top and branch_at + FFC * T + 2048 <= top
        o_row = at(mid, TT * D, TT, D)
        decay = [at(low, 2 * ST * T, 2, ST * T), at(XHAT_AT, 2 * ST * T, 2, ST * T)]
        h_row = ctx_row
        norm_row = at(CAT_AT, D)
        a_outT = at(mid, KC * T, KC, T)
        d_kT = at(high, 4 * S, 4, S)
        d_v = at(high + 2048, ST * 512, ST, 512)
        d_q = at(high + 4096, 8 * T, 8, T)
        raw = at(high + 6144, 1024, 2, 512)
        turned = at(high + 7168, 512)
        aT = shaped(const[:, SPARE + 1536:SPARE + 2560], (2, 512))
        probs = at(low, 2048, 2, 2, S)
        b_row = xhat
        squares = at(low, 2 * D)
        b_outT = at(high, KC * T, KC, T)
        gate_a, gate_bb = at(low, 1024), at(low + 1024, 1024)
        yT = at(high + 2048, KC * T, KC, T)
        b1_rows = at(high + 4096, 2 * D)
        b2_rows = at(high + 6144, D)
        router_w = at(high + 7168, KC * N_EXP, KC, N_EXP)
        final_row = const[:, SPARE + 1536:SPARE + 2560]
        u2T = at(CAT_AT + 1024, KC * T, KC, T)
        xgT = at(mid, KC * P, KC, P)
        pick = at(mid + 1024, TT * P, TT, P)
        pick_gated = at(mid + 1280, TT * P, TT, P)
        spread_T = at(mid + 1536, T)
        assert mid + 1792 <= CAT_AT + 1024
        glu, sig, lin, act_ = ([at(CAT_AT + 1024 + 512 * (4 * e + i), 512) for e in (0, 1)] for i in range(4))
        actT = at(low, KC * P, KC, P)
        pick_e = at(low + 1024, P)
        gT = at(low + 1152, T)
        out_sb = at(high, D)
        router_at = [SPARE]

        def routed(n, *shape):
            a = router_at[0]
            router_at[0] += n
            assert router_at[0] <= SPARE + 1536
            return shaped(const[:, a:a + n], shape)

        n_wide = N_EXP + 4
        logits, others, exps = (routed(TT * n_wide, TT, n_wide) for _ in range(3))
        top8 = routed(TT * 8, TT, 8)
        neg_top, gate_sum, gate_inv = routed(TT), routed(TT), routed(TT)
        chosen, gate_row = routed(TT * N_EXP, TT, N_EXP), routed(TT * N_EXP, TT, N_EXP)
        pair_gate, pair_slot = routed(TT * N_EXP), routed(TT * N_EXP)
        most, n_pass = routed(1), routed(1)
        passes = ctx.enter_context(nc.sbuf_tensor("passes", [P, 1], mybir.dt.int32))

        small = sb("small", 800)
        small_at = [0]

        def tiny(n, *shape):
            a = small_at[0]
            small_at[0] += n
            assert small_at[0] <= 800
            return shaped(small[:, a:a + n], shape)

        modT = tiny(64, 32, 2)
        scale1, shift1 = tiny(16, 2, KC), tiny(16, 2, KC)
        scale2 = tiny(KC)
        gates = tiny(64, ST, 16)
        f_neg, f_abs, f_min, log_f = (tiny(32, ST * 2, 4) for _ in range(4))
        g_sub = tiny(32, ST, 8)
        ctx_max = tiny(2)
        m_neg = tiny(16)
        den, den2 = tiny(16), tiny(16)
        h_sq, h_rms, h_inv = tiny(8), tiny(8), tiny(8)
        lam_prod = tiny(128, 2, DHD)
        lam_sum, lam_exp, neg_lam = tiny(2), tiny(2), tiny(1)
        row_max, neg_max, row_sum, row_inv, map_scale = (tiny(4, 2, 2) for _ in range(5))
        b_sq, b_rms, b_inv = tiny(16), tiny(16), tiny(16)
        iota = tiny(CAP)

        filled = [sem(f"bank{b}_filled") for b in range(8)]
        evacuated = [sem(f"bank{b}_evacuated") for b in range(8)]
        slot_loaded = [sem(f"slot{s}_loaded") for s in range(6)]
        slot_free = sem("slot_free")
        const_loaded, x_loaded, mix_par_loaded, ffn_par_loaded = (
            sem(n) for n in ("const_loaded", "x_loaded", "mix_par_loaded", "ffn_par_loaded"))
        zeros_ready = sem("zeros_ready")
        x_ready = sem("x_ready")
        act_step, dve_step = sem("act_step"), sem("dve_step")
        rms_ready, xhat_ready = sem("rms_ready"), sem("xhat_ready")
        sb_abs, sb_log, sb_soft, sb_arg, sb_attn = (
            sem(n) for n in ("sb_abs_ready", "sb_log_ready", "sb_soft_ready", "sb_arg_ready", "sb_attn_ready"))
        rq_ready, rk_ready, ret_var_ready, ret_std_ready, ret_ready = (
            sem(n) for n in ("rq_ready", "rk_ready", "ret_var_ready", "ret_std_ready", "ret_ready"))
        conf_ready, conf_sq_ready, conf_normed, conf_cat = (
            sem(n) for n in ("conf_conv_ready", "conf_sq_ready", "conf_normed", "conf_cat_ready"))
        sc_cat = sem("sc_cat_ready")
        tap_ready, silu_ready, ff_ready = (sem(n) for n in ("first_tap_ready", "silu_ready", "ff_ready"))
        out_stored = sem("out_stored")
        names = ("early_loaded ctx_loaded g_bias_loaded norm_row_loaded late_loaded siluc_ready scale1_ready ctx_hat_ready "
                 "gate_abs_ready gate_log_ready gate_ready cummax_ready m_neg_ready decay_exp_ready "
                 "h_ready h_normed lam_sum_ready lam_exp_ready qk_ready row_max_ready probs_ready "
                 "attn_ready b_normed y_ready").split()
        (early_loaded, ctx_loaded, g_bias_loaded, norm_row_loaded, late_loaded, siluc_ready, scale1_ready, ctx_hat_ready,
         gate_abs_ready, gate_log_ready, gate_ready, cummax_ready, m_neg_ready, decay_exp_ready,
         h_ready, h_normed, lam_sum_ready, lam_exp_ready, qk_ready, row_max_ready, probs_ready,
         attn_ready, b_normed, y_ready) = (sem(n) for n in names)
        pairs_step, mask_ready, exp_ready, gates_ready, passes_ready = (
            sem(n) for n in ("pairs_step", "chosen_ready", "exp_ready", "expert_gates_ready", "passes_ready"))
        b1_zeroed, picks_ready, sig_ready, hidden_ready, combined, out_ready = (
            sem(n) for n in ("b1_rows_zeroed", "picks_ready", "glu_sigmoid_ready", "hidden_ready", "pair_combined",
                             "out_ready"))
        expert_slot_free, expert_load_claimed = sem("expert_slot_free"), sem("expert_load_claimed")
        L2 = DEPTH
        slot_rounds = [DEPTH * (len(LAYER_SLOTS) // RING) + len(range(s, len(B2_SLOTS), RING)) for s in range(RING)] + [0]

        def bank_of(key):
            return earlier_fills(key, 0)[0]

        def fill(pe, key, l):
            b, n = earlier_fills(key, l)
            pe.wait_ge(evacuated[b], n + 1)
            return psum[:, b, :]

        def take(eng, key, l):
            b, n = earlier_fills(key, l)
            eng.wait_ge(filled[b], n + 1)
            return psum[:, b, :]

        def after_evacuation(eng, key, l):
            b, n = earlier_fills(key, l)
            eng.wait_ge(evacuated[b], n + 2)

        def slot_ready(pe, n, l):
            pe.wait_ge(slot_loaded[n % RING], 32 * (l * (len(LAYER_SLOTS) // RING) + n // RING + 1))
            return ring[:, (n % RING) * SLOT:(n % RING + 1) * SLOT]

        block = ctx.enter_context(nc.Block())

        def slot_used(eng, l, n):
            kind, s = B2_SLOTS[n] if l == L2 else LAYER_SLOTS[n]
            last_item = {"ada": s, "mq": 1, "mk": 3, "mv": 4 * s + 3, "mo": 2 * s + 1, "dv": 4 * s + 3, "dq": 4 * s + 3,
                         "dk": 4 * s + 3, "pa": 2 * s + 1, "pb": 2 * s + 1, "wa": 2 * s + 1, "wb": 2 * s + 1}
            if kind in last_item:
                take(eng, (kind, last_item[kind]), l)
            elif kind == "wo":
                if s == 0:
                    eng.wait_ge(slot_free, 6 * L2 + 1)
                else:
                    take(eng, ("Y", 3), l)
            elif kind == "in":
                take(eng, ("s", 2 * s), l)
                take(eng, ("s", 2 * s + 1), l)
            elif kind == "up":
                take(eng, ("U", 2 * s + 1), l)
            elif (kind, s) == ("out", 1):
                take(eng, ("M", 3), l)
            elif (kind, s) == ("down", 5):
                take(eng, ("D", 3), l)
            else:
                eng.wait_ge(slot_free, l * 6 + (0 if kind == "out" else 1 + s) + 1)

        def expert_slot(pe, it, n):
            s = PAIR_RING[n % 6]
            pe.wait_ge(slot_loaded[s], 32 * (2 * it) + 32 * (slot_rounds[s] + n // 6 + 1))
            return ring[:, s * SLOT:(s + 1) * SLOT]

        def over_pairs(eng, pair):
            with eng.Fori(0, PAIRS) as j:
                pair(j, j)
            eng.wait_ge(passes_ready, 1)
            n = eng.value_load(passes[0:1, 0:1], min_val=1, max_val=T // CAP)
            with eng.If(n > 1), eng.Fori(1, n) as r:
                with eng.Fori(0, PAIRS) as j:
                    pair(r * PAIRS + j, j)
            return n

        def loop_layers(eng, layer):
            with eng.Fori(0, DEPTH) as l:
                layer(l)

        @block.sync
        def _(sp):
            def load_slot(l, n):
                kind, s = B2_SLOTS[n] if l == L2 else LAYER_SLOTS[n]
                g = l * len(LAYER_SLOTS) + n
                if g >= RING:
                    l_before = min((g - RING) // len(LAYER_SLOTS), L2)
                    slot_used(sp, l_before, g - RING - l_before * len(LAYER_SLOTS))
                at = (n % RING) * SLOT
                dst = ring[:, at:at + SLOT]
                if kind == "in":
                    src = w["w_in"][l].rearrange("(k p) n -> p k n", p=P)
                    d3 = dst.rearrange("p (k n) -> p k n", k=KC)
                    two = [(d3[:, h * 4:h * 4 + 4, :], src[:, h * 4:h * 4 + 4, s * 512:(s + 1) * 512]) for h in (0, 1)]
                elif kind == "ada" or kind in W_IN2_COLS or kind in ("wa", "wb"):
                    if kind == "ada":
                        src, c0 = w["ada_w_2"][0], 512 * s
                    elif kind in W_IN2_COLS:
                        src, c0 = w["w_in_2"][0], W_IN2_COLS[kind] + 512 * s
                    else:
                        src, c0 = w["w_branch_a_2" if kind == "wa" else "w_branch_b_2"][0], 512 * s
                    src = src.rearrange("(k p) n -> p k n", p=P)
                    d3 = dst.rearrange("p (k n) -> p k n", k=KC)
                    two = [(d3[:, h * 4:h * 4 + 4, :], src[:, h * 4:h * 4 + 4, c0:c0 + 512]) for h in (0, 1)]
                elif kind == "up":
                    src = w["ffn_up"][l].rearrange("(k p) n -> p k n", p=P)
                    d4 = dst.rearrange("p (u k n) -> p u k n", u=2, k=KC)
                    two = [(d4[:, u], src[:, :, u * D_FF + s * 256:u * D_FF + (s + 1) * 256]) for u in (0, 1)]
                else:
                    src = {"out": w["w_out"], "down": w["ffn_down"], "wo": w["w_out_2"]}[kind][l % L2].rearrange("(k p) n -> p k n", p=P)
                    n_k = min(4, src.shape[1] - 4 * s)
                    d3 = dst.rearrange("p (k n) -> p k n", k=4)
                    half = n_k // 2
                    two = [(d3[:, h * half:(h + 1) * half, :], src[:, 4 * s + h * half:4 * s + (h + 1) * half, :]) for h in (0, 1)]
                for d, s_ in two:
                    sp.dma_start(d, s_).then_inc(slot_loaded[n % RING], 16)

            for l in range(DEPTH):
                for n in range(len(LAYER_SLOTS)):
                    load_slot(l, n)
            for n in range(len(B2_SLOTS)):
                load_slot(L2, n)

            def pair(it, j):
                for n, (kind, xx, q) in enumerate(PAIR_SLOTS):
                    s = PAIR_RING[n % 6]
                    sp.wait_ge(expert_slot_free, 12 * it + (n + 1))
                    sp.sem_inc(expert_load_claimed, 1)
                    n_k = 2 if kind == "w1" else 4
                    src = w["exp_w1_2" if kind == "w1" else "exp_w2_2"][0, 2 * j + xx].rearrange("(k p) n -> p k n", p=P)
                    dst = ring[:, s * SLOT:(s + 1) * SLOT].rearrange("p (k n) -> p k n", k=n_k)
                    for h in (0, 1):
                        half = n_k // 2
                        sp.dma_start(dst[:, h * half:(h + 1) * half, :],
                                     src[:, n_k * q + h * half:n_k * q + (h + 1) * half, :]
                                     ).then_inc(slot_loaded[s], 16)

            over_pairs(sp, pair)
            for t in range(TT):
                sp.wait_ge(out_ready, t + 1)
                sp.dma_start(out[t * P:(t + 1) * P, :], xhat[:, t, :]).then_inc(out_stored, 16)
            sp.wait_ge(out_stored, 32)

        @block.gpsimd
        def _(pool):
            nc.gpsimd.memset(flatten(siluc), 0.0).then_inc(zeros_ready, 1)
            for v in (conf_pad[:, :, 0:30], sc_pad[:, :, 0:2]):
                nc.gpsimd.memset(v, 0.0).then_inc(zeros_ready, 1)
            for dst, src in ((const2, w["const2"]), (cols2, w["cols2"]), (flatten(cT), w["cT"]),
                             (gate_w, w["w_in_2"][0].rearrange("(k p) n -> p k n", p=P)[:, :, 2048:2064]),
                             (gate_b, w["mlstm_gate_b_2"].partition_broadcast(P)),
                             (flatten(lam_row), w["diff_lambda_2"].rearrange("l a b -> l (a b)").partition_broadcast(P)),
                             (router_b, w["router_b_2"].partition_broadcast(P))):
                pool.dma_start(dst, src).then_inc(early_loaded, 16)
            pool.dma_start(ctx_row, w["ctx_2"].rearrange("b (t p) d -> p (b t) d", p=P)).then_inc(ctx_loaded, 16)
            for l in range(DEPTH):
                if l:
                    pool.wait_ge(x_ready, 2 * l)
                pool.dma_start(cols[:, 0:COL_FFN_PRE], w["cols"][l][:, 0:COL_FFN_PRE]).then_inc(mix_par_loaded, 16)
                pool.dma_start(mix_row[:, 0:D], w["norm_mix_post"][l:l + 1, :].partition_broadcast(P)
                               ).then_inc(mix_par_loaded, 16)
                pool.dma_start(mix_row[:, D:], w["ret_norm_g"][l:l + 1, :].partition_broadcast(P)
                               ).then_inc(mix_par_loaded, 16)
                if l:
                    pool.wait_ge(x_ready, 2 * l + 1)
                pool.dma_start(cols[:, COL_FFN_PRE:N_COLS], w["cols"][l][:, COL_FFN_PRE:N_COLS]).then_inc(ffn_par_loaded, 16)
                pool.dma_start(ffn_row, w["norm_ffn_post"][l:l + 1, :].partition_broadcast(P)
                               ).then_inc(ffn_par_loaded, 16)

            pool.wait_ge(x_ready, 2 * DEPTH)
            for i, c0 in enumerate((2 * D, 5 * D)):
                pool.dma_start(g_rows[:, i, :], w["ada_b_2"][:, c0:c0 + D].partition_broadcast(P)).then_inc(g_bias_loaded, 16)
            take(pool, ("mR", 11), L2)
            pool.dma_start(norm_row, w["mlstm_norm_g_2"].rearrange("l a b -> l (a b)").partition_broadcast(P)
                           ).then_inc(norm_row_loaded, 16)
            pool.wait_ge(h_normed, 1)
            pool.dma_start(norm_row, w["diff_norm_g_2"].rearrange("l a b -> l (a b)").partition_broadcast(P)
                           ).then_inc(norm_row_loaded, 16)
            take(pool, ("O", NHD - 1), L2)
            nc.gpsimd.memset(b1_rows, 0.0).then_inc(b1_zeroed, 1)
            pool.wait_ge(b1_zeroed, 1)
            for dst, src in ((b1_rows[0:N_EXP, :], w["exp_b1_2"][0]), (b2_rows[0:N_EXP, :], w["exp_b2_2"][0]),
                             (router_w, w["router_w_2"][0].rearrange("(k p) e -> p k e", p=P)),
                             (final_row, w["final_norm_g_2"].partition_broadcast(P))):
                pool.dma_start(dst, src).then_inc(late_loaded, 16)

        @block.scalar
        def _(act):
            n_step = [0]

            def step(ins, l):
                n_step[0] += 1
                ins.then_inc(act_step, 1)
                act.wait_ge(act_step, l * ACT_STEPS + n_step[0])

            def flat(v):
                return v.rearrange("p a b -> p (a b)")

            def rms_of(rows, l):
                for t in range(TT):
                    ins = nc.scalar.activation(xhat[:, t, :], rows[t], ACT.Square, accum_out=sumsq[:, t:t + 1])
                step(ins, l)
                nc.scalar.activation(rms, sumsq, ACT.Sqrt, bias=EPS, scale=1.0 / D).then_inc(rms_ready, 1)

            def evac(key, l, out_, in_, func=ACT.Copy, **kw):
                nc.scalar.activation(out_, in_, func, **kw).then_inc(evacuated[bank_of(key)], 1)

            def halves(key, l, dst, scale):
                b = take(act, key, l).rearrange("p (c t) -> p c t", c=2)
                nc.scalar.activation(dst[0:64, 0:NH:2, :], b[0:64], ACT.Copy, scale=scale)
                evac(key, l, dst[64:128, 1:NH:2, :], b[64:128], scale=scale)

            def layer(l):
                n_step[0] = 0
                act.wait_ge(x_ready, 2 * l + 1)
                rms_of([x[:, t, :] for t in range(TT)], l)
                act.wait_ge(mix_par_loaded, 48 * l + 48)
                for i in (0, 2):
                    b = take(act, ("T", i), l)
                    for c in (0, 1):
                        k = 2 * i + c
                        ins = nc.scalar.activation(hT[:, k, :], b[:, c * T:(c + 1) * T], ACT.Copy,
                                                   scale=cols[:, COL_MIX_PRE + k:COL_MIX_PRE + k + 1])
                    ins.then_inc(evacuated[bank_of(("T", i))], 1)

                evac(("s", 1), l, flat(conf_gate), take(act, ("s", 1), l), ACT.Sigmoid)
                halves(("s", 2), l, q_z, SCALE)
                evac(("s", 3), l, flat(kT), take(act, ("s", 3), l))
                evac(("s", 4), l, flat(v_sb), take(act, ("s", 4), l))
                for h in range(NH):
                    evac(("Z", h), l, z[:, h, :], take(act, ("Z", h), l)[:, 0:DIAG])
                evac(("s", 7), l, flat(rv), take(act, ("s", 7), l))
                act.wait_ge(sb_abs, l + 1)
                step(nc.scalar.activation(soft, soft, ACT.Exp, scale=-1.0), l)
                nc.scalar.activation(soft, soft, ACT.Ln, bias=1.0).then_inc(sb_log, 1)
                halves(("RQ", 0), l, rq_z, 1.0)
                evac(("RK", 0), l, flat(rkT), take(act, ("RK", 0), l))
                evac(("s", 8), l, flat(rg), take(act, ("s", 8), l), ACT.Silu)
                evac(("s", 9), l, flat(sc_b), take(act, ("s", 9), l))
                evac(("s", 10), l, flat(sc_c), take(act, ("s", 10), l))
                act.wait_ge(sb_arg, l + 1)
                nc.scalar.activation(z, z, ACT.Exp).then_inc(sb_attn, 1)
                after_evacuation(act, ("CM", 0), l)
                nc.scalar.activation(conf_sq, conf, ACT.Square).then_inc(conf_sq_ready, 1)
                for c in (0, 1):
                    evac(("SB", c), l, catT[:, 2 + c, :], take(act, ("SB", c), l)[:, 0:T])
                evac(("CV", 0), l, conf_gate[:, 0, :], take(act, ("CV", 0), l)[:, 0:T], ACT.Sqrt,
                     bias=EPS, scale=1.0 / GW)
                act.wait_ge(ret_var_ready, l + 1)
                nc.scalar.activation(ret_std, ret_var, ACT.Sqrt, bias=EPS, scale=1.0 / HD).then_inc(ret_std_ready, 1)
                act.wait_ge(conf_normed, l + 1)
                for c in (0, 1):
                    ins = nc.scalar.activation(catT[:, c, :], conf[:, c, :], ACT.Silu,
                                               bias=cols[:, COL_CONF_LB + c:COL_CONF_LB + c + 1],
                                               scale=cols[:, COL_CONF_LG + c:COL_CONF_LG + c + 1])
                ins.then_inc(conf_cat, 1)
                evac(("RT", 0), l, flat(catT[:, 4:6, :]), take(act, ("RT", 0), l))
                for i in range(4):
                    b = take(act, ("M", i), l)
                rms_of([psum[:, 4 + 2 * t:6 + 2 * t, :].rearrange("p b n -> p (b n)") for t in range(TT)], l)
                act.wait_ge(x_ready, 2 * l + 2)
                rms_of([x[:, t, :] for t in range(TT)], l)
                act.wait_ge(ffn_par_loaded, 32 * l + 32)
                for i in (0, 2):
                    b = take(act, ("F", i), l)
                    for c in (0, 1):
                        k = 2 * i + c
                        ins = nc.scalar.activation(hT[:, k, :], b[:, c * T:(c + 1) * T], ACT.Copy,
                                                   scale=cols[:, COL_FFN_PRE + k:COL_FFN_PRE + k + 1])
                    ins.then_inc(evacuated[bank_of(("F", i))], 1)

                def silu(g):
                    after_evacuation(act, ("U", 2 * g), l)
                    nc.scalar.activation(taps[:, g % 2, 0:2, :], taps[:, g % 2, 0:2, :], ACT.Silu).then_inc(silu_ready, 1)

                for g in range(11):
                    if g >= 2:
                        act.wait_ge(ff_ready, l * 11 + g - 1)
                    for u in (0, 1):
                        b = take(act, ("U", 2 * g + u), l)
                        for c in (0, 1):
                            at = COL_FFN_W + (2 * FFC) * 2 + u * FFC + 2 * g + c
                            ins = nc.scalar.activation(taps[:, g % 2, 2 * u + c, :], b[:, c * T:(c + 1) * T],
                                                       ACT.Copy, scale=cols[:, at:at + 1])
                        ins.then_inc(tap_ready, 1)
                    if g:
                        silu(g - 1)
                silu(10)
                for i in range(4):
                    take(act, ("D", i), l)
                rms_of([psum[:, 4 + 2 * t:6 + 2 * t, :].rearrange("p b n -> p (b n)") for t in range(TT)], l)
                assert n_step[0] == ACT_STEPS, n_step

            def second():
                n_step[0] = 0
                l = L2
                act.wait_ge(early_loaded, 112)
                act.wait_ge(zeros_ready, 4)
                nc.scalar.activation(siluc[:, :, 0:2], cT, ACT.Silu).then_inc(siluc_ready, 1)
                for n in range(12):
                    evac(("ada", n), l, ada_rows[:, n % 2, :], take(act, ("ada", n), l))
                act.wait_ge(ctx_loaded, 16)
                act.wait_ge(x_ready, 2 * L2 + 1)
                rms_of([ctx_row[:, t, :] for t in range(TT)], l)
                act.wait_ge(ctx_hat_ready, 1)
                rms_of([x[:, t, :] for t in range(TT)], l)
                act.wait_ge(scale1_ready, 1)
                for key, v, t0 in (("CT", 1, 0), ("XT", 0, T)):
                    for i in (0, 2):
                        b = take(act, (key, i), l)
                        for c in (0, 1):
                            k = 2 * i + c
                            ins = nc.scalar.activation(uT[:, k, t0:t0 + T], b[:, c * T:(c + 1) * T], ACT.Identity,
                                                       scale=scale1[:, v, k:k + 1], bias=shift1[:, v, k:k + 1])
                        ins.then_inc(evacuated[bank_of((key, i))], 1)
                for i in (0, 1):
                    evac(("mq", i), l, flat(m_qT[:, 2 * i:2 * i + 2, :]), take(act, ("mq", i), l), scale=DQK ** -0.5)
                for h in range(NHM):
                    evac(("mk", h), l, m_kT[:, h, :], take(act, ("mk", h), l))
                for i in (0, 1):
                    evac(("mv", i), l, m_v[:, i, 0:2, 0:DV], take(act, ("mv", i), l).rearrange("p (h e) -> p h e", h=2))
                act.wait_ge(gate_abs_ready, 1)
                step(nc.scalar.activation(f_abs, f_abs, ACT.Exp, scale=-1.0), l)
                nc.scalar.activation(f_abs, f_abs, ACT.Ln, bias=1.0).then_inc(gate_log_ready, 1)
                for i in (2, 3, 4, 5, 6, 7):
                    evac(("mv", i), l, m_v[:, i % 4, 2 * (i // 4):2 * (i // 4) + 2, 0:DV],
                         take(act, ("mv", i), l).rearrange("p (h e) -> p h e", h=2))
                for i in range(4):
                    evac(("mo", i), l, o_row[:, i % 2, 512 * (i // 2):512 * (i // 2 + 1)], take(act, ("mo", i), l), ACT.Sigmoid)
                act.wait_ge(m_neg_ready, 1)
                step(nc.scalar.activation(m_neg, m_neg, ACT.Exp), l)
                for h in range(NHM):
                    after_evacuation(act, ("MB", h), l)
                    nc.scalar.activation(flat(decay[h % 2]), flat(decay[h % 2]), ACT.Exp, scale=-1.0).then_inc(decay_exp_ready, 1)
                act.wait_ge(h_ready, NHM)
                for t in range(TT):
                    for h in range(NHM):
                        ins = nc.scalar.activation(flat(decay[0])[:, (t * NHM + h) * DV:(t * NHM + h + 1) * DV], h_row[:, t, h * DV:(h + 1) * DV], ACT.Square,
                                                   accum_out=h_sq[:, t * NHM + h:t * NHM + h + 1])
                step(ins, l)
                nc.scalar.activation(h_rms, h_sq, ACT.Sqrt, bias=EPS, scale=1.0 / DV).then_inc(rms_ready, 1)
                for i in range(4):
                    evac(("AT", i), l, flat(a_outT[:, 2 * i:2 * i + 2, :]), take(act, ("AT", i), l))
                act.wait_ge(lam_sum_ready, 1)
                nc.scalar.activation(lam_exp, lam_sum, ACT.Exp).then_inc(lam_exp_ready, 1)

                def raws(h):
                    if h % 4 == 0:
                        for i in range(4):
                            evac(("dv", h + i), l, d_v[:, i, :], take(act, ("dv", h + i), l))
                    evac(("dq", h), l, raw[:, h % 2, 0:T], take(act, ("dq", h), l)[:, 0:T])
                    b = take(act, ("dk", h), l)
                    nc.scalar.activation(d_kT[:, h % 4, 0:T], b[:, 0:T], ACT.Copy)
                    evac(("dk", h), l, raw[:, h % 2, T:S], b[:, T:S])

                def softmax(h):
                    for t in range(TT):
                        act.wait_ge(row_max_ready, 2 * h + t + 1)
                        for m in (0, 1):
                            b = psum[:, bank_of(("S", 4 * h + 2 * t + m)), :]
                            ins = nc.scalar.activation(probs[:, t, m, :], b, ACT.Exp, bias=neg_max[:, t, m:m + 1],
                                                       scale=DHD ** -0.5, accum_out=row_sum[:, t, m:m + 1])
                            ins.then_inc(evacuated[bank_of(("S", 4 * h + 2 * t + m))], 1)

                def out_of(h):
                    for t in range(TT):
                        evac(("PT", 2 * h + t), l, aT[:, t, :], take(act, ("PT", 2 * h + t), l))
                    evac(("O", h), l, b_row[:, :, h * P:(h + 1) * P],
                         take(act, ("O", h), l)[:, 0:T].rearrange("p (t e) -> p t e", t=TT))

                for h in range(NHD):
                    if h % 4 == 0:
                        raws(h)
                    if h % 4 < 3:
                        raws(h + 1)
                    softmax(h)
                    out_of(h)
                after_evacuation(act, ("O", NHD - 1), l)
                for t in range(TT):
                    for h in range(NHD):
                        ins = nc.scalar.activation(squares[:, (t * NHD + h) * P:(t * NHD + h + 1) * P], b_row[:, t, h * P:(h + 1) * P], ACT.Square,
                                                   accum_out=b_sq[:, t * NHD + h:t * NHD + h + 1])
                step(ins, l)
                nc.scalar.activation(b_rms, b_sq, ACT.Sqrt, bias=EPS, scale=1.0 / P).then_inc(rms_ready, 1)
                for i in range(4):
                    evac(("BT", i), l, flat(b_outT[:, 2 * i:2 * i + 2, :]), take(act, ("BT", i), l))
                for g in (0, 1):
                    for key, dst in (("pa", gate_a), ("pb", gate_bb)):
                        for i in (0, 1):
                            if g:
                                after_evacuation(act, ("wa", i), l) if key == "pa" else act.wait_ge(y_ready, i + 1)
                            evac((key, 2 * g + i), l, dst[:, 512 * i:512 * i + 512], take(act, (key, 2 * g + i), l), ACT.Sigmoid)
                act.wait_ge(x_ready, 2 * L2 + 2)
                rms_of([x[:, t, :] for t in range(TT)], l)
                for i in (0, 2):
                    b = take(act, ("R", i), l)
                    for c in (0, 1):
                        k = 2 * i + c
                        ins = nc.scalar.activation(u2T[:, k, :], b[:, c * T:(c + 1) * T], ACT.Identity,
                                                   scale=scale2[:, k:k + 1], bias=modT[:, 2 * KC + k, 0:1])
                    ins.then_inc(evacuated[bank_of(("R", i))], 1)
                act.wait_ge(mask_ready, 1)
                for t in range(TT):
                    ins = nc.scalar.activation(exps[:, t, 0:N_EXP], logits[:, t, 0:N_EXP], ACT.Exp, bias=neg_top[:, t:t + 1])
                ins.then_inc(exp_ready, 1)
                evac(("gT", 0), l, gT[0:N_EXP, :], take(act, ("gT", 0), l)[0:N_EXP, 0:T])

                def pair(it, j):
                    b = take(act, ("G", 0), it)
                    for k in range(4):
                        ins = nc.scalar.activation(xgT[:, k, :], b[:, k * P:(k + 1) * P], ACT.Identity,
                                                   scale=scale2[:, k:k + 1], bias=modT[:, 2 * KC + k, 0:1])
                    ins.then_inc(evacuated[bank_of(("G", 0))], 1)
                    for n in (0, 1):
                        after_evacuation(act, ("GLU", n), it)
                        nc.scalar.activation(sig[n], glu[n], ACT.Sigmoid, scale=ALPHA).then_inc(sig_ready, 1)
                    evac(("ST", 0), it, spread_T, take(act, ("ST", 0), it)[:, 0:T])
                    evac(("AT2", 0), it, flat(actT[:, 0:4, :]), take(act, ("AT2", 0), it))
                    for n in (0, 1):
                        evac(("OUT", n), it, out_sb[:, 512 * n:512 * n + 512], take(act, ("OUT", n), it))

                over_pairs(act, pair)
                act.wait_ge(x_ready, 2 * L2 + 3)
                rms_of([x[:, t, :] for t in range(TT)], l)

            act.dma_start(x, w["x"].rearrange("b (t p) d -> p (b t) d", p=P)).then_inc(x_loaded, 16)
            act.dma_start(const[:, :], w["const"]).then_inc(const_loaded, 16)
            loop_layers(act, layer)
            second()

        @block.vector
        def _(dve):
            n_step = [0]

            def step(ins, l, wait=True):
                n_step[0] += 1
                ins.then_inc(dve_step, 1)
                if wait:
                    dve.wait_ge(dve_step, l * DVE_STEPS + n_step[0])

            def inverse_rms(l, i):
                dve.wait_ge(rms_ready, 4 * l + i + 1)
                step(nc.vector.reciprocal(rinv, rms), l)

            def normalise(l, i):
                inverse_rms(l, i)
                for t in range(TT):
                    ins = nc.vector.tensor_scalar(xhat[:, t, :], x[:, t, :], rinv[:, t:t + 1], None, ALU.mult)
                ins.then_inc(xhat_ready, 1)

            def add_normed(l, i, keys, gain):
                inverse_rms(l, i)
                for t in range(TT):
                    for n in (0, 1):
                        b = bank_of(keys[2 * t + n])
                        cut = slice(512 * n, 512 * n + 512)
                        ins = nc.vector.scalar_tensor_tensor(out=xhat[:, t, cut], in0=psum[:, b, :],
                                                             scalar=rinv[:, t:t + 1], in1=gain[:, cut],
                                                             op0=ALU.mult, op1=ALU.mult)
                        ins.then_inc(evacuated[b], 1)
                after_evacuation(dve, keys[3], l)
                nc.vector.tensor_tensor(x_row[:, :], x_row[:, :], xhat.rearrange("p t d -> p (t d)"),
                                        ALU.add).then_inc(x_ready, 1)

            def gain_out(key, i, l, col):
                b = take(dve, (key, i), l)
                for c in (0, 1):
                    k = 2 * i + c
                    ins = nc.vector.tensor_scalar(hT[:, k, :], b[:, c * T:(c + 1) * T],
                                                  cols[:, col + k:col + k + 1], None, ALU.mult)
                ins.then_inc(evacuated[bank_of((key, i))], 1)

            def rotate(key, l, dst, ready):
                b = take(dve, key, l)
                d = dst.rearrange("p a b -> p (a b)")
                halves = lambda v: v.rearrange("p (g e) -> p g e", e=HD)
                bs, sn, sw = halves(b), halves(cst("ret_sin")), halves(swapped)
                nc.vector.tensor_tensor(d, b, cst("ret_cos"), ALU.mult)
                nc.vector.tensor_tensor(sw[:, :, 0:32], bs[:, :, 32:64], sn[:, :, 0:32], ALU.mult)
                nc.vector.tensor_tensor(sw[:, :, 32:64], bs[:, :, 0:32], sn[:, :, 32:64], ALU.mult
                                        ).then_inc(evacuated[bank_of(key)], 1)
                after_evacuation(dve, key, l)
                nc.vector.tensor_tensor(d, d, swapped, ALU.add).then_inc(ready, 1)

            def layer(l):
                n_step[0] = 0
                normalise(l, 0)
                dve.wait_ge(mix_par_loaded, 48 * l + 48)
                gain_out("T", 1, l, COL_MIX_PRE)
                gain_out("T", 3, l, COL_MIX_PRE)
                b = take(dve, ("s", 0), l).rearrange("p (c t) -> p c t", c=2)
                after_evacuation(dve, ("s", 1), l)
                nc.vector.tensor_tensor(conf_pad[:, :, 30:30 + T], b, conf_gate, ALU.mult
                                        ).then_inc(evacuated[bank_of(("s", 0))], 1)
                after_evacuation(dve, ("s", 0), l)

                def conf_taps(lo, hi):
                    for k in range(lo, hi):
                        for c in (0, 1):
                            wk = cols[:, COL_CONF_W + 2 * k + c:COL_CONF_W + 2 * k + c + 1]
                            src = conf_pad[:, c, k:k + T]
                            if k == 0:
                                ins = nc.vector.tensor_scalar(conf[:, c, :], src, wk,
                                                              cols[:, COL_CONF_B + c:COL_CONF_B + c + 1],
                                                              ALU.mult, ALU.add)
                            else:
                                dve.wait_ge(dve_step, l * DVE_STEPS + n_step[0] - 1)
                                ins = nc.vector.scalar_tensor_tensor(out=conf[:, c, :], in0=src, scalar=wk,
                                                                     in1=conf[:, c, :], op0=ALU.mult, op1=ALU.add)
                            if k == CONF_K - 1 and c == 1:
                                ins.then_inc(conf_ready, 1)
                            else:
                                step(ins, l, wait=False)

                conf_taps(0, 10)
                rotate(("s", 5), l, rq, rq_ready)
                for h in range(NH):
                    after_evacuation(dve, ("Z", h), l)
                nc.vector.scalar_tensor_tensor(out=soft, in0=z, scalar=-1.0, in1=z, op0=ALU.mult, op1=ALU.max
                                               ).then_inc(sb_abs, 1)
                dve.wait_ge(rq_ready, l + 1)
                rotate(("s", 6), l, rk, rk_ready)
                conf_taps(10, 16)
                dve.wait_ge(sb_log, l + 1)
                step(nc.vector.scalar_tensor_tensor(out=soft, in0=z, scalar=0.0, in1=soft,
                                                    op0=ALU.max, op1=ALU.add), l)
                nc.vector.tensor_tensor(soft, soft, sb_mask4, ALU.mult).then_inc(sb_soft, 1)
                for h in range(NH):
                    b = take(dve, ("RS", h), l)
                    nc.vector.tensor_tensor(r_scores[:, h, :], b[:, 0:DIAG], ret_decay[:, h, :], ALU.mult
                                            ).then_inc(evacuated[bank_of(("RS", h))], 1)
                conf_taps(16, 20)
                for h in range(NH):
                    b = take(dve, ("I", h), l)
                    nc.vector.tensor_tensor(z[:, h, :], z[:, h, :], b[:, 0:DIAG], ALU.subtract
                                            ).then_inc(evacuated[bank_of(("I", h))], 1)
                after_evacuation(dve, ("I", 3), l)
                nc.vector.tensor_tensor(z, z, sb_neg4, ALU.add).then_inc(sb_arg, 1)
                conf_taps(20, CONF_K)
                b = take(dve, ("s", 11), l).rearrange("p (c t) -> p c t", c=2)
                after_evacuation(dve, ("s", 10), l)
                nc.vector.tensor_tensor(sc_pad[:, :, 2:2 + T], b, sc_c, ALU.mult
                                        ).then_inc(evacuated[bank_of(("s", 11))], 1)
                after_evacuation(dve, ("s", 11), l)
                for k in range(SC_K):
                    for c in (0, 1):
                        wk = cols[:, COL_SC_W + 2 * k + c:COL_SC_W + 2 * k + c + 1]
                        src = sc_pad[:, c, k:k + T]
                        if k == 0:
                            step(nc.vector.tensor_scalar(sc_c[:, c, :], src, wk, None, ALU.mult), l, wait=False)
                        else:
                            dve.wait_ge(dve_step, l * DVE_STEPS + n_step[0] - 1)
                            step(nc.vector.scalar_tensor_tensor(out=sc_c[:, c, :], in0=src, scalar=wk,
                                                                in1=sc_c[:, c, :], op0=ALU.mult, op1=ALU.add),
                                 l, wait=k == SC_K - 1 and c == 1)
                after_evacuation(dve, ("s", 9), l)
                nc.vector.tensor_tensor(catT[:, 6:8, :], sc_c, sc_b, ALU.mult).then_inc(sc_cat, 1)
                b = take(dve, ("CM", 0), l)
                for c in (0, 1):
                    ins = nc.vector.scalar_tensor_tensor(out=conf[:, c, :], in0=b[:, 0:T], scalar=-1.0 / GW,
                                                         in1=conf[:, c, :], op0=ALU.mult, op1=ALU.add)
                ins.then_inc(evacuated[bank_of(("CM", 0))], 1)
                b = take(dve, ("RO", 0), l).rearrange("p (g e) -> p g e", e=HD)
                retg = ret.rearrange("p a b -> p (a b)").rearrange("p (g e) -> p g e", e=HD)
                sqg = swapped.rearrange("p (g e) -> p g e", e=HD)
                wide = lambda v: v.unsqueeze(2).broadcast_to([P, 8, HD])
                step(nc.vector.tensor_reduce(ret_mu, b, AX, ALU.add), l)
                step(nc.vector.tensor_scalar(ret_mu, ret_mu, 1.0 / HD, None, ALU.mult), l)
                take(dve, ("CV", 0), l)
                nc.vector.tensor_tensor(retg, b, wide(ret_mu), ALU.subtract).then_inc(evacuated[bank_of(("RO", 0))], 1)
                after_evacuation(dve, ("RO", 0), l)
                step(nc.vector.tensor_tensor(sqg, retg, retg, ALU.mult), l)
                nc.vector.tensor_reduce(ret_var, sqg, AX, ALU.add).then_inc(ret_var_ready, 1)
                after_evacuation(dve, ("CV", 0), l)
                step(nc.vector.reciprocal(conf_gate[:, 1, :], conf_gate[:, 0, :]), l)
                nc.vector.tensor_tensor(conf, conf, conf_gate[:, 1:2, :].broadcast_to([P, 2, T]), ALU.mult
                                        ).then_inc(conf_normed, 1)
                dve.wait_ge(ret_std_ready, l + 1)
                step(nc.vector.reciprocal(ret_rinv, ret_std), l)
                step(nc.vector.tensor_tensor(retg, retg, wide(ret_rinv), ALU.mult), l)
                gain = mix_row[:, D:].unsqueeze(1).broadcast_to([P, TT, GW])
                step(nc.vector.tensor_tensor(ret, ret, gain, ALU.mult), l)
                after_evacuation(dve, ("s", 8), l)
                nc.vector.tensor_tensor(ret, ret, rg, ALU.mult).then_inc(ret_ready, 1)
                add_normed(l, 1, [("M", i) for i in range(4)], mix_row)
                dve.wait_ge(x_ready, 2 * l + 2)
                normalise(l, 2)
                dve.wait_ge(ffn_par_loaded, 32 * l + 32)
                gain_out("F", 1, l, COL_FFN_PRE)
                gain_out("F", 3, l, COL_FFN_PRE)

                def product(g):
                    dve.wait_ge(silu_ready, l * 11 + g + 1)
                    nc.vector.tensor_tensor(ffT[:, 2 * g:2 * g + 2, :], taps[:, g % 2, 0:2, :], taps[:, g % 2, 2:4, :],
                                            ALU.mult).then_inc(ff_ready, 1)

                for g in range(11):
                    for u in (0, 1):
                        b = take(dve, ("U", 2 * g + u), l)
                        dve.wait_ge(tap_ready, l * 22 + 2 * g + u + 1)
                        for k in (1, 2):
                            for c in (0, 1):
                                at = COL_FFN_W + (2 * FFC) * (2 - k) + u * FFC + 2 * g + c
                                o = taps[:, g % 2, 2 * u + c, k:T]
                                ins = nc.vector.scalar_tensor_tensor(
                                    out=o, in0=b[:, c * T:(c + 1) * T - k], scalar=cols[:, at:at + 1], in1=o,
                                    op0=ALU.mult, op1=ALU.add)
                                if k == 1:
                                    step(ins, l, wait=c == 1)
                        ins.then_inc(evacuated[bank_of(("U", 2 * g + u))], 1)
                        if u == 0:
                            after_evacuation(dve, ("U", 2 * g), l)
                            if g:
                                product(g - 1)
                after_evacuation(dve, ("U", 21), l)
                product(10)
                add_normed(l, 3, [("D", i) for i in range(4)], ffn_row)
                assert n_step[0] == DVE_STEPS, n_step

            def ptr_affine(key, v, i, l):
                b = take(dve, (key, i), l)
                t0 = 0 if key == "CT" else T
                for c in (0, 1):
                    k = 2 * i + c
                    ins = nc.vector.tensor_scalar(uT[:, k, t0:t0 + T], b[:, c * T:(c + 1) * T], scale1[:, v, k:k + 1],
                                                  shift1[:, v, k:k + 1], ALU.mult, ALU.add)
                ins.then_inc(evacuated[bank_of((key, i))], 1)

            def second():
                n_step[0] = 0
                l = L2
                norm_g = cols2[:, 0:2 * KC].rearrange("p (a k) -> p a k", a=2)
                ada_b = cols2[:, 2 * KC:6 * KC].unsqueeze(2).broadcast_to([P, 4 * KC, 2])
                dve.wait_ge(early_loaded, 112)
                step(nc.vector.tensor_copy(iota, cst2("iota")), l, wait=False)
                pairs = lam_row.rearrange("p (a b) e -> p a b e", b=2)
                step(nc.vector.tensor_tensor(lam_prod, pairs[:, :, 0, :], pairs[:, :, 1, :], ALU.mult), l)
                nc.vector.tensor_reduce(lam_sum, lam_prod, AX, ALU.add).then_inc(lam_sum_ready, 1)
                dve.wait_ge(g_bias_loaded, 32)

                def spread_rows(n):
                    i = 0 if n < 6 else 1
                    cut = slice(512 * (n % 2), 512 * (n % 2) + 512)
                    b = take(dve, ("mR", n), l)
                    nc.vector.tensor_tensor(g_rows[:, i, cut], g_rows[:, i, cut], b, ALU.add
                                            ).then_inc(evacuated[bank_of(("mR", n))], 1)

                def mod_columns(i):
                    b = take(dve, ("mT", i), l)[:, 0:32].rearrange("p (k v) -> p k v", v=2)
                    nc.vector.tensor_tensor(modT[:, 16 * i:16 * i + 16, :], b, ada_b[:, 16 * i:16 * i + 16, :], ALU.add
                                            ).then_inc(evacuated[bank_of(("mT", i))], 1)
                    after_evacuation(dve, ("mT", i), l)

                mod_columns(0)
                for v in (0, 1):
                    step(nc.vector.tensor_copy(shift1[:, v, :], modT[:, 0:KC, v]), l, wait=False)
                    ins = nc.vector.scalar_tensor_tensor(out=scale1[:, v, :], in0=modT[:, KC:2 * KC, v], scalar=1.0,
                                                         in1=norm_g[:, 0, :], op0=ALU.add, op1=ALU.mult)
                    ins.then_inc(scale1_ready, 1) if v else step(ins, l, wait=False)
                spread_rows(4)
                spread_rows(5)
                mod_columns(1)
                step(nc.vector.scalar_tensor_tensor(out=scale2, in0=modT[:, 3 * KC:4 * KC, 0], scalar=1.0,
                                                    in1=norm_g[:, 1, :], op0=ALU.add, op1=ALU.mult), l, wait=False)
                spread_rows(10)
                spread_rows(11)
                inverse_rms(l, 0)
                for t in range(TT):
                    ins = nc.vector.tensor_scalar(ctx_row[:, t, :], ctx_row[:, t, :], rinv[:, t:t + 1], None, ALU.mult)
                ins.then_inc(ctx_hat_ready, 1)
                dve.wait_ge(ctx_hat_ready, 1)
                normalise(l, 1)
                dve.wait_ge(scale1_ready, 1)
                for key, v in (("CT", 1), ("XT", 0)):
                    ptr_affine(key, v, 1, l)
                    ptr_affine(key, v, 3, l)
                ones_col = m_v[:, :, :, DV:DV + 1]
                step(nc.vector.memset(ones_col, 1.0), l, wait=False)
                for d in (0, 1):
                    for i in (0, 1):
                        step(nc.vector.memset(cummax[d][i], 0.0), l, wait=False)
                b = take(dve, ("mg", 0), l)[:, 0:ST * 16].rearrange("p (s n) -> p s n", n=16)
                nc.vector.tensor_tensor(gates, b, gate_b.unsqueeze(1).broadcast_to([P, ST, 16]), ALU.add
                                        ).then_inc(evacuated[bank_of(("mg", 0))], 1)
                after_evacuation(dve, ("mg", 0), l)
                by_dir = gates.rearrange("p s (d g h) -> p (s d) g h", d=2, g=2)
                in_gate, f_gate = by_dir[:, :, 0, :], by_dir[:, :, 1, :]
                step(nc.vector.tensor_scalar(f_neg, f_gate, -1.0, None, ALU.mult), l, wait=False)
                step(nc.vector.tensor_scalar(f_min, f_gate, 0.0, None, ALU.min), l)
                nc.vector.tensor_tensor(f_abs, f_gate, f_neg, ALU.max).then_inc(gate_abs_ready, 1)
                dve.wait_ge(gate_log_ready, 1)
                nc.vector.tensor_tensor(log_f, f_min, f_abs, ALU.subtract).then_inc(gate_ready, 1)
                b = take(dve, ("F", 9), l)
                f_sum = b[:, 0:32].rearrange("p (s h) -> p s h", h=4)
                step(nc.vector.tensor_copy(f_neg[:, 0:4, :], f_sum[:, 4:8, :]), l, wait=False)
                nc.vector.tensor_tensor(g_sub.rearrange("p s (d h) -> p (s d) h", d=2), in_gate, f_sum, ALU.subtract
                                        ).then_inc(evacuated[bank_of(("F", 9))], 1)
                for d in (0, 1):
                    b = take(dve, ("GT", d), l)[0:NHM, :]
                    step(nc.vector.tensor_reduce(ctx_max[0:NHM, d:d + 1], b[:, 0:T], AX, ALU.max), l)
                    step(nc.vector.tensor_scalar(ctx_max[0:NHM, d:d + 1], ctx_max[0:NHM, d:d + 1], 0.0, None, ALU.max), l)
                    at0 = P * (1 - d)
                    nc.vector.tensor_scalar(cummax[d][0][:, at0:at0 + T], b[:, T:S], ctx_max[0:NHM, d:d + 1], None,
                                            ALU.max).then_inc(evacuated[bank_of(("GT", d))], 1)
                    after_evacuation(dve, ("GT", d), l)
                for i in range(8):
                    for d in (0, 1):
                        src, dst = cummax[d][i % 2], cummax[d][(i + 1) % 2]
                        at0, shift = P * (1 - d), (1 << i) * (2 * d - 1)
                        ins = nc.vector.tensor_tensor(dst[:, at0:at0 + T], src[:, at0:at0 + T],
                                                      src[:, at0 + shift:at0 + shift + T], ALU.max)
                        if i == 7 and d == 1:
                            ins.then_inc(cummax_ready, 1)
                        else:
                            step(ins, l, wait=d == 1)
                b = take(dve, ("MR", 0), l)[:, 0:16].rearrange("p (s h) -> p s h", h=4)
                mn = m_neg.rearrange("p (s h) -> p s h", h=4)
                nc.vector.scalar_tensor_tensor(out=mn, in0=b, scalar=-1.0, in1=f_neg[:, 0:4, :],
                                               op0=ALU.mult, op1=ALU.subtract).then_inc(evacuated[bank_of(("MR", 0))], 1)
                after_evacuation(dve, ("MR", 0), l)
                nc.vector.tensor_scalar(m_neg, m_neg, 88.0, None, ALU.min).then_inc(m_neg_ready, 1)

                def decay_args(h):
                    b = take(dve, ("MB", h), l)
                    if h >= 2:
                        take(dve, ("H", 4 * (h - 2) + 3), l)
                    for d in (0, 1):
                        for st in range(ST):
                            g = g_sub[:, st, 4 * d + h:4 * d + h + 1]
                            ins = nc.vector.tensor_scalar(decay[h % 2][:, d, st * T:(st + 1) * T], b[:, d * T:(d + 1) * T],
                                                          g, 0.0, ALU.subtract, ALU.max)
                            if d == 0 or st < ST - 1:
                                step(ins, l, wait=False)
                    ins.then_inc(evacuated[bank_of(("MB", h))], 1)

                def weigh(h):
                    dve.wait_ge(decay_exp_ready, h + 1)
                    for d, tri in ((0, cst2("prefix")), (1, suffix)):
                        for t in range(TT):
                            v = decay[h % 2][:, d, (TT + t) * T + t * P:(TT + t) * T + (t + 1) * P]
                            step(nc.vector.tensor_tensor(v, v, tri, ALU.mult), l, wait=d == 1 and t == 1)
                    for q in (0, 1):
                        b = take(dve, ("QK", 2 * h + q), l)
                        for d in (0, 1):
                            v = decay[h % 2][:, d, 512 * q:512 * q + 512]
                            ins = nc.vector.tensor_tensor(v, v, b, ALU.mult)
                            if d == 0:
                                step(ins, l, wait=False)
                        ins.then_inc(evacuated[bank_of(("QK", 2 * h + q))], 1)

                def outputs(h):
                    for d in (0, 1):
                        for t in range(TT):
                            b = take(dve, ("H", 4 * h + 2 * d + t), l)
                            i = 2 * d + t
                            step(nc.vector.tensor_scalar(den[:, i:i + 1], b[:, DV:DV + 1], -1.0, None, ALU.mult), l)
                            step(nc.vector.tensor_tensor(den[:, i:i + 1], den[:, i:i + 1], b[:, DV:DV + 1], ALU.max), l)
                            e = m_neg[:, 4 * (2 * t + d) + h:4 * (2 * t + d) + h + 1]
                            step(nc.vector.tensor_tensor(den[:, i:i + 1], den[:, i:i + 1], e, ALU.max), l)
                            step(nc.vector.reciprocal(den2[:, i:i + 1], den[:, i:i + 1]), l)
                            o = h_row[:, t, h * DV:(h + 1) * DV]
                            if d == 0:
                                ins = nc.vector.tensor_scalar(o, b[:, 0:DV], den2[:, i:i + 1], None, ALU.mult)
                            else:
                                after_evacuation(dve, ("H", 4 * h + t), l)
                                ins = nc.vector.scalar_tensor_tensor(out=o, in0=b[:, 0:DV], scalar=den2[:, i:i + 1],
                                                                     in1=o, op0=ALU.mult, op1=ALU.add)
                            ins.then_inc(evacuated[bank_of(("H", 4 * h + i))], 1)
                    after_evacuation(dve, ("H", 4 * h + 3), l)
                    dve.sem_inc(h_ready, 1)

                decay_args(0)
                weigh(0)
                for h in range(1, NHM + 1):
                    if h < NHM:
                        decay_args(h)
                    if h < NHM:
                        weigh(h)
                    outputs(h - 1)
                dve.wait_ge(rms_ready, 4 * L2 + 3)
                dve.wait_ge(norm_row_loaded, 16)
                step(nc.vector.reciprocal(h_inv, h_rms), l)
                for t in range(TT):
                    for h in range(NHM):
                        v = h_row[:, t, h * DV:(h + 1) * DV]
                        i = t * NHM + h
                        step(nc.vector.scalar_tensor_tensor(out=v, in0=v, scalar=h_inv[:, i:i + 1],
                                                            in1=norm_row[:, h * DV:(h + 1) * DV],
                                                            op0=ALU.mult, op1=ALU.mult), l, wait=i == 2 * NHM - 1)
                after_evacuation(dve, ("mo", 3), l)
                nc.vector.tensor_tensor(h_row, h_row, o_row, ALU.mult).then_inc(h_normed, 1)
                dve.wait_ge(lam_exp_ready, 1)
                step(nc.vector.tensor_tensor(neg_lam, lam_exp[:, 1:2], lam_exp[:, 0:1], ALU.subtract), l)
                step(nc.vector.tensor_scalar(neg_lam, neg_lam, -LAM_INIT, None, ALU.add), l)
                for h in range(4):
                    step(nc.vector.memset(d_q[0:64, 2 * h + 1, :], 0.0), l, wait=False)
                    step(nc.vector.memset(d_q[64:128, 2 * h, :], 0.0), l, wait=False)
                cos2 = cst2("rope_cos").unsqueeze(1).broadcast_to([P, 2, T])
                sin2 = cst2("rope_sin").unsqueeze(1).broadcast_to([P, 2, T])

                def rope(h):
                    b = take(dve, ("rot", h), l)
                    r = raw[:, h % 2, :]
                    two = lambda v: v.rearrange("p (a t) -> p a t", a=2)
                    step(nc.vector.tensor_tensor(two(r), two(r), cos2, ALU.mult), l, wait=False)
                    if h:
                        dve.wait_ge(qk_ready, h)
                    nc.vector.tensor_tensor(two(turned), two(b), sin2, ALU.mult).then_inc(evacuated[bank_of(("rot", h))], 1)
                    after_evacuation(dve, ("rot", h), l)
                    if h >= 4:
                        take(dve, ("S", 4 * (h - 4) + 3), l)
                    for m in (0, 1):
                        rows = slice(64 * m, 64 * m + 64)
                        step(nc.vector.tensor_tensor(d_q[rows, 2 * (h % 4) + m, :], r[rows, 0:T], turned[rows, 0:T], ALU.add),
                             l, wait=False)
                    nc.vector.tensor_tensor(d_kT[:, h % 4, T:S], r[:, T:S], turned[:, T:S], ALU.add).then_inc(qk_ready, 1)

                def maxima(h):
                    for t in range(TT):
                        for m in (0, 1):
                            b = take(dve, ("S", 4 * h + 2 * t + m), l)
                            step(nc.vector.tensor_reduce(row_max[:, t, m:m + 1], b, AX, ALU.max), l, wait=m == 1)
                        nc.vector.tensor_scalar(neg_max[:, t, :], row_max[:, t, :], -DHD ** -0.5, None, ALU.mult
                                                ).then_inc(row_max_ready, 1)

                def difference(h):
                    for t in range(TT):
                        after_evacuation(dve, ("S", 4 * h + 2 * t), l)
                        after_evacuation(dve, ("S", 4 * h + 2 * t + 1), l)
                        step(nc.vector.reciprocal(row_inv[:, t, :], row_sum[:, t, :]), l)
                        step(nc.vector.tensor_tensor(map_scale[:, t, 0:1], row_inv[:, t, 1:2], neg_lam, ALU.mult), l)
                        p1 = probs[:, t, 1, :]
                        step(nc.vector.tensor_scalar(p1, p1, map_scale[:, t, 0:1], None, ALU.mult), l)
                        p0 = probs[:, t, 0, :]
                        nc.vector.scalar_tensor_tensor(out=p0, in0=p0, scalar=row_inv[:, t, 0:1], in1=p1,
                                                       op0=ALU.mult, op1=ALU.add).then_inc(attn_ready, 1)

                for h in range(NHD):
                    if h % 4 == 0:
                        rope(h)
                    maxima(h)
                    if h % 4 < 3:
                        rope(h + 1)
                    difference(h)
                dve.wait_ge(rms_ready, 4 * L2 + 4)
                dve.wait_ge(norm_row_loaded, 32)
                step(nc.vector.reciprocal(b_inv, b_rms), l)
                step(nc.vector.tensor_scalar(b_inv, b_inv, 1.0 - LAM_INIT, None, ALU.mult), l)
                for t in range(TT):
                    for h in range(NHD):
                        v = b_row[:, t, h * P:(h + 1) * P]
                        i = t * NHD + h
                        ins = nc.vector.scalar_tensor_tensor(out=v, in0=v, scalar=b_inv[:, i:i + 1],
                                                             in1=norm_row[:, h * P:(h + 1) * P], op0=ALU.mult, op1=ALU.mult)
                        if i < 2 * NHD - 1:
                            step(ins, l, wait=False)
                ins.then_inc(b_normed, 1)
                for g in (0, 1):
                    for i in (0, 1):
                        cut = slice(512 * i, 512 * i + 512)
                        y = flatten(yT[:, 4 * g + 2 * i:4 * g + 2 * i + 2, :])
                        b = take(dve, ("wa", 2 * g + i), l)
                        after_evacuation(dve, ("pa", 2 * g + i), l)
                        nc.vector.tensor_tensor(y, b, gate_a[:, cut], ALU.mult
                                                ).then_inc(evacuated[bank_of(("wa", 2 * g + i))], 1)
                        b = take(dve, ("wb", 2 * g + i), l)
                        after_evacuation(dve, ("pb", 2 * g + i), l)
                        nc.vector.tensor_tensor(gate_bb[:, cut], b, gate_bb[:, cut], ALU.mult
                                                ).then_inc(evacuated[bank_of(("wb", 2 * g + i))], 1)
                        after_evacuation(dve, ("wa", 2 * g + i), l)
                        after_evacuation(dve, ("wb", 2 * g + i), l)
                        nc.vector.tensor_tensor(y, y, gate_bb[:, cut], ALU.add).then_inc(y_ready, 1)
                for i in range(4):
                    t, half = divmod(i, 2)
                    cut = slice(512 * half, 512 * half + 512)
                    b = take(dve, ("Y", i), l)
                    nc.vector.tensor_tensor(xhat[:, t, cut], b, g_rows[:, 0, cut], ALU.mult
                                            ).then_inc(evacuated[bank_of(("Y", i))], 1)
                after_evacuation(dve, ("Y", 3), l)
                nc.vector.tensor_tensor(x_row[:, :], x_row[:, :], flatten(xhat), ALU.add).then_inc(x_ready, 1)
                dve.wait_ge(x_ready, 2 * L2 + 2)
                normalise(l, 4)
                for i in (1, 3):
                    b = take(dve, ("R", i), l)
                    for c in (0, 1):
                        k = 2 * i + c
                        ins = nc.vector.tensor_scalar(u2T[:, k, :], b[:, c * T:(c + 1) * T], scale2[:, k:k + 1],
                                                      modT[:, 2 * KC + k, 0:1], ALU.mult, ALU.add)
                    ins.then_inc(evacuated[bank_of(("R", i))], 1)
                below = -3e38
                step(nc.vector.memset(logits[:, :, N_EXP:], below), l, wait=False)
                b = take(dve, ("L", 0), l)[:, 0:TT * N_EXP].rearrange("p (t e) -> p t e", t=TT)
                nc.vector.tensor_tensor(logits[:, :, 0:N_EXP], b, router_b.unsqueeze(1).broadcast_to([P, TT, N_EXP]), ALU.add
                                        ).then_inc(evacuated[bank_of(("L", 0))], 1)
                after_evacuation(dve, ("L", 0), l)
                for t in range(TT):
                    step(nc.vector.max(top8[:, t, :], logits[:, t, 0:N_EXP]), l, wait=t == 1)
                step(nc.vector.tensor_scalar(neg_top, top8[:, :, 0], -1.0, None, ALU.mult), l, wait=False)
                step(nc.vector.memset(top8[:, :, TOP_K:], below), l)
                for t in range(TT):
                    step(nc.vector.match_replace(others[:, t, :], top8[:, t, :], logits[:, t, :], below), l, wait=t == 1)
                nc.vector.tensor_tensor(chosen, logits[:, :, 0:N_EXP], others[:, :, 0:N_EXP], ALU.not_equal
                                        ).then_inc(mask_ready, 1)
                dve.wait_ge(exp_ready, 1)
                step(nc.vector.tensor_tensor(gate_row, exps[:, :, 0:N_EXP], chosen, ALU.mult), l)
                step(nc.vector.tensor_reduce(gate_sum, gate_row, AX, ALU.add), l)
                step(nc.vector.reciprocal(gate_inv, gate_sum), l)
                nc.vector.tensor_tensor(gate_row, gate_row, gate_inv.unsqueeze(2).broadcast_to([P, TT, N_EXP]), ALU.mult
                                        ).then_inc(gates_ready, 1)
                by_pair = lambda v: v.rearrange("p (j t x) -> p t j x", j=PAIRS, t=TT)
                pairs = lambda v: v.rearrange("p (j x) -> p j x", x=2)
                dve.wait_ge(gates_ready, 1)
                b = take(dve, ("PC", 0), l)
                for t in range(TT):
                    step(nc.vector.tensor_copy(by_pair(pair_gate)[:, t], pairs(gate_row[:, t, :])), l, wait=False)
                    ins = nc.vector.scalar_tensor_tensor(out=by_pair(pair_slot)[:, t], in0=pairs(b[:, t * N_EXP:(t + 1) * N_EXP]),
                                                         scalar=1.0, in1=pairs(chosen[:, t, :]), op0=ALU.add, op1=ALU.mult)
                    if t == 0:
                        step(ins, l, wait=False)
                ins.then_inc(evacuated[bank_of(("PC", 0))], 1)
                after_evacuation(dve, ("PC", 0), l)
                step(nc.vector.tensor_scalar(pair_slot, pair_slot, -1.0, None, ALU.add), l)
                b = take(dve, ("CN", 0), l)
                nc.vector.tensor_reduce(most, b[:, 0:N_EXP], AX, ALU.max).then_inc(evacuated[bank_of(("CN", 0))], 1)
                after_evacuation(dve, ("CN", 0), l)
                step(nc.vector.tensor_scalar(n_pass, most, float(CAP), 1.0, ALU.is_gt, ALU.add), l)
                for k in range(2, T // CAP):
                    step(nc.vector.scalar_tensor_tensor(out=n_pass, in0=most, scalar=float(k * CAP), in1=n_pass,
                                                        op0=ALU.is_gt, op1=ALU.add), l)
                nc.vector.tensor_copy(passes[:, :], n_pass).then_inc(passes_ready, 1)
                slots4 = iota.unsqueeze(1).broadcast_to([P, 4, CAP])

                def pair(it, j):
                    n_pair_step = [0]

                    def pair_step(ins):
                        n_pair_step[0] += 1
                        ins.then_inc(pairs_step, 1)
                        dve.wait_ge(pairs_step, 5 * it + n_pair_step[0])

                    four = pair_slot[:, bass.ds(4 * j, 4)]
                    to_slots = lambda v: v.rearrange("p t (x s) -> p (t x) s", x=2)
                    pair_step(nc.vector.tensor_tensor(to_slots(pick), slots4, four.unsqueeze(2).broadcast_to([P, 4, CAP]),
                                                      ALU.is_equal))
                    nc.vector.tensor_copy(pick_e.rearrange("p (x s) -> p x s", x=2),
                                          ident[:, bass.ds(2 * j, 2)].unsqueeze(2).broadcast_to([P, 2, CAP]))
                    pair_step(nc.vector.tensor_scalar(four, four, -float(CAP), None, ALU.add))
                    nc.vector.tensor_tensor(to_slots(pick_gated), to_slots(pick),
                                            pair_gate[:, bass.ds(4 * j, 4)].unsqueeze(2).broadcast_to([P, 4, CAP]),
                                            ALU.mult).then_inc(picks_ready, 1)
                    b = take(dve, ("G", 1), it)
                    for k in range(4):
                        ins = nc.vector.tensor_scalar(xgT[:, 4 + k, :], b[:, k * P:(k + 1) * P], scale2[:, 4 + k:5 + k],
                                                      modT[:, 2 * KC + 4 + k, 0:1], ALU.mult, ALU.add)
                    ins.then_inc(evacuated[bank_of(("G", 1))], 1)
                    for n in (0, 1):
                        nc.vector.tensor_scalar(glu[n], take(dve, ("GLU", n), it), LIMIT, None, ALU.min
                                                ).then_inc(evacuated[bank_of(("GLU", n))], 1)
                        nc.vector.tensor_scalar(lin[n], take(dve, ("LIN", n), it), LIMIT, -LIMIT, ALU.min, ALU.max
                                                ).then_inc(evacuated[bank_of(("LIN", n))], 1)
                        after_evacuation(dve, ("LIN", n), it)
                        pair_step(nc.vector.scalar_tensor_tensor(out=lin[n], in0=lin[n], scalar=1.0, in1=glu[n],
                                                                 op0=ALU.add, op1=ALU.mult))
                        dve.wait_ge(sig_ready, 2 * it + (n + 1))
                        nc.vector.tensor_tensor(act_[n], lin[n], sig[n], ALU.mult).then_inc(hidden_ready, 1)
                    nc.vector.tensor_copy(flatten(actT[:, 4:8, :]), take(dve, ("AT2", 1), it)
                                          ).then_inc(evacuated[bank_of(("AT2", 1))], 1)
                    dve.sem_inc(pairs_step, 1)

                n = over_pairs(dve, pair)
                dve.wait_ge(late_loaded, 64)
                dve.wait_ge(combined, n * PAIRS)
                for i in range(4):
                    t, half = divmod(i, 2)
                    cut = slice(512 * half, 512 * half + 512)
                    step(nc.vector.tensor_tensor(xhat[:, t, cut], psum[:, i, :], g_rows[:, 1, cut], ALU.mult), l, wait=i == 3)
                nc.vector.tensor_tensor(x_row[:, :], x_row[:, :], flatten(xhat), ALU.add).then_inc(x_ready, 1)
                dve.wait_ge(x_ready, 2 * L2 + 3)
                inverse_rms(l, 5)
                for t in range(TT):
                    nc.vector.scalar_tensor_tensor(out=xhat[:, t, :], in0=x[:, t, :], scalar=rinv[:, t:t + 1], in1=final_row,
                                                   op0=ALU.mult, op1=ALU.mult).then_inc(out_ready, 1)

            for v in (q_z, rq_z):
                nc.vector.memset(v[0:64, 1:NH:2, :], 0.0)
                ins = nc.vector.memset(v[64:128, 0:NH:2, :], 0.0)
            ins.then_inc(zeros_ready, 1)
            dve.wait_ge(const_loaded, 16)
            dve.wait_ge(zeros_ready, 4)
            dve.wait_ge(x_loaded, 16)
            dve.sem_inc(x_ready, 1)
            loop_layers(dve, layer)
            second()

        @block.tensor
        def _(pe):
            def mm(out_, lhsT, rhs, first=True, last=True):
                return nc.tensor.matmul(out_, lhsT, rhs, start=first, stop=last)

            def done(ins, key):
                ins.then_inc(filled[bank_of(key)], 1)

            def transposed(key0, l, n, rows=xhat):
                if n:
                    pe.wait_ge(xhat_ready, 2 * l + n)
                for i in range(4):
                    b = fill(pe, (key0, i), l)
                    for c in (0, 1):
                        for t in range(TT):
                            k = 2 * i + c
                            ins = nc.tensor.transpose(b[:, c * T + t * P:c * T + (t + 1) * P],
                                                      rows[:, t, k * P:(k + 1) * P], ident)
                    done(ins, (key0, i))
                for i in range(4):
                    after_evacuation(pe, (key0, i), l)

            def transposed_pair(key, l, rows):
                b = fill(pe, key, l)
                for c in (0, 1):
                    for t in range(TT):
                        ins = nc.tensor.transpose(b[:, c * T + t * P:c * T + (t + 1) * P],
                                                  rows[:, t, c * P:(c + 1) * P], ident)
                done(ins, key)

            def diagonal_scores(key, l, keysT, queries, h):
                b = fill(pe, (key, h), l)
                mm(b[:, 0:T], keysT[:, h // 2, 0:P], queries[:, h, :])
                done(mm(b[:, T:DIAG], keysT[:, h // 2, P:T], queries[:, h, P:T]), (key, h))

            def tokens_down(key, l, n, lhs, first_k, n_k, ks, last_slot):
                wt = slot_ready(pe, n, l).rearrange("p (k n) -> p k n", k=4)
                for i in range(4):
                    t, half = divmod(i, 2)
                    for k in range(n_k):
                        kk = first_k + k
                        ins = mm(psum[:, bank_of((key, i)), :], lhs[:, kk, t * P:(t + 1) * P],
                                 wt[:, k, half * 512:(half + 1) * 512], kk == 0, kk == ks - 1)
                    if last_slot:
                        done(ins, (key, i))
                if not last_slot:
                    ins.then_inc(expert_slot_free if key == "Y" else slot_free, 1)

            def second():
                l = L2
                n_slot = [0]

                def next_slot(kind, s):
                    assert B2_SLOTS[n_slot[0]] == (kind, s)
                    n_slot[0] += 1
                    return slot_ready(pe, n_slot[0] - 1, l).rearrange("p (k n) -> p k n", k=KC)

                def summed(b, lhs, rhs, n_k=KC):
                    for k in range(n_k):
                        ins = mm(b, lhs(k), rhs(k), k == 0, k == n_k - 1)
                    return ins

                pe.wait_ge(siluc_ready, 1)

                def ada_follow(n):
                    after_evacuation(pe, ("ada", n), l)
                    rows = ada_rows[:, n % 2, :]
                    if n in (4, 5, 10, 11):
                        b = fill(pe, ("mR", n), l)
                        done(mm(b, cst2("spread"), rows), ("mR", n))
                    else:
                        i, j = (0, n) if n < 4 else (1, n - 6)
                        b = psum[:, bank_of(("mT", i)), :]
                        if j == 0:
                            fill(pe, ("mT", i), l)
                        for c in range(4):
                            at_ = 8 * j + 2 * c
                            ins = mm(b[:, at_:at_ + 2], rows[:, c * P:(c + 1) * P], cst2("pick"))
                        if j == 3:
                            done(ins, ("mT", i))

                for n in range(12):
                    wt = next_slot("ada", n)
                    b = fill(pe, ("ada", n), l)
                    for k in range(KC):
                        q = k % 4
                        ins = mm(b[32 * q:32 * q + 32, :], siluc[:, k, :], wt[:, k, :], k < 4, k >= 4)
                    done(ins, ("ada", n))
                    if n:
                        ada_follow(n - 1)
                ada_follow(11)
                pe.wait_ge(ctx_hat_ready, 1)
                transposed("CT", l, 0, ctx_row)
                transposed("XT", l, 1)
                wt = next_slot("mq", 0)
                for i in (0, 1):
                    b = fill(pe, ("mq", i), l)
                    for c in (0, 1):
                        ins = summed(b[:, c * T:(c + 1) * T], lambda k: wt[:, k, (2 * i + c) * P:(2 * i + c + 1) * P],
                                     lambda k: uT[:, k, T:S])
                    done(ins, ("mq", i))
                wt = next_slot("mk", 0)
                for h in range(NHM):
                    b = fill(pe, ("mk", h), l)
                    done(summed(b, lambda k: wt[:, k, h * P:(h + 1) * P], lambda k: uT[:, k, :]), ("mk", h))
                b = fill(pe, ("mg", 0), l)
                for st in range(ST):
                    ins = summed(b[:, 16 * st:16 * st + 16], lambda k: uT[:, k, st * P:(st + 1) * P],
                                 lambda k: gate_w[:, k, :])
                done(ins, ("mg", 0))

                def token_rows(key, s, tiles):
                    wt = next_slot(key, s)
                    for i, st in enumerate(tiles):
                        item = (key, len(tiles) * s + i)
                        b = fill(pe, item, l)
                        done(summed(b, lambda k: uT[:, k, st * P:(st + 1) * P], lambda k: wt[:, k, :]), item)

                token_rows("mv", 0, range(ST))
                pe.wait_ge(gate_ready, 1)
                b = fill(pe, ("F", 9), l)
                prefix = cst2("prefix")
                for st in range(ST):
                    terms = [(s_, ones) for s_ in range(st)] + [(st, prefix)]
                    for n, (s_, tri) in enumerate(terms):
                        mm(b[:, 8 * st:8 * st + 4], tri, log_f[:, 2 * s_, :], n == 0, n == len(terms) - 1)
                    whole = [0, 1] if st >= TT else []
                    later = [s_ for s_ in range(st + 1, TT if st < TT else ST)]
                    terms = [(s_, ones) for s_ in whole + later] + [(st, suffix)]
                    for n, (s_, tri) in enumerate(terms):
                        ins = mm(b[:, 8 * st + 4:8 * st + 8], tri, log_f[:, 2 * s_ + 1, :], n == 0,
                                 n == len(terms) - 1)
                done(ins, ("F", 9))
                after_evacuation(pe, ("F", 9), l)
                for d in (0, 1):
                    b = fill(pe, ("GT", d), l)
                    for st in range(ST):
                        ins = nc.tensor.transpose(b[0:NHM, st * P:(st + 1) * P], g_sub[:, st, 4 * d:4 * d + 4], ident)
                    done(ins, ("GT", d))
                token_rows("mv", 1, range(ST))
                token_rows("mo", 0, (2, 3))
                token_rows("mo", 1, (2, 3))
                pe.wait_ge(cummax_ready, 1)
                b = fill(pe, ("MR", 0), l)
                for t in range(TT):
                    for d in (0, 1):
                        i = 2 * t + d
                        at_ = P * (1 - d) + t * P
                        ins = nc.tensor.transpose(b[:, 4 * i:4 * i + 4], cummax[d][0][:, at_:at_ + P], ident[0:NHM, 0:NHM])
                done(ins, ("MR", 0))
                for i in (0, 1):
                    after_evacuation(pe, ("mq", i), l)

                def m_scores(h):
                    b = fill(pe, ("MB", h), l)
                    pick_h = ident[0:NHM, h:h + 1].broadcast_to([NHM, P])
                    for d in (0, 1):
                        ins = mm(b[:, d * T:(d + 1) * T], pick_h, cummax[d][0][:, P * (1 - d):P * (1 - d) + T])
                    done(ins, ("MB", h))
                    after_evacuation(pe, ("mk", h), l)
                    for q in (0, 1):
                        b = fill(pe, ("QK", 2 * h + q), l)
                        for c in (0, 1):
                            st = 2 * q + c
                            ins = mm(b[:, c * T:(c + 1) * T], m_kT[:, h, st * P:(st + 1) * P], m_qT[:, h, :])
                        done(ins, ("QK", 2 * h + q))

                def m_outputs(h):
                    after_evacuation(pe, ("QK", 2 * h + 1), l)
                    for d in (0, 1):
                        for t in range(TT):
                            tiles = [0, 1, 2, 3]
                            if (d, t) == (0, 0):
                                tiles = [0, 1, 2]
                            if (d, t) == (1, 1):
                                tiles = [0, 1, 3]
                            b = fill(pe, ("H", 4 * h + 2 * d + t), l)
                            for n, st in enumerate(tiles):
                                ins = mm(b[:, 0:DV + 1], decay[h % 2][:, d, st * T + t * P:st * T + (t + 1) * P],
                                         m_v[:, st, h, 0:DV + 1], n == 0, n == len(tiles) - 1)
                            done(ins, ("H", 4 * h + 2 * d + t))

                for i in range(8):
                    after_evacuation(pe, ("mv", i), l)
                for h in range(NHM + 1):
                    if h < NHM:
                        m_scores(h)
                    if h:
                        m_outputs(h - 1)
                pe.wait_ge(h_normed, 1)
                transposed("AT", l, 0, h_row)
                for g in (0, 1):
                    token_rows("dv", g, range(ST))
                    wq, wk = next_slot("dq", g), next_slot("dk", g)

                    def project_head(h):
                        hh = h % 4
                        b = fill(pe, ("dq", h), l)
                        done(summed(b[:, 0:T], lambda k: wq[:, k, hh * P:(hh + 1) * P], lambda k: uT[:, k, T:S]), ("dq", h))
                        b = fill(pe, ("dk", h), l)
                        done(summed(b, lambda k: wk[:, k, hh * P:(hh + 1) * P], lambda k: uT[:, k, :]), ("dk", h))

                    def partners(h):
                        after_evacuation(pe, ("dq", h), l)
                        after_evacuation(pe, ("dk", h), l)
                        b = fill(pe, ("rot", h), l)
                        done(mm(b, cst2("partner"), raw[:, h % 2, :]), ("rot", h))

                    project_head(4 * g)
                    partners(4 * g)
                    for h in range(4 * g, 4 * g + 4):
                        if h % 4 < 3:
                            project_head(h + 1)
                        pe.wait_ge(qk_ready, h + 1)
                        for i in range(4):
                            t, m = divmod(i, 2)
                            b = fill(pe, ("S", 4 * h + i), l)
                            done(mm(b, d_q[:, 2 * (h % 4) + m, t * P:(t + 1) * P], d_kT[:, h % 4, :]), ("S", 4 * h + i))
                        if h % 4 < 3:
                            partners(h + 1)
                        for t in range(TT):
                            pe.wait_ge(attn_ready, 2 * h + t + 1)
                            b = fill(pe, ("PT", 2 * h + t), l)
                            for st in range(ST):
                                ins = nc.tensor.transpose(b[:, st * P:(st + 1) * P], probs[:, t, 0, st * P:(st + 1) * P], ident)
                            done(ins, ("PT", 2 * h + t))
                        if h % 4 == 0:
                            for i in range(4):
                                after_evacuation(pe, ("dv", 4 * g + i), l)
                        b = fill(pe, ("O", h), l)
                        for t in range(TT):
                            after_evacuation(pe, ("PT", 2 * h + t), l)
                            for st in range(ST):
                                ins = mm(b[:, t * P:(t + 1) * P], aT[:, t, st * P:(st + 1) * P],
                                         d_v[:, st, (h % 4) * P:(h % 4 + 1) * P], st == 0, st == ST - 1)
                        done(ins, ("O", h))
                pe.wait_ge(b_normed, 1)
                transposed("BT", l, 0, b_row)
                for i in range(4):
                    after_evacuation(pe, ("AT", i), l)
                for g in (0, 1):
                    for key in ("pa", "pb", "wa", "wb"):
                        wt = next_slot(key, g)
                        src, t0 = {"wa": (a_outT, 0), "wb": (b_outT, 0)}.get(key, (uT, T))
                        for i in (0, 1):
                            b = fill(pe, (key, 2 * g + i), l)
                            for c in (0, 1):
                                    ins = summed(b[:, c * T:(c + 1) * T], lambda k: wt[:, k, (2 * i + c) * P:(2 * i + c + 1) * P],
                                             lambda k: src[:, k, t0:t0 + T])
                            done(ins, (key, 2 * g + i))
                        if g == 1 and key != "pa":
                            take(pe, (key, 3), l)
                            pe.sem_inc(expert_slot_free, 1)
                pe.wait_ge(y_ready, 4)
                for i in range(4):
                    fill(pe, ("Y", i), l)
                for s_ in (0, 1):
                    tokens_down("Y", l, n_slot[0] + s_, yT, 4 * s_, 4, KC, s_ == 1)
                take(pe, ("Y", 3), l)
                pe.sem_inc(expert_slot_free, 1)
                transposed("R", l, 2)
                pe.wait_ge(late_loaded, 64)
                b = fill(pe, ("L", 0), l)
                for t in range(TT):
                    ins = summed(b[:, t * N_EXP:(t + 1) * N_EXP], lambda k: u2T[:, k, t * P:(t + 1) * P],
                                 lambda k: router_w[:, k, :])
                done(ins, ("L", 0))
                pe.wait_ge(mask_ready, 1)
                b = fill(pe, ("PC", 0), l)
                before = cst2("before")
                mm(b[:, 0:N_EXP], before, chosen[:, 0, :])
                mm(b[:, N_EXP:2 * N_EXP], ones, chosen[:, 0, :], True, False)
                done(mm(b[:, N_EXP:2 * N_EXP], before, chosen[:, 1, :], False, True), ("PC", 0))
                take(pe, ("PC", 0), l)
                pe.sem_inc(expert_slot_free, 1)
                b = fill(pe, ("CN", 0), l)
                mm(b[:, 0:N_EXP], ones, chosen[:, 0, :], True, False)
                done(mm(b[:, 0:N_EXP], ones, chosen[:, 1, :], False, True), ("CN", 0))
                pe.wait_ge(gates_ready, 1)
                b = fill(pe, ("gT", 0), l)
                for t in range(TT):
                    ins = nc.tensor.transpose(b[0:N_EXP, t * P:(t + 1) * P], gate_row[:, t, :], ident)
                done(ins, ("gT", 0))
                after_evacuation(pe, ("gT", 0), l)

                def sum_up(i, lhsT, rhs, first=False):
                    return nc.tensor.matmul(psum[:, i, :], lhsT, rhs, start=first, stop=True, skip_group_check=True)

                for i in range(4):
                    t, n = divmod(i, 2)
                    fill(pe, ("YM", i), l)
                    sum_up(i, gT[0:N_EXP, t * P:(t + 1) * P], b2_rows[0:N_EXP, 512 * n:512 * n + 512], True)

                def part_mm(b, xx, lhs, rhs, first=False, last=False):
                    rows = slice(CAP * xx, CAP * (xx + 1))
                    return nc.tensor.matmul(b[rows, :], lhs[:, rows], rhs, start=first, stop=last, skip_group_check=True)

                def pair(it, j):
                    pe.wait_ge(picks_ready, it + 1)
                    for g in (0, 1):
                        b = fill(pe, ("G", g), it)
                        for c in range(4):
                            k = 4 * g + c
                            for t in range(TT):
                                ins = mm(b[:, c * P:(c + 1) * P], xhat[:, t, k * P:(k + 1) * P], pick[:, t, :], t == 0, t == 1)
                        done(ins, ("G", g))
                    banks = [("GLU", 0, 0), ("LIN", 0, D), ("GLU", 1, 512), ("LIN", 1, D + 512)]
                    for key, n, c0 in banks:
                        b = fill(pe, (key, n), it)
                        nc.tensor.matmul(b, pick_e, b1_rows[:, c0:c0 + 512], start=True, stop=False, skip_group_check=True)
                    after_evacuation(pe, ("G", 0), it)
                    for q in range(4):
                        if q == 2:
                            after_evacuation(pe, ("G", 1), it)
                        wt = [expert_slot(pe, it, 2 * q + xx).rearrange("p (k n) -> p k n", k=2) for xx in (0, 1)]
                        order = ([(k, i) for k in (0, 1) for i in range(4)] if q < 3 else
                                 [(k, i) for i in range(4) for k in (0, 1)])
                        for k, i in order:
                            key, n, c0 = banks[i]
                            end_of_bank = q == 3 and k == 1
                            for xx in (0, 1):
                                ins = part_mm(psum[:, bank_of((key, n)), :], xx, xgT[:, 2 * q + k, :],
                                              wt[xx][:, k, c0:c0 + 512], last=end_of_bank)
                                if xx and end_of_bank:
                                    done(ins, (key, n))
                                elif (k, i) == (1, 3):
                                    ins.then_inc(expert_slot_free, 1)
                    b = fill(pe, ("ST", 0), it)
                    nc.tensor.transpose(b[:, 0:P], pick_gated[:, 0, :], ident).then_inc(expert_slot_free, 1)
                    done(nc.tensor.transpose(b[:, P:T], pick_gated[:, 1, :], ident), ("ST", 0))

                    def hidden_transposed(n):
                        pe.wait_ge(hidden_ready, 2 * it + (n + 1))
                        b = fill(pe, ("AT2", n), it)
                        for c in range(4):
                            ins = nc.tensor.transpose(b[:, c * P:(c + 1) * P], act_[n][:, c * P:(c + 1) * P], ident)
                        done(ins, ("AT2", n))

                    hidden_transposed(0)
                    after_evacuation(pe, ("AT2", 0), it)
                    for n in (0, 1):
                        fill(pe, ("OUT", n), it)
                    for q in (0, 1):
                        wt = [expert_slot(pe, it, 8 + 2 * q + xx).rearrange("p (k n) -> p k n", k=4) for xx in (0, 1)]
                        if q:
                            after_evacuation(pe, ("AT2", 1), it)
                        order = [(k, n) for k in range(4) for n in (0, 1)] if q == 0 else [(k, n) for n in (0, 1) for k in range(4)]
                        for k, n in order:
                            if (q, k, n) == (0, 2, 0):
                                hidden_transposed(1)
                            for xx in (0, 1):
                                ins = part_mm(psum[:, bank_of(("OUT", n)), :], xx, actT[:, 4 * q + k, :],
                                              wt[xx][:, k, 512 * n:512 * n + 512], q + k == 0, q + k == 4)
                                if xx and q and k == 3:
                                    done(ins, ("OUT", n))
                                elif (k, n) == (3, 1):
                                    ins.then_inc(expert_slot_free, 1)
                    after_evacuation(pe, ("ST", 0), it)
                    for n in (0, 1):
                        after_evacuation(pe, ("OUT", n), it)
                        for t in range(TT):
                            ins = sum_up(2 * t + n, spread_T[:, t * P:(t + 1) * P], out_sb[:, 512 * n:512 * n + 512])
                            if (n, t) == (0, 0):
                                ins.then_inc(expert_slot_free, 1)
                    ins.then_inc(combined, 1)

                over_pairs(pe, pair)

            def layer(l):
                def project(s):
                    wt = slot_ready(pe, s, l).rearrange("p (k n) -> p k n", k=KC)
                    for i in (2 * s, 2 * s + 1):
                        b = fill(pe, ("s", i), l)
                        at = (i % 2) * 256
                        for c in (0, 1):
                            for k in range(KC):
                                if i in ROW_SLICES:
                                    lhsT, rhs = hT[:, k, c * P:(c + 1) * P], wt[:, k, at:at + 256]
                                else:
                                    lhsT, rhs = wt[:, k, at + c * P:at + (c + 1) * P], hT[:, k, :]
                                ins = mm(b[:, c * T:(c + 1) * T], lhsT, rhs, k == 0, k == KC - 1)
                        done(ins, ("s", i))

                transposed("T", l, 1)
                for s in range(3):
                    project(s)
                after_evacuation(pe, ("s", 2), l)
                after_evacuation(pe, ("s", 3), l)
                for h in range(NH):
                    diagonal_scores("Z", l, kT, q_z, h)
                project(3)
                pe.wait_ge(rq_ready, l + 1)
                transposed_pair(("RQ", 0), l, rq)
                pe.wait_ge(rk_ready, l + 1)
                transposed_pair(("RK", 0), l, rk)
                project(4)
                after_evacuation(pe, ("RQ", 0), l)
                after_evacuation(pe, ("RK", 0), l)
                for h in range(NH):
                    diagonal_scores("RS", l, rkT, rq_z, h)
                project(5)
                pe.wait_ge(sb_soft, l + 1)
                for h in range(NH):
                    b = fill(pe, ("I", h), l)
                    mm(b[:, 0:T], suffix, soft[:, h, 0:T], True, False)
                    mm(b[:, P:T], ones, soft[:, h, T:DIAG], False, True)
                    done(mm(b[:, T:DIAG], suffix, soft[:, h, T:DIAG]), ("I", h))
                after_evacuation(pe, ("s", 7), l)
                b = fill(pe, ("RO", 0), l).rearrange("p (t h e) -> p t h e", t=TT, h=NH)
                for h in range(NH):
                    after_evacuation(pe, ("RS", h), l)
                    cut = slice(h * HD, (h + 1) * HD)
                    mm(b[:, 0, h, :], r_scores[:, h, 0:P], rv[:, 0, cut])
                    mm(b[:, 1, h, :], r_scores[:, h, P:T], rv[:, 0, cut], True, False)
                    ins = mm(b[:, 1, h, :], r_scores[:, h, T:DIAG], rv[:, 1, cut], False, True)
                done(ins, ("RO", 0))
                pe.wait_ge(sb_attn, l + 1)
                after_evacuation(pe, ("s", 4), l)
                for c in (0, 1):
                    b = fill(pe, ("SB", c), l)
                    for h in (2 * c, 2 * c + 1):
                        rows = slice((h % 2) * HD, (h % 2 + 1) * HD)
                        cut = slice(h * HD, (h + 1) * HD)
                        mm(b[rows, 0:T], v_sb[:, 0, cut], z[:, h, 0:T], True, False)
                        ins = mm(b[rows, P:T], v_sb[:, 1, cut], z[:, h, T:DIAG], False, True)
                    done(ins, ("SB", c))
                pe.wait_ge(conf_ready, l + 1)
                b = fill(pe, ("CM", 0), l)
                mm(b[:, 0:T], ones, conf[:, 0, :], True, False)
                done(mm(b[:, 0:T], ones, conf[:, 1, :], False, True), ("CM", 0))
                pe.wait_ge(conf_sq_ready, l + 1)
                b = fill(pe, ("CV", 0), l)
                mm(b[:, 0:T], ones, conf_sq[:, 0, :], True, False)
                done(mm(b[:, 0:T], ones, conf_sq[:, 1, :], False, True), ("CV", 0))
                pe.wait_ge(ret_ready, l + 1)
                transposed_pair(("RT", 0), l, ret)
                pe.wait_ge(sc_cat, l + 1)
                pe.wait_ge(conf_cat, l + 1)
                after_evacuation(pe, ("SB", 1), l)
                after_evacuation(pe, ("RT", 0), l)
                for i in range(4):
                    fill(pe, ("M", i), l)
                tokens_down("M", l, 6, catT, 0, 4, KC, False)
                tokens_down("M", l, 7, catT, 4, 4, KC, True)
                transposed("F", l, 2)
                for n in range(8, len(LAYER_SLOTS)):
                    kind, g = LAYER_SLOTS[n]
                    if kind == "up":
                        wt = slot_ready(pe, n, l).rearrange("p (u k n) -> p u k n", u=2, k=KC)
                        for u in (0, 1):
                            b = fill(pe, ("U", 2 * g + u), l)
                            for c in (0, 1):
                                for k in range(KC):
                                    ins = mm(b[:, c * T:(c + 1) * T], wt[:, u, k, c * P:(c + 1) * P], hT[:, k, :],
                                             k == 0, k == KC - 1)
                            done(ins, ("U", 2 * g + u))
                    else:
                        if g == 0:
                            for i in range(4):
                                fill(pe, ("D", i), l)
                        pe.wait_ge(ff_ready, l * 11 + min(2 * g + 2, 11))
                        tokens_down("D", l, n, ffT, 4 * g, min(4, FFC - 4 * g), FFC, g == 5)

            for b in range(8):
                pe.sem_inc(evacuated[b], 1)
            pe.wait_ge(const_loaded, 16)
            pe.wait_ge(zeros_ready, 4)
            loop_layers(pe, layer)
            second()


def pack_cols(inputs):
    def chunks(a):
        a = np.asarray(a)
        a = a.reshape(DEPTH, -1, a.shape[-1] // P, P)
        return a.transpose(0, 3, 1, 2).reshape(DEPTH, P, -1)

    names = ("norm_mix_pre", "conf_dw_w", "conf_dw_b", "conf_ln_g", "conf_ln_b", "sc_conv_w", "norm_ffn_pre",
             "ffn_conv_w")
    return np.ascontiguousarray(np.concatenate([chunks(inputs[n]) for n in names], axis=2))


def pack_cols2(inputs):
    ada = np.asarray(inputs["ada_b_2"])[0].reshape(6, D)[[0, 1, 3, 4]].reshape(-1)
    flat = np.concatenate([np.asarray(inputs["norm1_g_2"])[0], np.asarray(inputs["norm2_g_2"])[0], ada])
    return np.ascontiguousarray(flat.reshape(-1, P).T)


def pack_c(inputs):
    both = np.stack([np.asarray(inputs["c_2"])[0], np.asarray(inputs["c_ctx_2"])])
    return np.ascontiguousarray(both.reshape(2, KC, P).transpose(2, 1, 0).reshape(P, 2 * KC))


PACKED = ("norm_mix_pre", "norm_ffn_pre", "conf_dw_w", "conf_dw_b", "conf_ln_g", "conf_ln_b", "sc_conv_w", "ffn_conv_w",
          "c_2", "c_ctx_2", "norm1_g_2", "norm2_g_2")


def kernel(**inputs):
    import concourse.bacc as bacc
    from concourse.bass_utils import run_bass_kernel_spmd

    nc = bacc.Bacc("TRN2", target_bir_lowering=False, num_devices=1)
    arrays = {n: np.ascontiguousarray(a) for n, a in inputs.items() if n not in PACKED}
    arrays.update(const=shape_constants(), cols=pack_cols(inputs), const2=shape_constants2(), cols2=pack_cols2(inputs),
                  cT=pack_c(inputs))
    w = {n: nc.dram_tensor(f"{n}_dram", a.shape, mybir.dt.from_np(a.dtype), kind="ExternalInput").ap()
         for n, a in arrays.items()}
    out = nc.dram_tensor("out_dram", (T, D), F32, kind="ExternalOutput").ap()
    build_program(nc, w, out)
    result = run_bass_kernel_spmd(nc, [{f"{n}_dram": a for n, a in arrays.items()}], core_ids=[0])
    return np.asarray(result.results[0]["out_dram"]).reshape(inputs["x"].shape)
```

```python
from contextlib import ExitStack

import numpy as np

import concourse.bass as bass
from concourse import mybir

F32 = mybir.dt.float32
F32R = mybir.dt.float32r
ALU = mybir.AluOpType
ACT = mybir.ActivationFunctionType
AX = mybir.AxisListType.X

P = 128
T = 256
TT = T // P
D = 1024
KC = D // P
DEPTH = 2
GW = 256
HD = 64
NH = GW // HD
CONF_K = 31
SC_K = 3
FFN_K = 3
D_FF = 2816
FFC = D_FF // P
EPS = 1e-6
SCALE = HD ** -0.5

WORK = 21600
XHAT_AT = 2526
CAT_AT = XHAT_AT + 2 * 2048
HALF = 2048
ACT_STEPS = 5
DVE_STEPS = 123
ROW_SLICES = (4, 5, 6, 7, 8)
RING = 5
RING2 = 10
UNIT = 1024
DIAG = 384

COL_MIX_PRE = 0
COL_CONF_W = COL_MIX_PRE + KC
COL_CONF_B = COL_CONF_W + 2 * CONF_K
COL_CONF_LG = COL_CONF_B + 2
COL_CONF_LB = COL_CONF_LG + 2
COL_SC_W = COL_CONF_LB + 2
COL_FFN_PRE = COL_SC_W + 2 * SC_K
COL_FFN_W = COL_FFN_PRE + KC
N_COLS = COL_FFN_W + 2 * FFC * FFN_K
N_MIXROW = D + GW

CONSTS = {}
_at = 0
for _name, _n in (("ident", P), ("ones", P), ("suffix", P), ("sb_mask", DIAG), ("sb_neg", DIAG),
                  ("ret_decay", NH * DIAG), ("ret_cos", TT * GW), ("ret_sin", TT * GW)):
    CONSTS[_name] = (_at, _n)
    _at += _n
N_CONST = _at
SPARE = 3 * P


def shape_constants():
    c = np.zeros((P, N_CONST), np.float32)

    def put(name, a):
        at, n = CONSTS[name]
        c[:, at:at + n] = np.asarray(a, np.float32).reshape(P, n)

    i = np.arange(P)
    put("ident", np.eye(P))
    put("ones", np.ones((P, P)))
    put("suffix", i[:, None] >= i[None, :])
    strict = (i[:, None] < i[None, :]).astype(np.float32)
    mask = np.concatenate([strict, np.ones((P, P)), strict], axis=1)
    put("sb_mask", mask)
    put("sb_neg", np.where(mask > 0, 0.0, -1e30))
    log_gamma = np.log1p(-np.exp2(-5.0 - np.arange(NH)))
    diff = i[None, :] - i[:, None]
    decay = []
    for h in range(NH):
        diag = np.where(diff >= 0, np.exp(np.maximum(diff, 0) * log_gamma[h]), 0.0)
        full = np.exp((diff + P) * log_gamma[h])
        decay.append(np.concatenate([diag, full, diag], axis=1) * SCALE)
    put("ret_decay", np.stack(decay, axis=1))
    inv = (np.float32(10000.0) ** (-np.arange(0, HD, 2, dtype=np.float32) / np.float32(HD))).astype(np.float32)
    pos = (i[:, None] + P * np.arange(TT)[None, :]).astype(np.float32)
    ang = (pos[:, :, None] * inv[None, None, :]).astype(np.float32)
    cos, sin = np.cos(ang), np.sin(ang)
    put("ret_cos", np.tile(np.concatenate([cos, cos], -1)[:, :, None, :], (1, 1, NH, 1)))
    put("ret_sin", np.tile(np.concatenate([-sin, sin], -1)[:, :, None, :], (1, 1, NH, 1)))
    return c


LAYER_SLOTS = [("in", s) for s in range(6)] + [("out", s) for s in range(2)]
for _m in range(5):
    LAYER_SLOTS += [("up", g) for g in ((0, 1, 2) if _m == 0 else (2 * _m + 1, 2 * _m + 2))] + [("down", _m)]
LAYER_SLOTS += [("down", 5)]
assert 2 * len(LAYER_SLOTS) % RING == 0
LAYER_ROUNDS = 2 * len(LAYER_SLOTS) // RING

FFN_SLOTS = LAYER_SLOTS[8:]
UNITS = [(n, j) for n, (_kind, _g) in enumerate(FFN_SLOTS) for j in range(2 if (_kind, _g) == ("down", 5) else 4)]
UNIT_BUFFERS = 3
assert len(UNITS) % UNIT_BUFFERS == 0


def ends_item(n):
    slot, j = UNITS[n]
    return (FFN_SLOTS[slot][0] == "up" and j % 2 == 1) or n == len(UNITS) - 1


PASSES = [(0, 0), (0, 1), (1, 0)]
UNITS_INSIDE = sum(not ends_item(n) for n in range(len(UNITS)))

LAYER_BANKS = [("T", i, i) for i in range(4)]
LAYER_BANKS += [("s", i, (4 + i) % 8) for i in range(6)]
LAYER_BANKS += [("Z", h, 2 + h) for h in range(4)]
LAYER_BANKS += [("s", 6, 6), ("s", 7, 7), ("RQ", 0, 0), ("RK", 0, 1), ("s", 8, 2), ("s", 9, 3)]
LAYER_BANKS += [("RS", h, 4 + h) for h in range(4)]
LAYER_BANKS += [("s", 10, 0), ("s", 11, 1)]
LAYER_BANKS += [("I", h, 2 + h) for h in range(4)]
LAYER_BANKS += [("RO", 0, 6), ("CM", 0, 7), ("SB", 0, 0), ("SB", 1, 1), ("CV", 0, 2), ("RT", 0, 3)]
LAYER_BANKS += [("M", i, 4 + i) for i in range(4)]
LAYER_BANKS += [("F", i, i) for i in range(4)]
LAYER_BANKS += [("U", g, (2 * (g // 2)) % 4 + g % 2) for g in range(6)]
LAYER_BANKS += [("D", i, 4 + i) for i in range(4)]
LAYER_BANKS += [("U", g, (2 * (g // 2)) % 4 + g % 2) for g in range(6, 22)]


NHM, DQK, DV = 4, 128, 256
ST = 2 * TT
S = ST * P
NHD, DHD = 8, 64
N_EXP, TOP_K = 32, 4
CAP = 64
PAIRS = N_EXP // 2
W_IN2_COLS = dict(mq=0, mk=512, mv=1024, gates=2048, mo=2064, dq=3088, dk=4112, dv=5136, pa=6160, pb=7184)
LAM_INIT = 0.2
LIMIT, ALPHA = 7.0, 1.702

CONSTS2 = {}
_at = 0
for _name, _n in (("rope_cos", T), ("rope_sin", T), ("partner", P), ("prefix", P), ("before", P), ("iota", CAP),
                  ("pick", 2), ("spread", P)):
    CONSTS2[_name] = (_at, _n)
    _at += _n
N_CONST2 = _at


def shape_constants2():
    c = np.zeros((P, N_CONST2), np.float32)

    def put(name, a):
        at, n = CONSTS2[name]
        c[:, at:at + n] = np.asarray(a, np.float32).reshape(P, n)

    i = np.arange(P)
    d = i % DHD
    nf = DHD // 4
    inv = (np.float32(10000.0) ** (-np.arange(nf, dtype=np.float32) / np.float32(nf))).astype(np.float32)
    tok = np.arange(T)
    pos = np.where((d < DHD // 2)[:, None], (tok // 64)[None, :], (tok % 64)[None, :]).astype(np.float32)
    ang = (pos * inv[d % nf][:, None]).astype(np.float32)
    first = (d % (2 * nf)) < nf
    put("rope_cos", np.cos(ang))
    put("rope_sin", np.where(first[:, None], -np.sin(ang), np.sin(ang)))
    partner = np.where(first, i + nf, i - nf)
    put("partner", partner[:, None] == i[None, :])
    put("prefix", i[:, None] <= i[None, :])
    put("before", i[:, None] < i[None, :])
    put("iota", np.tile(np.arange(CAP), (P, 1)))
    put("pick", (i % 32)[:, None] == np.arange(2)[None, :])
    put("spread", np.tile((i % 32 == 0)[:, None], (1, P)))
    return c


B2_SLOTS = [("ada", n) for n in range(12)]
B2_SLOTS += [("mq", 0), ("mk", 0), ("mv", 0), ("mv", 1), ("mo", 0), ("mo", 1)]
B2_SLOTS += [(k, g) for g in (0, 1) for k in ("dv", "dq", "dk")]
B2_SLOTS += [(k, g) for g in (0, 1) for k in ("pa", "pb", "wa", "wb")]
B2_SLOTS += [("wo", 0), ("wo", 1)]

B2_BANKS = []
for _n in range(12):
    B2_BANKS.append(("ada", _n, _n % 2))
    if _n >= 1:
        _m = _n - 1
        B2_BANKS += [("mT", 0, 2)] if _m == 3 else [("mT", 1, 3)] if _m == 9 else []
        B2_BANKS += [("mR", _m, 4 + _m % 2)] if _m in (4, 5, 10) else []
B2_BANKS += [("mR", 11, 5)]
B2_BANKS += [("CT", i, i) for i in range(4)] + [("XT", i, 4 + i) for i in range(4)]
B2_BANKS += [("mq", 0, 0), ("mq", 1, 1)] + [("mk", h, 2 + h) for h in range(4)] + [("mg", 0, 6), ("F", 9, 7)]
B2_BANKS += [("mv", i, i) for i in range(4)]
B2_BANKS += [("GT", 0, 4), ("GT", 1, 5)]
B2_BANKS += [("mv", 4, 6), ("mv", 5, 7), ("mv", 6, 0), ("mv", 7, 1)]
B2_BANKS += [("mo", 0, 2), ("mo", 1, 3), ("mo", 2, 4), ("mo", 3, 5), ("MR", 0, 6)]


def _heads_banks():
    out = []
    for h in range(NHM + 1):
        if h < NHM:
            out += [("MB", h, 7), ("QK", 2 * h, 0), ("QK", 2 * h + 1, 1)]
        if h >= 1:
            out += [("H", 4 * (h - 1) + i, 2 + i) for i in range(4)]
    return out


B2_BANKS += _heads_banks()
B2_BANKS += [("AT", i, 6 + i % 2) for i in range(4)]
for _g in (0, 1):
    B2_BANKS += [("dv", 4 * _g + i, i) for i in range(4)]
    B2_BANKS += [("dq", 4 * _g, 4), ("dk", 4 * _g, 5), ("rot", 4 * _g, 6)]
    for _hh in range(4):
        _h = 4 * _g + _hh
        if _hh < 3:
            B2_BANKS += [("dq", _h + 1, 4), ("dk", _h + 1, 5)]
        B2_BANKS += [("S", 4 * _h + i, i) for i in range(4)]
        if _hh < 3:
            B2_BANKS += [("rot", _h + 1, 6)]
        B2_BANKS += [("PT", 2 * _h, 7), ("PT", 2 * _h + 1, 4), ("O", _h, 5)]
B2_BANKS += [("BT", i, i) for i in range(4)]
for _g in (0, 1):
    B2_BANKS += [("pa", 2 * _g, 4), ("pa", 2 * _g + 1, 5), ("pb", 2 * _g, 6), ("pb", 2 * _g + 1, 7)]
    B2_BANKS += [("wa", 2 * _g, 0), ("wa", 2 * _g + 1, 1), ("wb", 2 * _g, 2), ("wb", 2 * _g + 1, 3)]
B2_BANKS += [("Y", i, 4 + i) for i in range(4)]
B2_BANKS += [("R", i, i) for i in range(4)]
B2_BANKS += [("L", 0, 4), ("PC", 0, 5), ("CN", 0, 6), ("gT", 0, 7)]
B2_BANKS += [("YM", i, i) for i in range(4)]
MOE_BANKS = [("G", 0, 4), ("G", 1, 5), ("GLU", 0, 6), ("LIN", 0, 7), ("GLU", 1, 4), ("LIN", 1, 5),
             ("ST", 0, 6), ("AT2", 0, 7), ("OUT", 0, 4), ("OUT", 1, 5), ("AT2", 1, 6)]
PAIR_SLOTS = [("w1", x, q) for q in range(4) for x in (0, 1)] + [("w2", x, q) for q in range(2) for x in (0, 1)]
PAIR_RING = (8, 9, 0, 1, 2, 3, 4, 5, 6, 7, 10, 11)


def bank_rounds(items):
    used, where = [0] * 8, {}
    for kind, i, b in items:
        where[kind, i] = (b, used[b])
        used[b] += 1
    return where, used


LAYER_WHERE, LAYER_FILLS = bank_rounds(LAYER_BANKS)
B2_WHERE, B2_FILLS = bank_rounds(B2_BANKS)
MOE_WHERE, MOE_FILLS = bank_rounds(MOE_BANKS)


def earlier_fills(key, l):
    if key in MOE_WHERE:
        b, n = MOE_WHERE[key]
        return b, l * MOE_FILLS[b] + (DEPTH * LAYER_FILLS[b] + B2_FILLS[b] + n)
    if key in B2_WHERE:
        b, n = B2_WHERE[key]
        return b, DEPTH * LAYER_FILLS[b] + n
    b, n = LAYER_WHERE[key]
    return b, l * LAYER_FILLS[b] + n


def build_program(nc, w, out):
    with ExitStack() as ctx:
        def sb(name, n, p=P):
            return ctx.enter_context(nc.sbuf_tensor(name, [p, n], F32))

        def sem(name):
            return ctx.enter_context(nc.semaphore(name))

        psum = ctx.enter_context(nc.psum_tensor("psum", [P, 8, 512], F32))
        with (nc.sbuf_tensor("split_weights", [P, UNIT_BUFFERS * 2 * UNIT], F32R) as split_w,
              nc.sbuf_tensor("split_rows", [P, 2 * (KC + 8) * T], F32R) as split_x):
            pass
        late = sb("late", UNIT_BUFFERS * 2 * UNIT + 2 * (KC + 8) * T)
        ring = sb("ring", RING * HALF)
        const = sb("const", N_CONST)
        x_row = sb("x_row", TT * D)
        stats = sb("stats", 64)
        work = sb("work", WORK)
        offset = [0]

        def part(n, *shape):
            at = offset[0]
            offset[0] += n
            assert offset[0] <= WORK, offset
            v = work[:, at:at + n]
            if shape:
                names = "abcd"[:len(shape)]
                v = v.rearrange(f"p ({' '.join(names)}) -> p {' '.join(names)}", **dict(zip(names, shape)))
            return v

        def cst(name):
            at, n = CONSTS[name]
            return const[:, at:at + n]

        ident, ones, suffix = cst("ident"), cst("ones"), cst("suffix")
        sb_mask4 = cst("sb_mask").unsqueeze(1).broadcast_to([P, NH, DIAG])
        sb_neg4 = cst("sb_neg").unsqueeze(1).broadcast_to([P, NH, DIAG])
        ret_decay = cst("ret_decay").rearrange("p (h n) -> p h n", h=NH)
        x = x_row[:, :].rearrange("p (t d) -> p t d", t=TT)
        sumsq, rms, rinv = stats[:, 0:2], stats[:, 2:4], stats[:, 4:6]
        ret_mu, ret_var, ret_std, ret_rinv = (stats[:, 8 + 8 * i:16 + 8 * i] for i in range(4))

        cols = part(N_COLS + N_COLS % 2)
        mix_row = part(N_MIXROW)
        ffn_row = part(D)
        assert offset[0] == XHAT_AT
        xhat = part(TT * D, TT, D)
        hT = part(KC * T, KC, T)
        assert offset[0] == CAT_AT
        catT = part(KC * T, KC, T)
        q_z = part(NH * T, NH, T)
        rq_z = part(NH * T, NH, T)
        conf_pad = part(2 * (T + 30), 2, T + 30)
        sc_pad = part(2 * (T + 2), 2, T + 2)
        branch_at = offset[0]
        kT = part(2 * T, 2, T)
        v_sb = part(TT * GW, TT, GW)
        z = part(NH * DIAG, NH, DIAG)
        soft = part(NH * DIAG, NH, DIAG)
        rq = part(TT * GW, TT, GW)
        rk = part(TT * GW, TT, GW)
        swapped = part(TT * GW)
        rkT = part(2 * T, 2, T)
        rv = part(TT * GW, TT, GW)
        rg = part(TT * GW, TT, GW)
        conf_gate = part(2 * T, 2, T)
        conf = part(2 * T, 2, T)
        conf_sq = part(2 * T, 2, T)
        sc_b = part(2 * T, 2, T)
        sc_c = part(2 * T, 2, T)
        r_scores = xhat.rearrange("p t d -> p (t d)")[:, 0:NH * DIAG].rearrange("p (h n) -> p h n", h=NH)
        ret = conf_sq
        offset[0] = branch_at
        taps = part(2 * 4 * T, 2, 4, T)
        hT_split = split_x[:, 0:2 * KC * T].rearrange("p (s k t) -> p s k t", s=2, k=KC)
        ffT_split = split_x[:, 2 * KC * T:].rearrange("p (s k t) -> p s k t", s=2, k=8)

        extra_at = [5 * HALF]

        def extra(n, *shape):
            at = extra_at[0]
            extra_at[0] += n
            assert extra_at[0] <= 7 * HALF
            return shaped(late[:, at:at + n], shape)

        def shaped(v, shape):
            if not shape:
                return v
            names = "abcd"[:len(shape)]
            return v.rearrange(f"p ({' '.join(names)}) -> p {' '.join(names)}", **dict(zip(names, shape)))

        def at(start, n, *shape):
            assert start + n <= WORK
            return shaped(work[:, start:start + n], shape)

        ctx_row = extra(TT * D, TT, D)
        const2 = extra(N_CONST2)
        cols2 = extra(2 * KC + 4 * KC)
        gate_w = extra(KC * 16, KC, 16)
        gate_b = extra(16)
        lam_row = extra(4 * DHD, 4, DHD)
        router_b = extra(N_EXP)

        def cst2(name):
            a, n = CONSTS2[name]
            return const2[:, a:a + n]

        flatten = lambda v: v.rearrange("p a b -> p (a b)")
        low, mid = 0, XHAT_AT + TT * D
        ada_rows = at(CAT_AT, 1024, 2, 512)
        uT = at(CAT_AT + 1024, KC * S, KC, S)
        high = CAT_AT + 1024 + KC * S
        g_rows = at(WORK - 2048, 2048, 2, D)
        top = WORK - 2048
        m_v = at(high, ST * NHM * 258, ST, NHM, 258)
        m_kT = at(high + 4128, NHM * S, NHM, S)
        m_qT = at(high + 6176, NHM * T, NHM, T)
        cummax = [[const[0:NHM, SPARE + 384 * (2 * d + i):SPARE + 384 * (2 * d + i + 1)] for i in (0, 1)] for d in (0, 1)]
        assert high + 7200 <= top and high + 7680 <= top and branch_at + FFC * T + 2048 <= top
        o_row = at(mid, TT * D, TT, D)
        decay = [at(low, 2 * ST * T, 2, ST * T), at(XHAT_AT, 2 * ST * T, 2, ST * T)]
        h_row = ctx_row
        norm_row = at(CAT_AT, D)
        a_outT = at(mid, KC * T, KC, T)
        d_kT = at(high, 4 * S, 4, S)
        d_v = at(high + 2048, ST * 512, ST, 512)
        d_q = at(high + 4096, 8 * T, 8, T)
        raw = at(high + 6144, 1024, 2, 512)
        turned = at(high + 7168, 512)
        aT = shaped(const[:, SPARE + 1536:SPARE + 2560], (2, 512))
        probs = at(low, 2048, 2, 2, S)
        b_row = xhat
        squares = at(low, 2 * D)
        b_outT = at(high, KC * T, KC, T)
        gate_a, gate_bb = at(low, 1024), at(low + 1024, 1024)
        yT = at(high + 2048, KC * T, KC, T)
        b1_rows = at(high + 4096, 2 * D)
        b2_rows = at(high + 6144, D)
        router_w = at(high + 7168, KC * N_EXP, KC, N_EXP)
        final_row = const[:, SPARE + 1536:SPARE + 2560]
        u2T = at(CAT_AT + 1024, KC * T, KC, T)
        xgT = at(mid, KC * P, KC, P)
        pick = at(mid + 1024, TT * P, TT, P)
        pick_gated = at(mid + 1280, TT * P, TT, P)
        spread_T = at(mid + 1536, T)
        assert mid + 1792 <= CAT_AT + 1024
        glu, sig, lin, act_ = ([at(CAT_AT + 1024 + 512 * (4 * e + i), 512) for e in (0, 1)] for i in range(4))
        actT = at(low, KC * P, KC, P)
        pick_e = at(low + 1024, P)
        gT = at(low + 1152, T)
        out_sb = at(high, D)
        router_at = [SPARE]

        def routed(n, *shape):
            a = router_at[0]
            router_at[0] += n
            assert router_at[0] <= SPARE + 1536
            return shaped(const[:, a:a + n], shape)

        n_wide = N_EXP + 4
        logits, others, exps = (routed(TT * n_wide, TT, n_wide) for _ in range(3))
        top8 = routed(TT * 8, TT, 8)
        neg_top, gate_sum, gate_inv = routed(TT), routed(TT), routed(TT)
        chosen, gate_row = routed(TT * N_EXP, TT, N_EXP), routed(TT * N_EXP, TT, N_EXP)
        pair_gate, pair_slot = routed(TT * N_EXP), routed(TT * N_EXP)
        most, n_pass = routed(1), routed(1)
        passes = ctx.enter_context(nc.sbuf_tensor("passes", [P, 1], mybir.dt.int32))

        small = sb("small", 960)
        small_at = [0]

        def tiny(n, *shape):
            a = small_at[0]
            small_at[0] += n
            assert small_at[0] <= 960
            return shaped(small[:, a:a + n], shape)

        modT = tiny(64, 32, 2)
        scale1, shift1 = tiny(16, 2, KC), tiny(16, 2, KC)
        scale2 = tiny(KC)
        gates = tiny(64, ST, 16)
        f_neg, f_abs, f_min, log_f = (tiny(32, ST * 2, 4) for _ in range(4))
        g_sub = tiny(32, ST, 8)
        ctx_max = tiny(2)
        m_neg = tiny(16)
        den, den2 = tiny(16), tiny(16)
        h_sq, h_rms, h_inv = tiny(8), tiny(8), tiny(8)
        lam_prod = tiny(128, 2, DHD)
        lam_sum, lam_exp, neg_lam = tiny(2), tiny(2), tiny(1)
        row_max, neg_max, row_sum, row_inv, map_scale = (tiny(4, 2, 2) for _ in range(5))
        b_sq, b_rms, b_inv = tiny(16), tiny(16), tiny(16)
        iota = tiny(CAP)
        cT = tiny(2 * KC, KC, 2)
        siluc = tiny(KC * 32, KC, 32)

        filled = [sem(f"bank{b}_filled") for b in range(8)]
        evacuated = [sem(f"bank{b}_evacuated") for b in range(8)]
        half_loaded = [sem(f"half_slot{s}_loaded") for s in range(12)]
        hT_high_ready, w_high_ready, w_split, unit_used, product_ready, ff_high_ready, c_loaded = (
            sem(n) for n in ("hT_high_ready", "weights_high_ready", "weights_split", "unit_used", "ff_product_ready",
                             "ff_high_ready", "c_loaded"))
        slot_free = sem("slot_free")
        const_loaded, x_loaded, mix_par_loaded, ffn_par_loaded = (
            sem(n) for n in ("const_loaded", "x_loaded", "mix_par_loaded", "ffn_par_loaded"))
        zeros_ready, tables_loaded = sem("zeros_ready"), sem("tables_loaded")
        x_ready = sem("x_ready")
        act_step, dve_step = sem("act_step"), sem("dve_step")
        rms_ready, xhat_ready = sem("rms_ready"), sem("xhat_ready")
        sb_abs, sb_log, sb_soft, sb_arg, sb_attn = (
            sem(n) for n in ("sb_abs_ready", "sb_log_ready", "sb_soft_ready", "sb_arg_ready", "sb_attn_ready"))
        rq_ready, rk_ready, ret_var_ready, ret_std_ready, ret_ready = (
            sem(n) for n in ("rq_ready", "rk_ready", "ret_var_ready", "ret_std_ready", "ret_ready"))
        conf_ready, conf_sq_ready, conf_normed, conf_cat = (
            sem(n) for n in ("conf_conv_ready", "conf_sq_ready", "conf_normed", "conf_cat_ready"))
        sc_cat = sem("sc_cat_ready")
        tap_ready, silu_ready, ff_ready = (sem(n) for n in ("first_tap_ready", "silu_ready", "ff_ready"))
        out_stored = sem("out_stored")
        names = ("early_loaded ctx_loaded g_bias_loaded norm_row_loaded late_loaded siluc_ready scale1_ready ctx_hat_ready "
                 "gate_abs_ready gate_log_ready gate_ready cummax_ready m_neg_ready decay_exp_ready "
                 "h_ready h_normed lam_sum_ready lam_exp_ready qk_ready row_max_ready probs_ready "
                 "attn_ready b_normed y_ready").split()
        (early_loaded, ctx_loaded, g_bias_loaded, norm_row_loaded, late_loaded, siluc_ready, scale1_ready, ctx_hat_ready,
         gate_abs_ready, gate_log_ready, gate_ready, cummax_ready, m_neg_ready, decay_exp_ready,
         h_ready, h_normed, lam_sum_ready, lam_exp_ready, qk_ready, row_max_ready, probs_ready,
         attn_ready, b_normed, y_ready) = (sem(n) for n in names)
        pairs_step, mask_ready, exp_ready, gates_ready, passes_ready = (
            sem(n) for n in ("pairs_step", "chosen_ready", "exp_ready", "expert_gates_ready", "passes_ready"))
        b1_zeroed, picks_ready, sig_ready, hidden_ready, combined, out_ready = (
            sem(n) for n in ("b1_rows_zeroed", "picks_ready", "glu_sigmoid_ready", "hidden_ready", "pair_combined",
                             "out_ready"))
        expert_slot_free, expert_load_claimed = sem("expert_slot_free"), sem("expert_load_claimed")
        L2 = DEPTH
        half_rounds = [(DEPTH * LAYER_ROUNDS if s < RING else 0) + len(range(s, 2 * len(B2_SLOTS), RING2))
                       for s in range(RING2)] + [0, 0]

        def bank_of(key):
            return earlier_fills(key, 0)[0]

        def fill(pe, key, l):
            b, n = earlier_fills(key, l)
            pe.wait_ge(evacuated[b], n + 1)
            return psum[:, b, :]

        def take(eng, key, l):
            b, n = earlier_fills(key, l)
            eng.wait_ge(filled[b], n + 1)
            return psum[:, b, :]

        def after_evacuation(eng, key, l):
            b, n = earlier_fills(key, l)
            eng.wait_ge(evacuated[b], n + 2)

        def half_place(s):
            return ring[:, s * HALF:(s + 1) * HALF] if s < RING else late[:, (s - RING) * HALF:(s - RING + 1) * HALF]

        def half_ready(eng, h, l):
            if l is L2:
                s = h % RING2
                eng.wait_ge(half_loaded[s], 16 * ((DEPTH * LAYER_ROUNDS if s < RING else 0) + h // RING2 + 1))
            else:
                s = h % RING
                eng.wait_ge(half_loaded[s], 16 * (l * LAYER_ROUNDS + (h // RING + 1)))
            return half_place(s)

        def slot_ready(pe, n, l, n_k):
            halves = [half_ready(pe, 2 * n + h, l).rearrange("p (k n) -> p k n", k=n_k // 2) for h in (0, 1)]
            return lambda k, c0, c1: halves[k // (n_k // 2)][:, k % (n_k // 2), c0:c1]

        def after_unit(eng, n, l):
            if ends_item(n):
                kind, g = FFN_SLOTS[UNITS[n][0]]
                take(eng, ("U", 2 * g + UNITS[n][1] // 2) if kind == "up" else ("D", 3), l)
            else:
                eng.wait_ge(unit_used, l * UNITS_INSIDE + sum(not ends_item(i) for i in range(n + 1)))

        def unit_weights(n, v):
            slot, j = UNITS[n]
            up = FFN_SLOTS[slot][0] == "up"
            if v is not None:
                at = (2 * (n % UNIT_BUFFERS) + v) * UNIT
                return split_w[:, at:at + UNIT].rearrange("p (k n) -> p k n", k=KC if up else 1)
            n_units = sum(s == slot for s, _ in UNITS)
            h = 2 * (8 + slot) + j // (n_units // 2)
            raw = half_place(h % RING)
            if up:
                return raw.rearrange("p (k n) -> p k n", k=KC)[:, :, (j % 2) * P:(j % 2 + 1) * P], h
            at = j % (n_units // 2) * UNIT
            return raw[:, at:at + UNIT].rearrange("p (k n) -> p k n", k=1), h

        block = ctx.enter_context(nc.Block())

        def slot_used(eng, l, n):
            kind, s = B2_SLOTS[n] if l == L2 else LAYER_SLOTS[n]
            last_item = {"ada": s, "mq": 1, "mk": 3, "mv": 4 * s + 3, "mo": 2 * s + 1, "dv": 4 * s + 3, "dq": 4 * s + 3,
                         "dk": 4 * s + 3, "pa": 2 * s + 1, "pb": 2 * s + 1, "wa": 2 * s + 1, "wb": 2 * s + 1}
            if kind in last_item:
                take(eng, (kind, last_item[kind]), l)
            elif kind == "wo":
                take(eng, ("Y", 3), l)
            elif kind == "in":
                take(eng, ("s", 2 * s), l)
                take(eng, ("s", 2 * s + 1), l)
            elif (kind, s) == ("out", 1):
                take(eng, ("M", 3), l)
            else:
                eng.wait_ge(slot_free, l + 1)

        def half_used(eng, l, h):
            n = h // 2
            if l == L2 or n < 8:
                slot_used(eng, l, n)
            else:
                units = [i for i in range(len(UNITS)) if unit_weights(i, None)[1] == h]
                eng.wait_ge(w_split, l * len(UNITS) + units[-1] + 1)

        def last_unit(kind, g):
            return max(n for n, (slot, _) in enumerate(UNITS) if FFN_SLOTS[slot] == (kind, g))

        def ffn_stages(split, convolve, finish):
            n, pending, whole = 0, None, None
            for slot, (kind, g) in enumerate(FFN_SLOTS):
                for i in range(sum(s_ == slot for s_, _ in UNITS)):
                    split(n)
                    n += 1
                    if i == 0 and whole is not None:
                        finish(whole)
                        whole = None
                    if i in (1, 3) and pending is not None:
                        convolve(pending, i // 2)
                        if i == 3:
                            pending, whole = None, pending
                if kind == "up":
                    assert pending is None
                    pending = g

        def expert_slot(pe, it, n, n_k):
            halves = []
            for h in (0, 1):
                s = PAIR_RING[(2 * n + h) % 12]
                pe.wait_ge(half_loaded[s], 16 * (2 * it) + 16 * (half_rounds[s] + n // 6 + 1))
                halves.append(half_place(s).rearrange("p (k n) -> p k n", k=n_k // 2))
            return lambda k, c0, c1: halves[k // (n_k // 2)][:, k % (n_k // 2), c0:c1]

        def over_pairs(eng, pair):
            with eng.Fori(0, PAIRS) as j:
                pair(j, j)
            eng.wait_ge(passes_ready, 1)
            n = eng.value_load(passes[0:1, 0:1], min_val=1, max_val=T // CAP)
            with eng.If(n > 1), eng.Fori(1, n) as r:
                with eng.Fori(0, PAIRS) as j:
                    pair(r * PAIRS + j, j)
            return n

        def load_mixer_parameters(eng, l):
            eng.dma_start(cols[:, 0:COL_FFN_PRE], w["cols"][l][:, 0:COL_FFN_PRE]).then_inc(mix_par_loaded, 16)
            eng.dma_start(mix_row[:, 0:D], w["norm_mix_post"][l:l + 1, :].partition_broadcast(P)).then_inc(mix_par_loaded, 16)
            eng.dma_start(mix_row[:, D:], w["ret_norm_g"][l:l + 1, :].partition_broadcast(P)).then_inc(mix_par_loaded, 16)

        def load_ffn_parameters(eng, l):
            eng.dma_start(cols[:, COL_FFN_PRE:N_COLS], w["cols"][l][:, COL_FFN_PRE:N_COLS]).then_inc(ffn_par_loaded, 16)
            eng.dma_start(ffn_row, w["norm_ffn_post"][l:l + 1, :].partition_broadcast(P)).then_inc(ffn_par_loaded, 16)

        def loop_layers(eng, layer):
            with eng.Fori(0, DEPTH) as l:
                layer(l)

        @block.sync
        def _(sp):
            def load_slot(l, n):
                kind, s = B2_SLOTS[n] if l == L2 else LAYER_SLOTS[n]
                chunks = lambda a: a.rearrange("(k p) n -> p k n", p=P)
                if kind == "up":
                    src = chunks(w["ffn_up"][l])
                    two = [src[:, :, u * D_FF + s * 256:u * D_FF + (s + 1) * 256] for u in (0, 1)]
                elif kind in ("out", "down", "wo"):
                    src = chunks({"out": w["w_out"], "down": w["ffn_down"], "wo": w["w_out_2"]}[kind][l % L2])
                    half = min(4, src.shape[1] - 4 * s) // 2
                    two = [src[:, 4 * s + h * half:4 * s + (h + 1) * half, :] for h in (0, 1)]
                else:
                    name, c0 = {"in": ("w_in", 0), "ada": ("ada_w_2", 0), "wa": ("w_branch_a_2", 0),
                                "wb": ("w_branch_b_2", 0)}.get(kind) or ("w_in_2", W_IN2_COLS[kind])
                    c0 += 512 * s
                    src = chunks(w[name][l % L2])
                    two = [src[:, h * 4:h * 4 + 4, c0:c0 + 512] for h in (0, 1)]
                for h in (0, 1):
                    g = 2 * n + h
                    if l == L2:
                        place = g % RING2
                        if RING <= g < RING2:
                            sp.wait_ge(early_loaded, 96)
                        elif g >= RING2:
                            half_used(sp, L2, g - RING2)
                        else:
                            half_used(sp, L2 - 1, 2 * len(LAYER_SLOTS) - RING + g)
                    else:
                        place = g % RING
                        if g >= RING:
                            half_used(sp, l, g - RING)
                        elif l:
                            half_used(sp, l - 1, 2 * len(LAYER_SLOTS) - RING + g)
                    n_k, n_col = two[h].shape[1:]
                    sp.dma_start(half_place(place)[:, 0:n_k * n_col].rearrange("p (k n) -> p k n", k=n_k), two[h]
                                 ).then_inc(half_loaded[place], 16)

            for l in range(DEPTH):
                for n in range(len(LAYER_SLOTS)):
                    load_slot(l, n)
                    if n == 13 and l + 1 < DEPTH:
                        sp.wait_ge(x_ready, 2 * l + 2)
                        load_mixer_parameters(sp, l + 1)
                    if n == RING and l:
                        sp.wait_ge(x_ready, 2 * l + 1)
                        load_ffn_parameters(sp, l)
            for n in range(len(B2_SLOTS)):
                load_slot(L2, n)

            def pair(it, j):
                for n, (kind, xx, q) in enumerate(PAIR_SLOTS):
                    n_k = 1 if kind == "w1" else 2
                    src = w["exp_w1_2" if kind == "w1" else "exp_w2_2"][0, 2 * j + xx].rearrange("(k p) n -> p k n", p=P)
                    for h in (0, 1):
                        s = PAIR_RING[(2 * n + h) % 12]
                        if h == 0:
                            sp.wait_ge(expert_slot_free, 12 * it + (n + 1))
                            sp.sem_inc(expert_load_claimed, 1)
                        k0 = n_k * (2 * q + h)
                        sp.dma_start(half_place(s).rearrange("p (k n) -> p k n", k=n_k), src[:, k0:k0 + n_k, :]
                                     ).then_inc(half_loaded[s], 16)

            over_pairs(sp, pair)
            for t in range(TT):
                sp.wait_ge(out_ready, t + 1)
                sp.dma_start(out[t * P:(t + 1) * P, :], xhat[:, t, :]).then_inc(out_stored, 16)
            sp.wait_ge(out_stored, 32)

        @block.gpsimd
        def _(pool):
            nc.gpsimd.memset(flatten(siluc), 0.0).then_inc(zeros_ready, 1)
            for v in (conf_pad[:, :, 0:30], sc_pad[:, :, 0:2]):
                nc.gpsimd.memset(v, 0.0).then_inc(zeros_ready, 1)
            pool.wait_ge(x_ready, 2 * DEPTH)
            for i, c0 in enumerate((2 * D, 5 * D)):
                pool.dma_start(g_rows[:, i, :], w["ada_b_2"][:, c0:c0 + D].partition_broadcast(P)).then_inc(g_bias_loaded, 16)
            take(pool, ("mR", 11), L2)
            pool.dma_start(norm_row, w["mlstm_norm_g_2"].rearrange("l a b -> l (a b)").partition_broadcast(P)
                           ).then_inc(norm_row_loaded, 16)
            pool.wait_ge(h_normed, 1)
            pool.dma_start(norm_row, w["diff_norm_g_2"].rearrange("l a b -> l (a b)").partition_broadcast(P)
                           ).then_inc(norm_row_loaded, 16)
            take(pool, ("O", NHD - 1), L2)
            nc.gpsimd.memset(b1_rows, 0.0).then_inc(b1_zeroed, 1)
            pool.wait_ge(b1_zeroed, 1)
            for dst, src in ((b1_rows[0:N_EXP, :], w["exp_b1_2"][0]), (b2_rows[0:N_EXP, :], w["exp_b2_2"][0]),
                             (router_w, w["router_w_2"][0].rearrange("(k p) e -> p k e", p=P)),
                             (final_row, w["final_norm_g_2"].partition_broadcast(P))):
                pool.dma_start(dst, src).then_inc(late_loaded, 16)

        @block.scalar
        def _(act):
            n_step = [0]

            def step(ins, l):
                n_step[0] += 1
                ins.then_inc(act_step, 1)
                act.wait_ge(act_step, l * ACT_STEPS + n_step[0])

            def flat(v):
                return v.rearrange("p a b -> p (a b)")

            def rms_of(rows, l):
                for t in range(TT):
                    ins = nc.scalar.activation(xhat[:, t, :], rows[t], ACT.Square, accum_out=sumsq[:, t:t + 1])
                step(ins, l)
                nc.scalar.activation(rms, sumsq, ACT.Sqrt, bias=EPS, scale=1.0 / D).then_inc(rms_ready, 1)

            def evac(key, l, out_, in_, func=ACT.Copy, **kw):
                nc.scalar.activation(out_, in_, func, **kw).then_inc(evacuated[bank_of(key)], 1)

            def halves(key, l, dst, scale):
                b = take(act, key, l).rearrange("p (c t) -> p c t", c=2)
                nc.scalar.activation(dst[0:64, 0:NH:2, :], b[0:64], ACT.Copy, scale=scale)
                evac(key, l, dst[64:128, 1:NH:2, :], b[64:128], scale=scale)

            def layer(l):
                n_step[0] = 0
                act.wait_ge(x_ready, 2 * l + 1)
                rms_of([x[:, t, :] for t in range(TT)], l)
                act.wait_ge(mix_par_loaded, 48 * l + 48)
                for i in (0, 2):
                    b = take(act, ("T", i), l)
                    for c in (0, 1):
                        k = 2 * i + c
                        ins = nc.scalar.activation(hT[:, k, :], b[:, c * T:(c + 1) * T], ACT.Copy,
                                                   scale=cols[:, COL_MIX_PRE + k:COL_MIX_PRE + k + 1])
                    ins.then_inc(evacuated[bank_of(("T", i))], 1)

                evac(("s", 1), l, flat(conf_gate), take(act, ("s", 1), l), ACT.Sigmoid)
                halves(("s", 2), l, q_z, SCALE)
                evac(("s", 3), l, flat(kT), take(act, ("s", 3), l))
                evac(("s", 4), l, flat(v_sb), take(act, ("s", 4), l))
                for h in range(NH):
                    evac(("Z", h), l, z[:, h, :], take(act, ("Z", h), l)[:, 0:DIAG])
                evac(("s", 7), l, flat(rv), take(act, ("s", 7), l))
                act.wait_ge(sb_abs, l + 1)
                step(nc.scalar.activation(soft, soft, ACT.Exp, scale=-1.0), l)
                nc.scalar.activation(soft, soft, ACT.Ln, bias=1.0).then_inc(sb_log, 1)
                halves(("RQ", 0), l, rq_z, 1.0)
                evac(("RK", 0), l, flat(rkT), take(act, ("RK", 0), l))
                evac(("s", 8), l, flat(rg), take(act, ("s", 8), l), ACT.Silu)
                evac(("s", 9), l, flat(sc_b), take(act, ("s", 9), l))
                evac(("s", 10), l, flat(sc_c), take(act, ("s", 10), l))
                act.wait_ge(sb_arg, l + 1)
                nc.scalar.activation(z, z, ACT.Exp).then_inc(sb_attn, 1)
                after_evacuation(act, ("CM", 0), l)
                nc.scalar.activation(conf_sq, conf, ACT.Square).then_inc(conf_sq_ready, 1)
                for c in (0, 1):
                    evac(("SB", c), l, catT[:, 2 + c, :], take(act, ("SB", c), l)[:, 0:T])
                evac(("CV", 0), l, conf_gate[:, 0, :], take(act, ("CV", 0), l)[:, 0:T], ACT.Sqrt,
                     bias=EPS, scale=1.0 / GW)
                act.wait_ge(ret_var_ready, l + 1)
                nc.scalar.activation(ret_std, ret_var, ACT.Sqrt, bias=EPS, scale=1.0 / HD).then_inc(ret_std_ready, 1)
                act.wait_ge(conf_normed, l + 1)
                for c in (0, 1):
                    ins = nc.scalar.activation(catT[:, c, :], conf[:, c, :], ACT.Silu,
                                               bias=cols[:, COL_CONF_LB + c:COL_CONF_LB + c + 1],
                                               scale=cols[:, COL_CONF_LG + c:COL_CONF_LG + c + 1])
                ins.then_inc(conf_cat, 1)
                evac(("RT", 0), l, flat(catT[:, 4:6, :]), take(act, ("RT", 0), l))
                for i in range(4):
                    b = take(act, ("M", i), l)
                rms_of([psum[:, 4 + 2 * t:6 + 2 * t, :].rearrange("p b n -> p (b n)") for t in range(TT)], l)
                act.wait_ge(x_ready, 2 * l + 2)
                rms_of([x[:, t, :] for t in range(TT)], l)
                act.wait_ge(ffn_par_loaded, 32 * l + 32)
                for i in range(4):
                    b = take(act, ("F", i), l)
                    for c in (0, 1):
                        k = 2 * i + c
                        ins = nc.scalar.activation(hT_split[:, 0, k, :], b[:, c * T:(c + 1) * T], ACT.Copy,
                                                   scale=cols[:, COL_FFN_PRE + k:COL_FFN_PRE + k + 1])
                    ins.then_inc(hT_high_ready, 1)

                def split(n):
                    if n >= UNIT_BUFFERS:
                        after_unit(act, n - UNIT_BUFFERS, l)
                    raw, h = unit_weights(n, None)
                    half_ready(act, h, l)
                    nc.scalar.activation(unit_weights(n, 0), raw, ACT.Copy).then_inc(w_high_ready, 1)

                def first_tap(g, u):
                    if g >= 2 and u == 0:
                        act.wait_ge(ff_ready, l * 11 + (g - 1))
                    b = take(act, ("U", 2 * g + u), l)
                    for c in (0, 1):
                        at = COL_FFN_W + (2 * FFC) * 2 + u * FFC + 2 * g + c
                        ins = nc.scalar.activation(taps[:, g % 2, 2 * u + c, :], b[:, c * T:(c + 1) * T],
                                                   ACT.Copy, scale=cols[:, at:at + 1])
                    ins.then_inc(tap_ready, 1)
                    if u == 1:
                        after_evacuation(act, ("U", 2 * g), l)
                        nc.scalar.activation(taps[:, g % 2, 0:2, :], taps[:, g % 2, 0:2, :], ACT.Silu).then_inc(silu_ready, 1)

                def high_part(g):
                    act.wait_ge(product_ready, l * 11 + (g + 1))
                    if g >= 4:
                        after_unit(act, last_unit("down", (g - 4) // 2), l)
                    nc.scalar.activation(ffT_split[:, 0, 2 * (g % 4):2 * (g % 4) + 2, :], taps[:, g % 2, 0:2, :], ACT.Copy
                                         ).then_inc(ff_high_ready, 1)

                ffn_stages(split, first_tap, high_part)
                for i in range(4):
                    take(act, ("D", i), l)
                rms_of([psum[:, 4 + 2 * t:6 + 2 * t, :].rearrange("p b n -> p (b n)") for t in range(TT)], l)
                assert n_step[0] == ACT_STEPS, n_step

            def second():
                n_step[0] = 0
                l = L2
                act.wait_ge(c_loaded, 16)
                act.wait_ge(zeros_ready, 4)
                nc.scalar.activation(siluc[:, :, 0:2], cT, ACT.Silu).then_inc(siluc_ready, 1)
                act.wait_ge(x_ready, 2 * L2 + 1)
                for dst, src in ((const2, w["const2"]), (cols2, w["cols2"]),
                                 (gate_w, w["w_in_2"][0].rearrange("(k p) n -> p k n", p=P)[:, :, 2048:2064]),
                                 (gate_b, w["mlstm_gate_b_2"].partition_broadcast(P)),
                                 (flatten(lam_row), w["diff_lambda_2"].rearrange("l a b -> l (a b)").partition_broadcast(P)),
                                 (router_b, w["router_b_2"].partition_broadcast(P))):
                    act.dma_start(dst, src).then_inc(early_loaded, 16)
                act.dma_start(ctx_row, w["ctx_2"].rearrange("b (t p) d -> p (b t) d", p=P)).then_inc(ctx_loaded, 16)
                for n in range(12):
                    evac(("ada", n), l, ada_rows[:, n % 2, :], take(act, ("ada", n), l))
                act.wait_ge(ctx_loaded, 16)
                rms_of([ctx_row[:, t, :] for t in range(TT)], l)
                act.wait_ge(ctx_hat_ready, 1)
                rms_of([x[:, t, :] for t in range(TT)], l)
                act.wait_ge(scale1_ready, 1)
                for key, v, t0 in (("CT", 1, 0), ("XT", 0, T)):
                    for i in (0, 2):
                        b = take(act, (key, i), l)
                        for c in (0, 1):
                            k = 2 * i + c
                            ins = nc.scalar.activation(uT[:, k, t0:t0 + T], b[:, c * T:(c + 1) * T], ACT.Identity,
                                                       scale=scale1[:, v, k:k + 1], bias=shift1[:, v, k:k + 1])
                        ins.then_inc(evacuated[bank_of((key, i))], 1)
                for i in (0, 1):
                    evac(("mq", i), l, flat(m_qT[:, 2 * i:2 * i + 2, :]), take(act, ("mq", i), l), scale=DQK ** -0.5)
                for h in range(NHM):
                    evac(("mk", h), l, m_kT[:, h, :], take(act, ("mk", h), l))
                for i in (0, 1):
                    evac(("mv", i), l, m_v[:, i, 0:2, 0:DV], take(act, ("mv", i), l).rearrange("p (h e) -> p h e", h=2))
                act.wait_ge(gate_abs_ready, 1)
                step(nc.scalar.activation(f_abs, f_abs, ACT.Exp, scale=-1.0), l)
                nc.scalar.activation(f_abs, f_abs, ACT.Ln, bias=1.0).then_inc(gate_log_ready, 1)
                for i in (2, 3, 4, 5, 6, 7):
                    evac(("mv", i), l, m_v[:, i % 4, 2 * (i // 4):2 * (i // 4) + 2, 0:DV],
                         take(act, ("mv", i), l).rearrange("p (h e) -> p h e", h=2))
                for i in range(4):
                    evac(("mo", i), l, o_row[:, i % 2, 512 * (i // 2):512 * (i // 2 + 1)], take(act, ("mo", i), l), ACT.Sigmoid)
                act.wait_ge(m_neg_ready, 1)
                step(nc.scalar.activation(m_neg, m_neg, ACT.Exp), l)
                for h in range(NHM):
                    after_evacuation(act, ("MB", h), l)
                    nc.scalar.activation(flat(decay[h % 2]), flat(decay[h % 2]), ACT.Exp, scale=-1.0).then_inc(decay_exp_ready, 1)
                act.wait_ge(h_ready, NHM)
                for t in range(TT):
                    for h in range(NHM):
                        ins = nc.scalar.activation(flat(decay[0])[:, (t * NHM + h) * DV:(t * NHM + h + 1) * DV], h_row[:, t, h * DV:(h + 1) * DV], ACT.Square,
                                                   accum_out=h_sq[:, t * NHM + h:t * NHM + h + 1])
                step(ins, l)
                nc.scalar.activation(h_rms, h_sq, ACT.Sqrt, bias=EPS, scale=1.0 / DV).then_inc(rms_ready, 1)
                for i in range(4):
                    evac(("AT", i), l, flat(a_outT[:, 2 * i:2 * i + 2, :]), take(act, ("AT", i), l))
                act.wait_ge(lam_sum_ready, 1)
                nc.scalar.activation(lam_exp, lam_sum, ACT.Exp).then_inc(lam_exp_ready, 1)

                def raws(h):
                    if h % 4 == 0:
                        for i in range(4):
                            evac(("dv", h + i), l, d_v[:, i, :], take(act, ("dv", h + i), l))
                    evac(("dq", h), l, raw[:, h % 2, 0:T], take(act, ("dq", h), l)[:, 0:T])
                    b = take(act, ("dk", h), l)
                    nc.scalar.activation(d_kT[:, h % 4, 0:T], b[:, 0:T], ACT.Copy)
                    evac(("dk", h), l, raw[:, h % 2, T:S], b[:, T:S])

                def softmax(h):
                    for t in range(TT):
                        act.wait_ge(row_max_ready, 2 * h + t + 1)
                        for m in (0, 1):
                            b = psum[:, bank_of(("S", 4 * h + 2 * t + m)), :]
                            ins = nc.scalar.activation(probs[:, t, m, :], b, ACT.Exp, bias=neg_max[:, t, m:m + 1],
                                                       scale=DHD ** -0.5, accum_out=row_sum[:, t, m:m + 1])
                            ins.then_inc(evacuated[bank_of(("S", 4 * h + 2 * t + m))], 1)

                def out_of(h):
                    for t in range(TT):
                        evac(("PT", 2 * h + t), l, aT[:, t, :], take(act, ("PT", 2 * h + t), l))
                    evac(("O", h), l, b_row[:, :, h * P:(h + 1) * P],
                         take(act, ("O", h), l)[:, 0:T].rearrange("p (t e) -> p t e", t=TT))

                for h in range(NHD):
                    if h % 4 == 0:
                        raws(h)
                    if h % 4 < 3:
                        raws(h + 1)
                    softmax(h)
                    out_of(h)
                after_evacuation(act, ("O", NHD - 1), l)
                for t in range(TT):
                    for h in range(NHD):
                        ins = nc.scalar.activation(squares[:, (t * NHD + h) * P:(t * NHD + h + 1) * P], b_row[:, t, h * P:(h + 1) * P], ACT.Square,
                                                   accum_out=b_sq[:, t * NHD + h:t * NHD + h + 1])
                step(ins, l)
                nc.scalar.activation(b_rms, b_sq, ACT.Sqrt, bias=EPS, scale=1.0 / P).then_inc(rms_ready, 1)
                for i in range(4):
                    evac(("BT", i), l, flat(b_outT[:, 2 * i:2 * i + 2, :]), take(act, ("BT", i), l))
                for g in (0, 1):
                    for key, dst in (("pa", gate_a), ("pb", gate_bb)):
                        for i in (0, 1):
                            if g:
                                after_evacuation(act, ("wa", i), l) if key == "pa" else act.wait_ge(y_ready, i + 1)
                            evac((key, 2 * g + i), l, dst[:, 512 * i:512 * i + 512], take(act, (key, 2 * g + i), l), ACT.Sigmoid)
                act.wait_ge(x_ready, 2 * L2 + 2)
                rms_of([x[:, t, :] for t in range(TT)], l)
                for i in (0, 2):
                    b = take(act, ("R", i), l)
                    for c in (0, 1):
                        k = 2 * i + c
                        ins = nc.scalar.activation(u2T[:, k, :], b[:, c * T:(c + 1) * T], ACT.Identity,
                                                   scale=scale2[:, k:k + 1], bias=modT[:, 2 * KC + k, 0:1])
                    ins.then_inc(evacuated[bank_of(("R", i))], 1)
                act.wait_ge(mask_ready, 1)
                for t in range(TT):
                    ins = nc.scalar.activation(exps[:, t, 0:N_EXP], logits[:, t, 0:N_EXP], ACT.Exp, bias=neg_top[:, t:t + 1])
                ins.then_inc(exp_ready, 1)
                evac(("gT", 0), l, gT[0:N_EXP, :], take(act, ("gT", 0), l)[0:N_EXP, 0:T])

                def pair(it, j):
                    b = take(act, ("G", 0), it)
                    for k in range(4):
                        ins = nc.scalar.activation(xgT[:, k, :], b[:, k * P:(k + 1) * P], ACT.Identity,
                                                   scale=scale2[:, k:k + 1], bias=modT[:, 2 * KC + k, 0:1])
                    ins.then_inc(evacuated[bank_of(("G", 0))], 1)
                    for n in (0, 1):
                        after_evacuation(act, ("GLU", n), it)
                        nc.scalar.activation(sig[n], glu[n], ACT.Sigmoid, scale=ALPHA).then_inc(sig_ready, 1)
                    evac(("ST", 0), it, spread_T, take(act, ("ST", 0), it)[:, 0:T])
                    evac(("AT2", 0), it, flat(actT[:, 0:4, :]), take(act, ("AT2", 0), it))
                    for n in (0, 1):
                        evac(("OUT", n), it, out_sb[:, 512 * n:512 * n + 512], take(act, ("OUT", n), it))

                over_pairs(act, pair)
                act.wait_ge(x_ready, 2 * L2 + 3)
                rms_of([x[:, t, :] for t in range(TT)], l)

            act.dma_start(x, w["x"].rearrange("b (t p) d -> p (b t) d", p=P)).then_inc(x_loaded, 16)
            act.dma_start(const[:, 0:SPARE], w["const"][:, 0:SPARE]).then_inc(const_loaded, 16)
            load_mixer_parameters(act, 0)
            act.dma_start(const[:, SPARE:], w["const"][:, SPARE:]).then_inc(tables_loaded, 16)
            act.dma_start(flatten(cT), w["cT"]).then_inc(c_loaded, 16)
            load_ffn_parameters(act, 0)
            loop_layers(act, layer)
            second()

        @block.vector
        def _(dve):
            n_step = [0]

            def step(ins, l, wait=True):
                n_step[0] += 1
                ins.then_inc(dve_step, 1)
                if wait:
                    dve.wait_ge(dve_step, l * DVE_STEPS + n_step[0])

            def inverse_rms(l, i):
                dve.wait_ge(rms_ready, 4 * l + i + 1)
                step(nc.vector.reciprocal(rinv, rms), l)

            def normalise(l, i):
                inverse_rms(l, i)
                for t in range(TT):
                    ins = nc.vector.tensor_scalar(xhat[:, t, :], x[:, t, :], rinv[:, t:t + 1], None, ALU.mult)
                ins.then_inc(xhat_ready, 1)

            def add_normed(l, i, keys, gain):
                inverse_rms(l, i)
                for t in range(TT):
                    for n in (0, 1):
                        b = bank_of(keys[2 * t + n])
                        cut = slice(512 * n, 512 * n + 512)
                        ins = nc.vector.scalar_tensor_tensor(out=xhat[:, t, cut], in0=psum[:, b, :],
                                                             scalar=rinv[:, t:t + 1], in1=gain[:, cut],
                                                             op0=ALU.mult, op1=ALU.mult)
                        ins.then_inc(evacuated[b], 1)
                after_evacuation(dve, keys[3], l)
                nc.vector.tensor_tensor(x_row[:, :], x_row[:, :], xhat.rearrange("p t d -> p (t d)"),
                                        ALU.add).then_inc(x_ready, 1)

            def gain_out(key, i, l, col):
                b = take(dve, (key, i), l)
                for c in (0, 1):
                    k = 2 * i + c
                    ins = nc.vector.tensor_scalar(hT[:, k, :], b[:, c * T:(c + 1) * T],
                                                  cols[:, col + k:col + k + 1], None, ALU.mult)
                ins.then_inc(evacuated[bank_of((key, i))], 1)

            def rotate(key, l, dst, ready):
                b = take(dve, key, l)
                d = dst.rearrange("p a b -> p (a b)")
                halves = lambda v: v.rearrange("p (g e) -> p g e", e=HD)
                bs, sn, sw = halves(b), halves(cst("ret_sin")), halves(swapped)
                nc.vector.tensor_tensor(d, b, cst("ret_cos"), ALU.mult)
                nc.vector.tensor_tensor(sw[:, :, 0:32], bs[:, :, 32:64], sn[:, :, 0:32], ALU.mult)
                nc.vector.tensor_tensor(sw[:, :, 32:64], bs[:, :, 0:32], sn[:, :, 32:64], ALU.mult
                                        ).then_inc(evacuated[bank_of(key)], 1)
                after_evacuation(dve, key, l)
                nc.vector.tensor_tensor(d, d, swapped, ALU.add).then_inc(ready, 1)

            def layer(l):
                n_step[0] = 0
                normalise(l, 0)
                dve.wait_ge(mix_par_loaded, 48 * l + 48)
                gain_out("T", 1, l, COL_MIX_PRE)
                gain_out("T", 3, l, COL_MIX_PRE)
                b = take(dve, ("s", 0), l).rearrange("p (c t) -> p c t", c=2)
                after_evacuation(dve, ("s", 1), l)
                nc.vector.tensor_tensor(conf_pad[:, :, 30:30 + T], b, conf_gate, ALU.mult
                                        ).then_inc(evacuated[bank_of(("s", 0))], 1)
                after_evacuation(dve, ("s", 0), l)

                def conf_taps(lo, hi):
                    for k in range(lo, hi):
                        for c in (0, 1):
                            wk = cols[:, COL_CONF_W + 2 * k + c:COL_CONF_W + 2 * k + c + 1]
                            src = conf_pad[:, c, k:k + T]
                            if k == 0:
                                ins = nc.vector.tensor_scalar(conf[:, c, :], src, wk,
                                                              cols[:, COL_CONF_B + c:COL_CONF_B + c + 1],
                                                              ALU.mult, ALU.add)
                            else:
                                dve.wait_ge(dve_step, l * DVE_STEPS + n_step[0] - 1)
                                ins = nc.vector.scalar_tensor_tensor(out=conf[:, c, :], in0=src, scalar=wk,
                                                                     in1=conf[:, c, :], op0=ALU.mult, op1=ALU.add)
                            if k == CONF_K - 1 and c == 1:
                                ins.then_inc(conf_ready, 1)
                            else:
                                step(ins, l, wait=False)

                conf_taps(0, 10)
                dve.wait_ge(tables_loaded, 16)
                rotate(("s", 5), l, rq, rq_ready)
                for h in range(NH):
                    after_evacuation(dve, ("Z", h), l)
                nc.vector.scalar_tensor_tensor(out=soft, in0=z, scalar=-1.0, in1=z, op0=ALU.mult, op1=ALU.max
                                               ).then_inc(sb_abs, 1)
                dve.wait_ge(rq_ready, l + 1)
                rotate(("s", 6), l, rk, rk_ready)
                conf_taps(10, 16)
                dve.wait_ge(sb_log, l + 1)
                step(nc.vector.scalar_tensor_tensor(out=soft, in0=z, scalar=0.0, in1=soft,
                                                    op0=ALU.max, op1=ALU.add), l)
                nc.vector.tensor_tensor(soft, soft, sb_mask4, ALU.mult).then_inc(sb_soft, 1)
                for h in range(NH):
                    b = take(dve, ("RS", h), l)
                    nc.vector.tensor_tensor(r_scores[:, h, :], b[:, 0:DIAG], ret_decay[:, h, :], ALU.mult
                                            ).then_inc(evacuated[bank_of(("RS", h))], 1)
                conf_taps(16, 20)
                for h in range(NH):
                    b = take(dve, ("I", h), l)
                    nc.vector.tensor_tensor(z[:, h, :], z[:, h, :], b[:, 0:DIAG], ALU.subtract
                                            ).then_inc(evacuated[bank_of(("I", h))], 1)
                after_evacuation(dve, ("I", 3), l)
                nc.vector.tensor_tensor(z, z, sb_neg4, ALU.add).then_inc(sb_arg, 1)
                conf_taps(20, CONF_K)
                b = take(dve, ("s", 11), l).rearrange("p (c t) -> p c t", c=2)
                after_evacuation(dve, ("s", 10), l)
                nc.vector.tensor_tensor(sc_pad[:, :, 2:2 + T], b, sc_c, ALU.mult
                                        ).then_inc(evacuated[bank_of(("s", 11))], 1)
                after_evacuation(dve, ("s", 11), l)
                for k in range(SC_K):
                    for c in (0, 1):
                        wk = cols[:, COL_SC_W + 2 * k + c:COL_SC_W + 2 * k + c + 1]
                        src = sc_pad[:, c, k:k + T]
                        if k == 0:
                            step(nc.vector.tensor_scalar(sc_c[:, c, :], src, wk, None, ALU.mult), l, wait=False)
                        else:
                            dve.wait_ge(dve_step, l * DVE_STEPS + n_step[0] - 1)
                            step(nc.vector.scalar_tensor_tensor(out=sc_c[:, c, :], in0=src, scalar=wk,
                                                                in1=sc_c[:, c, :], op0=ALU.mult, op1=ALU.add),
                                 l, wait=k == SC_K - 1 and c == 1)
                after_evacuation(dve, ("s", 9), l)
                nc.vector.tensor_tensor(catT[:, 6:8, :], sc_c, sc_b, ALU.mult).then_inc(sc_cat, 1)
                b = take(dve, ("CM", 0), l)
                for c in (0, 1):
                    ins = nc.vector.scalar_tensor_tensor(out=conf[:, c, :], in0=b[:, 0:T], scalar=-1.0 / GW,
                                                         in1=conf[:, c, :], op0=ALU.mult, op1=ALU.add)
                ins.then_inc(evacuated[bank_of(("CM", 0))], 1)
                b = take(dve, ("RO", 0), l).rearrange("p (g e) -> p g e", e=HD)
                retg = ret.rearrange("p a b -> p (a b)").rearrange("p (g e) -> p g e", e=HD)
                sqg = swapped.rearrange("p (g e) -> p g e", e=HD)
                wide = lambda v: v.unsqueeze(2).broadcast_to([P, 8, HD])
                step(nc.vector.tensor_reduce(ret_mu, b, AX, ALU.add), l)
                step(nc.vector.tensor_scalar(ret_mu, ret_mu, 1.0 / HD, None, ALU.mult), l)
                take(dve, ("CV", 0), l)
                nc.vector.tensor_tensor(retg, b, wide(ret_mu), ALU.subtract).then_inc(evacuated[bank_of(("RO", 0))], 1)
                after_evacuation(dve, ("RO", 0), l)
                step(nc.vector.tensor_tensor(sqg, retg, retg, ALU.mult), l)
                nc.vector.tensor_reduce(ret_var, sqg, AX, ALU.add).then_inc(ret_var_ready, 1)
                after_evacuation(dve, ("CV", 0), l)
                step(nc.vector.reciprocal(conf_gate[:, 1, :], conf_gate[:, 0, :]), l)
                nc.vector.tensor_tensor(conf, conf, conf_gate[:, 1:2, :].broadcast_to([P, 2, T]), ALU.mult
                                        ).then_inc(conf_normed, 1)
                dve.wait_ge(ret_std_ready, l + 1)
                step(nc.vector.reciprocal(ret_rinv, ret_std), l)
                step(nc.vector.tensor_tensor(retg, retg, wide(ret_rinv), ALU.mult), l)
                gain = mix_row[:, D:].unsqueeze(1).broadcast_to([P, TT, GW])
                step(nc.vector.tensor_tensor(ret, ret, gain, ALU.mult), l)
                after_evacuation(dve, ("s", 8), l)
                nc.vector.tensor_tensor(ret, ret, rg, ALU.mult).then_inc(ret_ready, 1)
                add_normed(l, 1, [("M", i) for i in range(4)], mix_row)
                dve.wait_ge(x_ready, 2 * l + 2)
                normalise(l, 2)
                dve.wait_ge(ffn_par_loaded, 32 * l + 32)
                for i in range(4):
                    dve.wait_ge(hT_high_ready, 4 * l + (i + 1))
                    b = psum[:, bank_of(("F", i)), :]
                    for c in (0, 1):
                        k = 2 * i + c
                        ins = nc.vector.scalar_tensor_tensor(out=hT_split[:, 1, k, :], in0=b[:, c * T:(c + 1) * T],
                                                             scalar=cols[:, COL_FFN_PRE + k:COL_FFN_PRE + k + 1],
                                                             in1=hT_split[:, 0, k, :], op0=ALU.mult, op1=ALU.subtract)
                    ins.then_inc(evacuated[bank_of(("F", i))], 1)

                def split(n):
                    dve.wait_ge(w_high_ready, l * len(UNITS) + (n + 1))
                    nc.vector.tensor_tensor(unit_weights(n, 1), unit_weights(n, None)[0], unit_weights(n, 0), ALU.subtract
                                            ).then_inc(w_split, 1)

                def later_taps(g, u):
                    b = take(dve, ("U", 2 * g + u), l)
                    dve.wait_ge(tap_ready, l * 22 + (2 * g + u + 1))
                    for k in (1, 2):
                        for c in (0, 1):
                            at = COL_FFN_W + (2 * FFC) * (2 - k) + u * FFC + 2 * g + c
                            o = taps[:, g % 2, 2 * u + c, k:T]
                            ins = nc.vector.scalar_tensor_tensor(
                                out=o, in0=b[:, c * T:(c + 1) * T - k], scalar=cols[:, at:at + 1], in1=o,
                                op0=ALU.mult, op1=ALU.add)
                            if k == 1:
                                step(ins, l, wait=c == 1)
                    ins.then_inc(evacuated[bank_of(("U", 2 * g + u))], 1)
                    if u == 1:
                        after_evacuation(dve, ("U", 2 * g + 1), l)
                        dve.wait_ge(silu_ready, l * 11 + (g + 1))
                        nc.vector.tensor_tensor(taps[:, g % 2, 0:2, :], taps[:, g % 2, 0:2, :], taps[:, g % 2, 2:4, :],
                                                ALU.mult).then_inc(product_ready, 1)

                def low_part(g):
                    dve.wait_ge(ff_high_ready, l * 11 + (g + 1))
                    nc.vector.tensor_tensor(ffT_split[:, 1, 2 * (g % 4):2 * (g % 4) + 2, :], taps[:, g % 2, 0:2, :],
                                            ffT_split[:, 0, 2 * (g % 4):2 * (g % 4) + 2, :], ALU.subtract).then_inc(ff_ready, 1)

                ffn_stages(split, later_taps, low_part)
                add_normed(l, 3, [("D", i) for i in range(4)], ffn_row)
                assert n_step[0] == DVE_STEPS, n_step

            def ptr_affine(key, v, i, l):
                b = take(dve, (key, i), l)
                t0 = 0 if key == "CT" else T
                for c in (0, 1):
                    k = 2 * i + c
                    ins = nc.vector.tensor_scalar(uT[:, k, t0:t0 + T], b[:, c * T:(c + 1) * T], scale1[:, v, k:k + 1],
                                                  shift1[:, v, k:k + 1], ALU.mult, ALU.add)
                ins.then_inc(evacuated[bank_of((key, i))], 1)

            def second():
                n_step[0] = 0
                l = L2
                norm_g = cols2[:, 0:2 * KC].rearrange("p (a k) -> p a k", a=2)
                ada_b = cols2[:, 2 * KC:6 * KC].unsqueeze(2).broadcast_to([P, 4 * KC, 2])
                dve.wait_ge(early_loaded, 96)
                step(nc.vector.tensor_copy(iota, cst2("iota")), l, wait=False)
                pairs = lam_row.rearrange("p (a b) e -> p a b e", b=2)
                step(nc.vector.tensor_tensor(lam_prod, pairs[:, :, 0, :], pairs[:, :, 1, :], ALU.mult), l)
                nc.vector.tensor_reduce(lam_sum, lam_prod, AX, ALU.add).then_inc(lam_sum_ready, 1)
                dve.wait_ge(g_bias_loaded, 32)

                def spread_rows(n):
                    i = 0 if n < 6 else 1
                    cut = slice(512 * (n % 2), 512 * (n % 2) + 512)
                    b = take(dve, ("mR", n), l)
                    nc.vector.tensor_tensor(g_rows[:, i, cut], g_rows[:, i, cut], b, ALU.add
                                            ).then_inc(evacuated[bank_of(("mR", n))], 1)

                def mod_columns(i):
                    b = take(dve, ("mT", i), l)[:, 0:32].rearrange("p (k v) -> p k v", v=2)
                    nc.vector.tensor_tensor(modT[:, 16 * i:16 * i + 16, :], b, ada_b[:, 16 * i:16 * i + 16, :], ALU.add
                                            ).then_inc(evacuated[bank_of(("mT", i))], 1)
                    after_evacuation(dve, ("mT", i), l)

                mod_columns(0)
                for v in (0, 1):
                    step(nc.vector.tensor_copy(shift1[:, v, :], modT[:, 0:KC, v]), l, wait=False)
                    ins = nc.vector.scalar_tensor_tensor(out=scale1[:, v, :], in0=modT[:, KC:2 * KC, v], scalar=1.0,
                                                         in1=norm_g[:, 0, :], op0=ALU.add, op1=ALU.mult)
                    ins.then_inc(scale1_ready, 1) if v else step(ins, l, wait=False)
                spread_rows(4)
                spread_rows(5)
                mod_columns(1)
                step(nc.vector.scalar_tensor_tensor(out=scale2, in0=modT[:, 3 * KC:4 * KC, 0], scalar=1.0,
                                                    in1=norm_g[:, 1, :], op0=ALU.add, op1=ALU.mult), l, wait=False)
                spread_rows(10)
                spread_rows(11)
                inverse_rms(l, 0)
                for t in range(TT):
                    ins = nc.vector.tensor_scalar(ctx_row[:, t, :], ctx_row[:, t, :], rinv[:, t:t + 1], None, ALU.mult)
                ins.then_inc(ctx_hat_ready, 1)
                dve.wait_ge(ctx_hat_ready, 1)
                normalise(l, 1)
                dve.wait_ge(scale1_ready, 1)
                for key, v in (("CT", 1), ("XT", 0)):
                    ptr_affine(key, v, 1, l)
                    ptr_affine(key, v, 3, l)
                ones_col = m_v[:, :, :, DV:DV + 1]
                step(nc.vector.memset(ones_col, 1.0), l, wait=False)
                for d in (0, 1):
                    for i in (0, 1):
                        step(nc.vector.memset(cummax[d][i], 0.0), l, wait=False)
                b = take(dve, ("mg", 0), l)[:, 0:ST * 16].rearrange("p (s n) -> p s n", n=16)
                nc.vector.tensor_tensor(gates, b, gate_b.unsqueeze(1).broadcast_to([P, ST, 16]), ALU.add
                                        ).then_inc(evacuated[bank_of(("mg", 0))], 1)
                after_evacuation(dve, ("mg", 0), l)
                by_dir = gates.rearrange("p s (d g h) -> p (s d) g h", d=2, g=2)
                in_gate, f_gate = by_dir[:, :, 0, :], by_dir[:, :, 1, :]
                step(nc.vector.tensor_scalar(f_neg, f_gate, -1.0, None, ALU.mult), l, wait=False)
                step(nc.vector.tensor_scalar(f_min, f_gate, 0.0, None, ALU.min), l)
                nc.vector.tensor_tensor(f_abs, f_gate, f_neg, ALU.max).then_inc(gate_abs_ready, 1)
                dve.wait_ge(gate_log_ready, 1)
                nc.vector.tensor_tensor(log_f, f_min, f_abs, ALU.subtract).then_inc(gate_ready, 1)
                b = take(dve, ("F", 9), l)
                f_sum = b[:, 0:32].rearrange("p (s h) -> p s h", h=4)
                step(nc.vector.tensor_copy(f_neg[:, 0:4, :], f_sum[:, 4:8, :]), l, wait=False)
                nc.vector.tensor_tensor(g_sub.rearrange("p s (d h) -> p (s d) h", d=2), in_gate, f_sum, ALU.subtract
                                        ).then_inc(evacuated[bank_of(("F", 9))], 1)
                for d in (0, 1):
                    b = take(dve, ("GT", d), l)[0:NHM, :]
                    step(nc.vector.tensor_reduce(ctx_max[0:NHM, d:d + 1], b[:, 0:T], AX, ALU.max), l)
                    step(nc.vector.tensor_scalar(ctx_max[0:NHM, d:d + 1], ctx_max[0:NHM, d:d + 1], 0.0, None, ALU.max), l)
                    at0 = P * (1 - d)
                    nc.vector.tensor_scalar(cummax[d][0][:, at0:at0 + T], b[:, T:S], ctx_max[0:NHM, d:d + 1], None,
                                            ALU.max).then_inc(evacuated[bank_of(("GT", d))], 1)
                    after_evacuation(dve, ("GT", d), l)
                for i in range(8):
                    for d in (0, 1):
                        src, dst = cummax[d][i % 2], cummax[d][(i + 1) % 2]
                        at0, shift = P * (1 - d), (1 << i) * (2 * d - 1)
                        ins = nc.vector.tensor_tensor(dst[:, at0:at0 + T], src[:, at0:at0 + T],
                                                      src[:, at0 + shift:at0 + shift + T], ALU.max)
                        if i == 7 and d == 1:
                            ins.then_inc(cummax_ready, 1)
                        else:
                            step(ins, l, wait=d == 1)
                b = take(dve, ("MR", 0), l)[:, 0:16].rearrange("p (s h) -> p s h", h=4)
                mn = m_neg.rearrange("p (s h) -> p s h", h=4)
                nc.vector.scalar_tensor_tensor(out=mn, in0=b, scalar=-1.0, in1=f_neg[:, 0:4, :],
                                               op0=ALU.mult, op1=ALU.subtract).then_inc(evacuated[bank_of(("MR", 0))], 1)
                after_evacuation(dve, ("MR", 0), l)
                nc.vector.tensor_scalar(m_neg, m_neg, 88.0, None, ALU.min).then_inc(m_neg_ready, 1)

                def decay_args(h):
                    b = take(dve, ("MB", h), l)
                    if h >= 2:
                        take(dve, ("H", 4 * (h - 2) + 3), l)
                    for d in (0, 1):
                        for st in range(ST):
                            g = g_sub[:, st, 4 * d + h:4 * d + h + 1]
                            ins = nc.vector.tensor_scalar(decay[h % 2][:, d, st * T:(st + 1) * T], b[:, d * T:(d + 1) * T],
                                                          g, 0.0, ALU.subtract, ALU.max)
                            if d == 0 or st < ST - 1:
                                step(ins, l, wait=False)
                    ins.then_inc(evacuated[bank_of(("MB", h))], 1)

                def weigh(h):
                    dve.wait_ge(decay_exp_ready, h + 1)
                    for d, tri in ((0, cst2("prefix")), (1, suffix)):
                        for t in range(TT):
                            v = decay[h % 2][:, d, (TT + t) * T + t * P:(TT + t) * T + (t + 1) * P]
                            step(nc.vector.tensor_tensor(v, v, tri, ALU.mult), l, wait=d == 1 and t == 1)
                    for q in (0, 1):
                        b = take(dve, ("QK", 2 * h + q), l)
                        for d in (0, 1):
                            v = decay[h % 2][:, d, 512 * q:512 * q + 512]
                            ins = nc.vector.tensor_tensor(v, v, b, ALU.mult)
                            if d == 0:
                                step(ins, l, wait=False)
                        ins.then_inc(evacuated[bank_of(("QK", 2 * h + q))], 1)

                def outputs(h):
                    for d in (0, 1):
                        for t in range(TT):
                            b = take(dve, ("H", 4 * h + 2 * d + t), l)
                            i = 2 * d + t
                            step(nc.vector.tensor_scalar(den[:, i:i + 1], b[:, DV:DV + 1], -1.0, None, ALU.mult), l)
                            step(nc.vector.tensor_tensor(den[:, i:i + 1], den[:, i:i + 1], b[:, DV:DV + 1], ALU.max), l)
                            e = m_neg[:, 4 * (2 * t + d) + h:4 * (2 * t + d) + h + 1]
                            step(nc.vector.tensor_tensor(den[:, i:i + 1], den[:, i:i + 1], e, ALU.max), l)
                            step(nc.vector.reciprocal(den2[:, i:i + 1], den[:, i:i + 1]), l)
                            o = h_row[:, t, h * DV:(h + 1) * DV]
                            if d == 0:
                                ins = nc.vector.tensor_scalar(o, b[:, 0:DV], den2[:, i:i + 1], None, ALU.mult)
                            else:
                                after_evacuation(dve, ("H", 4 * h + t), l)
                                ins = nc.vector.scalar_tensor_tensor(out=o, in0=b[:, 0:DV], scalar=den2[:, i:i + 1],
                                                                     in1=o, op0=ALU.mult, op1=ALU.add)
                            ins.then_inc(evacuated[bank_of(("H", 4 * h + i))], 1)
                    after_evacuation(dve, ("H", 4 * h + 3), l)
                    dve.sem_inc(h_ready, 1)

                decay_args(0)
                weigh(0)
                for h in range(1, NHM + 1):
                    if h < NHM:
                        decay_args(h)
                    if h < NHM:
                        weigh(h)
                    outputs(h - 1)
                dve.wait_ge(rms_ready, 4 * L2 + 3)
                dve.wait_ge(norm_row_loaded, 16)
                step(nc.vector.reciprocal(h_inv, h_rms), l)
                for t in range(TT):
                    for h in range(NHM):
                        v = h_row[:, t, h * DV:(h + 1) * DV]
                        i = t * NHM + h
                        step(nc.vector.scalar_tensor_tensor(out=v, in0=v, scalar=h_inv[:, i:i + 1],
                                                            in1=norm_row[:, h * DV:(h + 1) * DV],
                                                            op0=ALU.mult, op1=ALU.mult), l, wait=i == 2 * NHM - 1)
                after_evacuation(dve, ("mo", 3), l)
                nc.vector.tensor_tensor(h_row, h_row, o_row, ALU.mult).then_inc(h_normed, 1)
                dve.wait_ge(lam_exp_ready, 1)
                step(nc.vector.tensor_tensor(neg_lam, lam_exp[:, 1:2], lam_exp[:, 0:1], ALU.subtract), l)
                step(nc.vector.tensor_scalar(neg_lam, neg_lam, -LAM_INIT, None, ALU.add), l)
                for h in range(4):
                    step(nc.vector.memset(d_q[0:64, 2 * h + 1, :], 0.0), l, wait=False)
                    step(nc.vector.memset(d_q[64:128, 2 * h, :], 0.0), l, wait=False)
                cos2 = cst2("rope_cos").unsqueeze(1).broadcast_to([P, 2, T])
                sin2 = cst2("rope_sin").unsqueeze(1).broadcast_to([P, 2, T])

                def rope(h):
                    b = take(dve, ("rot", h), l)
                    r = raw[:, h % 2, :]
                    two = lambda v: v.rearrange("p (a t) -> p a t", a=2)
                    step(nc.vector.tensor_tensor(two(r), two(r), cos2, ALU.mult), l, wait=False)
                    if h:
                        dve.wait_ge(qk_ready, h)
                    nc.vector.tensor_tensor(two(turned), two(b), sin2, ALU.mult).then_inc(evacuated[bank_of(("rot", h))], 1)
                    after_evacuation(dve, ("rot", h), l)
                    if h >= 4:
                        take(dve, ("S", 4 * (h - 4) + 3), l)
                    for m in (0, 1):
                        rows = slice(64 * m, 64 * m + 64)
                        step(nc.vector.tensor_tensor(d_q[rows, 2 * (h % 4) + m, :], r[rows, 0:T], turned[rows, 0:T], ALU.add),
                             l, wait=False)
                    nc.vector.tensor_tensor(d_kT[:, h % 4, T:S], r[:, T:S], turned[:, T:S], ALU.add).then_inc(qk_ready, 1)

                def maxima(h):
                    for t in range(TT):
                        for m in (0, 1):
                            b = take(dve, ("S", 4 * h + 2 * t + m), l)
                            step(nc.vector.tensor_reduce(row_max[:, t, m:m + 1], b, AX, ALU.max), l, wait=m == 1)
                        nc.vector.tensor_scalar(neg_max[:, t, :], row_max[:, t, :], -DHD ** -0.5, None, ALU.mult
                                                ).then_inc(row_max_ready, 1)

                def difference(h):
                    for t in range(TT):
                        after_evacuation(dve, ("S", 4 * h + 2 * t), l)
                        after_evacuation(dve, ("S", 4 * h + 2 * t + 1), l)
                        step(nc.vector.reciprocal(row_inv[:, t, :], row_sum[:, t, :]), l)
                        step(nc.vector.tensor_tensor(map_scale[:, t, 0:1], row_inv[:, t, 1:2], neg_lam, ALU.mult), l)
                        p1 = probs[:, t, 1, :]
                        step(nc.vector.tensor_scalar(p1, p1, map_scale[:, t, 0:1], None, ALU.mult), l)
                        p0 = probs[:, t, 0, :]
                        nc.vector.scalar_tensor_tensor(out=p0, in0=p0, scalar=row_inv[:, t, 0:1], in1=p1,
                                                       op0=ALU.mult, op1=ALU.add).then_inc(attn_ready, 1)

                for h in range(NHD):
                    if h % 4 == 0:
                        rope(h)
                    maxima(h)
                    if h % 4 < 3:
                        rope(h + 1)
                    difference(h)
                dve.wait_ge(rms_ready, 4 * L2 + 4)
                dve.wait_ge(norm_row_loaded, 32)
                step(nc.vector.reciprocal(b_inv, b_rms), l)
                step(nc.vector.tensor_scalar(b_inv, b_inv, 1.0 - LAM_INIT, None, ALU.mult), l)
                for t in range(TT):
                    for h in range(NHD):
                        v = b_row[:, t, h * P:(h + 1) * P]
                        i = t * NHD + h
                        ins = nc.vector.scalar_tensor_tensor(out=v, in0=v, scalar=b_inv[:, i:i + 1],
                                                             in1=norm_row[:, h * P:(h + 1) * P], op0=ALU.mult, op1=ALU.mult)
                        if i < 2 * NHD - 1:
                            step(ins, l, wait=False)
                ins.then_inc(b_normed, 1)
                for g in (0, 1):
                    for i in (0, 1):
                        cut = slice(512 * i, 512 * i + 512)
                        y = flatten(yT[:, 4 * g + 2 * i:4 * g + 2 * i + 2, :])
                        b = take(dve, ("wa", 2 * g + i), l)
                        after_evacuation(dve, ("pa", 2 * g + i), l)
                        nc.vector.tensor_tensor(y, b, gate_a[:, cut], ALU.mult
                                                ).then_inc(evacuated[bank_of(("wa", 2 * g + i))], 1)
                        b = take(dve, ("wb", 2 * g + i), l)
                        after_evacuation(dve, ("pb", 2 * g + i), l)
                        nc.vector.tensor_tensor(gate_bb[:, cut], b, gate_bb[:, cut], ALU.mult
                                                ).then_inc(evacuated[bank_of(("wb", 2 * g + i))], 1)
                        after_evacuation(dve, ("wa", 2 * g + i), l)
                        after_evacuation(dve, ("wb", 2 * g + i), l)
                        nc.vector.tensor_tensor(y, y, gate_bb[:, cut], ALU.add).then_inc(y_ready, 1)
                for i in range(4):
                    t, half = divmod(i, 2)
                    cut = slice(512 * half, 512 * half + 512)
                    b = take(dve, ("Y", i), l)
                    nc.vector.tensor_tensor(xhat[:, t, cut], b, g_rows[:, 0, cut], ALU.mult
                                            ).then_inc(evacuated[bank_of(("Y", i))], 1)
                after_evacuation(dve, ("Y", 3), l)
                nc.vector.tensor_tensor(x_row[:, :], x_row[:, :], flatten(xhat), ALU.add).then_inc(x_ready, 1)
                dve.wait_ge(x_ready, 2 * L2 + 2)
                normalise(l, 4)
                for i in (1, 3):
                    b = take(dve, ("R", i), l)
                    for c in (0, 1):
                        k = 2 * i + c
                        ins = nc.vector.tensor_scalar(u2T[:, k, :], b[:, c * T:(c + 1) * T], scale2[:, k:k + 1],
                                                      modT[:, 2 * KC + k, 0:1], ALU.mult, ALU.add)
                    ins.then_inc(evacuated[bank_of(("R", i))], 1)
                below = -3e38
                step(nc.vector.memset(logits[:, :, N_EXP:], below), l, wait=False)
                b = take(dve, ("L", 0), l)[:, 0:TT * N_EXP].rearrange("p (t e) -> p t e", t=TT)
                nc.vector.tensor_tensor(logits[:, :, 0:N_EXP], b, router_b.unsqueeze(1).broadcast_to([P, TT, N_EXP]), ALU.add
                                        ).then_inc(evacuated[bank_of(("L", 0))], 1)
                after_evacuation(dve, ("L", 0), l)
                for t in range(TT):
                    step(nc.vector.max(top8[:, t, :], logits[:, t, 0:N_EXP]), l, wait=t == 1)
                step(nc.vector.tensor_scalar(neg_top, top8[:, :, 0], -1.0, None, ALU.mult), l, wait=False)
                step(nc.vector.memset(top8[:, :, TOP_K:], below), l)
                for t in range(TT):
                    step(nc.vector.match_replace(others[:, t, :], top8[:, t, :], logits[:, t, :], below), l, wait=t == 1)
                nc.vector.tensor_tensor(chosen, logits[:, :, 0:N_EXP], others[:, :, 0:N_EXP], ALU.not_equal
                                        ).then_inc(mask_ready, 1)
                dve.wait_ge(exp_ready, 1)
                step(nc.vector.tensor_tensor(gate_row, exps[:, :, 0:N_EXP], chosen, ALU.mult), l)
                step(nc.vector.tensor_reduce(gate_sum, gate_row, AX, ALU.add), l)
                step(nc.vector.reciprocal(gate_inv, gate_sum), l)
                nc.vector.tensor_tensor(gate_row, gate_row, gate_inv.unsqueeze(2).broadcast_to([P, TT, N_EXP]), ALU.mult
                                        ).then_inc(gates_ready, 1)
                by_pair = lambda v: v.rearrange("p (j t x) -> p t j x", j=PAIRS, t=TT)
                pairs = lambda v: v.rearrange("p (j x) -> p j x", x=2)
                dve.wait_ge(gates_ready, 1)
                b = take(dve, ("PC", 0), l)
                for t in range(TT):
                    step(nc.vector.tensor_copy(by_pair(pair_gate)[:, t], pairs(gate_row[:, t, :])), l, wait=False)
                    ins = nc.vector.scalar_tensor_tensor(out=by_pair(pair_slot)[:, t], in0=pairs(b[:, t * N_EXP:(t + 1) * N_EXP]),
                                                         scalar=1.0, in1=pairs(chosen[:, t, :]), op0=ALU.add, op1=ALU.mult)
                    if t == 0:
                        step(ins, l, wait=False)
                ins.then_inc(evacuated[bank_of(("PC", 0))], 1)
                after_evacuation(dve, ("PC", 0), l)
                step(nc.vector.tensor_scalar(pair_slot, pair_slot, -1.0, None, ALU.add), l)
                b = take(dve, ("CN", 0), l)
                nc.vector.tensor_reduce(most, b[:, 0:N_EXP], AX, ALU.max).then_inc(evacuated[bank_of(("CN", 0))], 1)
                after_evacuation(dve, ("CN", 0), l)
                step(nc.vector.tensor_scalar(n_pass, most, float(CAP), 1.0, ALU.is_gt, ALU.add), l)
                for k in range(2, T // CAP):
                    step(nc.vector.scalar_tensor_tensor(out=n_pass, in0=most, scalar=float(k * CAP), in1=n_pass,
                                                        op0=ALU.is_gt, op1=ALU.add), l)
                nc.vector.tensor_copy(passes[:, :], n_pass).then_inc(passes_ready, 1)
                slots4 = iota.unsqueeze(1).broadcast_to([P, 4, CAP])

                def pair(it, j):
                    n_pair_step = [0]

                    def pair_step(ins):
                        n_pair_step[0] += 1
                        ins.then_inc(pairs_step, 1)
                        dve.wait_ge(pairs_step, 5 * it + n_pair_step[0])

                    four = pair_slot[:, bass.ds(4 * j, 4)]
                    to_slots = lambda v: v.rearrange("p t (x s) -> p (t x) s", x=2)
                    pair_step(nc.vector.tensor_tensor(to_slots(pick), slots4, four.unsqueeze(2).broadcast_to([P, 4, CAP]),
                                                      ALU.is_equal))
                    nc.vector.tensor_copy(pick_e.rearrange("p (x s) -> p x s", x=2),
                                          ident[:, bass.ds(2 * j, 2)].unsqueeze(2).broadcast_to([P, 2, CAP]))
                    pair_step(nc.vector.tensor_scalar(four, four, -float(CAP), None, ALU.add))
                    nc.vector.tensor_tensor(to_slots(pick_gated), to_slots(pick),
                                            pair_gate[:, bass.ds(4 * j, 4)].unsqueeze(2).broadcast_to([P, 4, CAP]),
                                            ALU.mult).then_inc(picks_ready, 1)
                    b = take(dve, ("G", 1), it)
                    for k in range(4):
                        ins = nc.vector.tensor_scalar(xgT[:, 4 + k, :], b[:, k * P:(k + 1) * P], scale2[:, 4 + k:5 + k],
                                                      modT[:, 2 * KC + 4 + k, 0:1], ALU.mult, ALU.add)
                    ins.then_inc(evacuated[bank_of(("G", 1))], 1)
                    for n in (0, 1):
                        nc.vector.tensor_scalar(glu[n], take(dve, ("GLU", n), it), LIMIT, None, ALU.min
                                                ).then_inc(evacuated[bank_of(("GLU", n))], 1)
                        nc.vector.tensor_scalar(lin[n], take(dve, ("LIN", n), it), LIMIT, -LIMIT, ALU.min, ALU.max
                                                ).then_inc(evacuated[bank_of(("LIN", n))], 1)
                        after_evacuation(dve, ("LIN", n), it)
                        pair_step(nc.vector.scalar_tensor_tensor(out=lin[n], in0=lin[n], scalar=1.0, in1=glu[n],
                                                                 op0=ALU.add, op1=ALU.mult))
                        dve.wait_ge(sig_ready, 2 * it + (n + 1))
                        nc.vector.tensor_tensor(act_[n], lin[n], sig[n], ALU.mult).then_inc(hidden_ready, 1)
                    nc.vector.tensor_copy(flatten(actT[:, 4:8, :]), take(dve, ("AT2", 1), it)
                                          ).then_inc(evacuated[bank_of(("AT2", 1))], 1)
                    dve.sem_inc(pairs_step, 1)

                n = over_pairs(dve, pair)
                dve.wait_ge(late_loaded, 64)
                dve.wait_ge(combined, n * PAIRS)
                for i in range(4):
                    t, half = divmod(i, 2)
                    cut = slice(512 * half, 512 * half + 512)
                    step(nc.vector.tensor_tensor(xhat[:, t, cut], psum[:, i, :], g_rows[:, 1, cut], ALU.mult), l, wait=i == 3)
                nc.vector.tensor_tensor(x_row[:, :], x_row[:, :], flatten(xhat), ALU.add).then_inc(x_ready, 1)
                dve.wait_ge(x_ready, 2 * L2 + 3)
                inverse_rms(l, 5)
                for t in range(TT):
                    nc.vector.scalar_tensor_tensor(out=xhat[:, t, :], in0=x[:, t, :], scalar=rinv[:, t:t + 1], in1=final_row,
                                                   op0=ALU.mult, op1=ALU.mult).then_inc(out_ready, 1)

            for v in (q_z, rq_z):
                nc.vector.memset(v[0:64, 1:NH:2, :], 0.0)
                ins = nc.vector.memset(v[64:128, 0:NH:2, :], 0.0)
            ins.then_inc(zeros_ready, 1)
            dve.wait_ge(const_loaded, 16)
            dve.wait_ge(zeros_ready, 4)
            dve.wait_ge(x_loaded, 16)
            dve.sem_inc(x_ready, 1)
            loop_layers(dve, layer)
            second()

        @block.tensor
        def _(pe):
            def mm(out_, lhsT, rhs, first=True, last=True):
                return nc.tensor.matmul(out_, lhsT, rhs, start=first, stop=last)

            def done(ins, key):
                ins.then_inc(filled[bank_of(key)], 1)

            def transposed(key0, l, n, rows=xhat):
                if n:
                    pe.wait_ge(xhat_ready, 2 * l + n)
                for i in range(4):
                    b = fill(pe, (key0, i), l)
                    for c in (0, 1):
                        for t in range(TT):
                            k = 2 * i + c
                            ins = nc.tensor.transpose(b[:, c * T + t * P:c * T + (t + 1) * P],
                                                      rows[:, t, k * P:(k + 1) * P], ident)
                    done(ins, (key0, i))
                for i in range(4):
                    after_evacuation(pe, (key0, i), l)

            def transposed_pair(key, l, rows):
                b = fill(pe, key, l)
                for c in (0, 1):
                    for t in range(TT):
                        ins = nc.tensor.transpose(b[:, c * T + t * P:c * T + (t + 1) * P],
                                                  rows[:, t, c * P:(c + 1) * P], ident)
                done(ins, key)

            def diagonal_scores(key, l, keysT, queries, h):
                b = fill(pe, (key, h), l)
                mm(b[:, 0:T], keysT[:, h // 2, 0:P], queries[:, h, :])
                done(mm(b[:, T:DIAG], keysT[:, h // 2, P:T], queries[:, h, P:T]), (key, h))

            def tokens_down(key, l, n, lhs, first_k, n_k, ks, last_slot):
                wt = slot_ready(pe, n, l, 4)
                for i in range(4):
                    t, half = divmod(i, 2)
                    for k in range(n_k):
                        kk = first_k + k
                        ins = mm(psum[:, bank_of((key, i)), :], lhs[:, kk, t * P:(t + 1) * P],
                                 wt(k, half * 512, (half + 1) * 512), kk == 0, kk == ks - 1)
                    if last_slot:
                        done(ins, (key, i))
                if not last_slot:
                    ins.then_inc(expert_slot_free if key == "Y" else slot_free, 1)

            def second():
                l = L2
                n_slot = [0]

                def next_slot(kind, s):
                    assert B2_SLOTS[n_slot[0]] == (kind, s)
                    n_slot[0] += 1
                    return slot_ready(pe, n_slot[0] - 1, l, KC)

                def summed(b, lhs, rhs, n_k=KC):
                    for k in range(n_k):
                        ins = mm(b, lhs(k), rhs(k), k == 0, k == n_k - 1)
                    return ins

                pe.wait_ge(siluc_ready, 1)

                def ada_follow(n):
                    if n == 0:
                        pe.wait_ge(early_loaded, 96)
                    after_evacuation(pe, ("ada", n), l)
                    rows = ada_rows[:, n % 2, :]
                    if n in (4, 5, 10, 11):
                        b = fill(pe, ("mR", n), l)
                        done(mm(b, cst2("spread"), rows), ("mR", n))
                    else:
                        i, j = (0, n) if n < 4 else (1, n - 6)
                        b = psum[:, bank_of(("mT", i)), :]
                        if j == 0:
                            fill(pe, ("mT", i), l)
                        for c in range(4):
                            at_ = 8 * j + 2 * c
                            ins = mm(b[:, at_:at_ + 2], rows[:, c * P:(c + 1) * P], cst2("pick"))
                        if j == 3:
                            done(ins, ("mT", i))

                for n in range(12):
                    wt = next_slot("ada", n)
                    b = fill(pe, ("ada", n), l)
                    for k in range(KC):
                        q = k % 4
                        ins = mm(b[32 * q:32 * q + 32, :], siluc[:, k, :], wt(k, 0, 512), k < 4, k >= 4)
                    done(ins, ("ada", n))
                    if n:
                        ada_follow(n - 1)
                ada_follow(11)
                pe.wait_ge(ctx_hat_ready, 1)
                transposed("CT", l, 0, ctx_row)
                transposed("XT", l, 1)
                wt = next_slot("mq", 0)
                for i in (0, 1):
                    b = fill(pe, ("mq", i), l)
                    for c in (0, 1):
                        ins = summed(b[:, c * T:(c + 1) * T], lambda k: wt(k, (2 * i + c) * P, (2 * i + c + 1) * P),
                                     lambda k: uT[:, k, T:S])
                    done(ins, ("mq", i))
                wt = next_slot("mk", 0)
                for h in range(NHM):
                    b = fill(pe, ("mk", h), l)
                    done(summed(b, lambda k: wt(k, h * P, (h + 1) * P), lambda k: uT[:, k, :]), ("mk", h))
                b = fill(pe, ("mg", 0), l)
                for st in range(ST):
                    ins = summed(b[:, 16 * st:16 * st + 16], lambda k: uT[:, k, st * P:(st + 1) * P],
                                 lambda k: gate_w[:, k, :])
                done(ins, ("mg", 0))

                def token_rows(key, s, tiles):
                    wt = next_slot(key, s)
                    for i, st in enumerate(tiles):
                        item = (key, len(tiles) * s + i)
                        b = fill(pe, item, l)
                        done(summed(b, lambda k: uT[:, k, st * P:(st + 1) * P], lambda k: wt(k, 0, 512)), item)

                token_rows("mv", 0, range(ST))
                pe.wait_ge(gate_ready, 1)
                b = fill(pe, ("F", 9), l)
                prefix = cst2("prefix")
                for st in range(ST):
                    terms = [(s_, ones) for s_ in range(st)] + [(st, prefix)]
                    for n, (s_, tri) in enumerate(terms):
                        mm(b[:, 8 * st:8 * st + 4], tri, log_f[:, 2 * s_, :], n == 0, n == len(terms) - 1)
                    whole = [0, 1] if st >= TT else []
                    later = [s_ for s_ in range(st + 1, TT if st < TT else ST)]
                    terms = [(s_, ones) for s_ in whole + later] + [(st, suffix)]
                    for n, (s_, tri) in enumerate(terms):
                        ins = mm(b[:, 8 * st + 4:8 * st + 8], tri, log_f[:, 2 * s_ + 1, :], n == 0,
                                 n == len(terms) - 1)
                done(ins, ("F", 9))
                after_evacuation(pe, ("F", 9), l)
                for d in (0, 1):
                    b = fill(pe, ("GT", d), l)
                    for st in range(ST):
                        ins = nc.tensor.transpose(b[0:NHM, st * P:(st + 1) * P], g_sub[:, st, 4 * d:4 * d + 4], ident)
                    done(ins, ("GT", d))
                token_rows("mv", 1, range(ST))
                token_rows("mo", 0, (2, 3))
                token_rows("mo", 1, (2, 3))
                pe.wait_ge(cummax_ready, 1)
                b = fill(pe, ("MR", 0), l)
                for t in range(TT):
                    for d in (0, 1):
                        i = 2 * t + d
                        at_ = P * (1 - d) + t * P
                        ins = nc.tensor.transpose(b[:, 4 * i:4 * i + 4], cummax[d][0][:, at_:at_ + P], ident[0:NHM, 0:NHM])
                done(ins, ("MR", 0))
                for i in (0, 1):
                    after_evacuation(pe, ("mq", i), l)

                def m_scores(h):
                    b = fill(pe, ("MB", h), l)
                    pick_h = ident[0:NHM, h:h + 1].broadcast_to([NHM, P])
                    for d in (0, 1):
                        ins = mm(b[:, d * T:(d + 1) * T], pick_h, cummax[d][0][:, P * (1 - d):P * (1 - d) + T])
                    done(ins, ("MB", h))
                    after_evacuation(pe, ("mk", h), l)
                    for q in (0, 1):
                        b = fill(pe, ("QK", 2 * h + q), l)
                        for c in (0, 1):
                            st = 2 * q + c
                            ins = mm(b[:, c * T:(c + 1) * T], m_kT[:, h, st * P:(st + 1) * P], m_qT[:, h, :])
                        done(ins, ("QK", 2 * h + q))

                def m_outputs(h):
                    after_evacuation(pe, ("QK", 2 * h + 1), l)
                    for d in (0, 1):
                        for t in range(TT):
                            tiles = [0, 1, 2, 3]
                            if (d, t) == (0, 0):
                                tiles = [0, 1, 2]
                            if (d, t) == (1, 1):
                                tiles = [0, 1, 3]
                            b = fill(pe, ("H", 4 * h + 2 * d + t), l)
                            for n, st in enumerate(tiles):
                                ins = mm(b[:, 0:DV + 1], decay[h % 2][:, d, st * T + t * P:st * T + (t + 1) * P],
                                         m_v[:, st, h, 0:DV + 1], n == 0, n == len(tiles) - 1)
                            done(ins, ("H", 4 * h + 2 * d + t))

                for i in range(8):
                    after_evacuation(pe, ("mv", i), l)
                for h in range(NHM + 1):
                    if h < NHM:
                        m_scores(h)
                    if h:
                        m_outputs(h - 1)
                pe.wait_ge(h_normed, 1)
                transposed("AT", l, 0, h_row)
                for g in (0, 1):
                    token_rows("dv", g, range(ST))
                    wq, wk = next_slot("dq", g), next_slot("dk", g)

                    def project_head(h):
                        hh = h % 4
                        b = fill(pe, ("dq", h), l)
                        done(summed(b[:, 0:T], lambda k: wq(k, hh * P, (hh + 1) * P), lambda k: uT[:, k, T:S]), ("dq", h))
                        b = fill(pe, ("dk", h), l)
                        done(summed(b, lambda k: wk(k, hh * P, (hh + 1) * P), lambda k: uT[:, k, :]), ("dk", h))

                    def partners(h):
                        after_evacuation(pe, ("dq", h), l)
                        after_evacuation(pe, ("dk", h), l)
                        b = fill(pe, ("rot", h), l)
                        done(mm(b, cst2("partner"), raw[:, h % 2, :]), ("rot", h))

                    project_head(4 * g)
                    partners(4 * g)
                    for h in range(4 * g, 4 * g + 4):
                        if h % 4 < 3:
                            project_head(h + 1)
                        pe.wait_ge(qk_ready, h + 1)
                        for i in range(4):
                            t, m = divmod(i, 2)
                            b = fill(pe, ("S", 4 * h + i), l)
                            done(mm(b, d_q[:, 2 * (h % 4) + m, t * P:(t + 1) * P], d_kT[:, h % 4, :]), ("S", 4 * h + i))
                        if h % 4 < 3:
                            partners(h + 1)
                        for t in range(TT):
                            pe.wait_ge(attn_ready, 2 * h + t + 1)
                            b = fill(pe, ("PT", 2 * h + t), l)
                            for st in range(ST):
                                ins = nc.tensor.transpose(b[:, st * P:(st + 1) * P], probs[:, t, 0, st * P:(st + 1) * P], ident)
                            done(ins, ("PT", 2 * h + t))
                        if h % 4 == 0:
                            for i in range(4):
                                after_evacuation(pe, ("dv", 4 * g + i), l)
                        b = fill(pe, ("O", h), l)
                        for t in range(TT):
                            after_evacuation(pe, ("PT", 2 * h + t), l)
                            for st in range(ST):
                                ins = mm(b[:, t * P:(t + 1) * P], aT[:, t, st * P:(st + 1) * P],
                                         d_v[:, st, (h % 4) * P:(h % 4 + 1) * P], st == 0, st == ST - 1)
                        done(ins, ("O", h))
                pe.wait_ge(b_normed, 1)
                transposed("BT", l, 0, b_row)
                for i in range(4):
                    after_evacuation(pe, ("AT", i), l)
                for g in (0, 1):
                    for key in ("pa", "pb", "wa", "wb"):
                        wt = next_slot(key, g)
                        src, t0 = {"wa": (a_outT, 0), "wb": (b_outT, 0)}.get(key, (uT, T))
                        for i in (0, 1):
                            b = fill(pe, (key, 2 * g + i), l)
                            for c in (0, 1):
                                    ins = summed(b[:, c * T:(c + 1) * T], lambda k: wt(k, (2 * i + c) * P, (2 * i + c + 1) * P),
                                             lambda k: src[:, k, t0:t0 + T])
                            done(ins, (key, 2 * g + i))
                        if g == 1 and key != "pa":
                            take(pe, (key, 3), l)
                            pe.sem_inc(expert_slot_free, 1)
                pe.wait_ge(y_ready, 4)
                for i in range(4):
                    fill(pe, ("Y", i), l)
                for s_ in (0, 1):
                    tokens_down("Y", l, n_slot[0] + s_, yT, 4 * s_, 4, KC, s_ == 1)
                take(pe, ("Y", 3), l)
                pe.sem_inc(expert_slot_free, 1)
                transposed("R", l, 2)
                pe.wait_ge(late_loaded, 64)
                b = fill(pe, ("L", 0), l)
                for t in range(TT):
                    ins = summed(b[:, t * N_EXP:(t + 1) * N_EXP], lambda k: u2T[:, k, t * P:(t + 1) * P],
                                 lambda k: router_w[:, k, :])
                done(ins, ("L", 0))
                pe.wait_ge(mask_ready, 1)
                b = fill(pe, ("PC", 0), l)
                before = cst2("before")
                mm(b[:, 0:N_EXP], before, chosen[:, 0, :])
                mm(b[:, N_EXP:2 * N_EXP], ones, chosen[:, 0, :], True, False)
                done(mm(b[:, N_EXP:2 * N_EXP], before, chosen[:, 1, :], False, True), ("PC", 0))
                take(pe, ("PC", 0), l)
                pe.sem_inc(expert_slot_free, 1)
                b = fill(pe, ("CN", 0), l)
                mm(b[:, 0:N_EXP], ones, chosen[:, 0, :], True, False)
                done(mm(b[:, 0:N_EXP], ones, chosen[:, 1, :], False, True), ("CN", 0))
                pe.wait_ge(gates_ready, 1)
                b = fill(pe, ("gT", 0), l)
                for t in range(TT):
                    ins = nc.tensor.transpose(b[0:N_EXP, t * P:(t + 1) * P], gate_row[:, t, :], ident)
                done(ins, ("gT", 0))
                after_evacuation(pe, ("gT", 0), l)

                def sum_up(i, lhsT, rhs, first=False):
                    return nc.tensor.matmul(psum[:, i, :], lhsT, rhs, start=first, stop=True, skip_group_check=True)

                for i in range(4):
                    t, n = divmod(i, 2)
                    fill(pe, ("YM", i), l)
                    sum_up(i, gT[0:N_EXP, t * P:(t + 1) * P], b2_rows[0:N_EXP, 512 * n:512 * n + 512], True)

                def part_mm(b, xx, lhs, rhs, first=False, last=False):
                    rows = slice(CAP * xx, CAP * (xx + 1))
                    return nc.tensor.matmul(b[rows, :], lhs[:, rows], rhs, start=first, stop=last, skip_group_check=True)

                def pair(it, j):
                    pe.wait_ge(picks_ready, it + 1)
                    for g in (0, 1):
                        b = fill(pe, ("G", g), it)
                        for c in range(4):
                            k = 4 * g + c
                            for t in range(TT):
                                ins = mm(b[:, c * P:(c + 1) * P], xhat[:, t, k * P:(k + 1) * P], pick[:, t, :], t == 0, t == 1)
                        done(ins, ("G", g))
                    banks = [("GLU", 0, 0), ("LIN", 0, D), ("GLU", 1, 512), ("LIN", 1, D + 512)]
                    for key, n, c0 in banks:
                        b = fill(pe, (key, n), it)
                        nc.tensor.matmul(b, pick_e, b1_rows[:, c0:c0 + 512], start=True, stop=False, skip_group_check=True)
                    after_evacuation(pe, ("G", 0), it)
                    for q in range(4):
                        if q == 2:
                            after_evacuation(pe, ("G", 1), it)
                        wt = [expert_slot(pe, it, 2 * q + xx, 2) for xx in (0, 1)]
                        order = ([(k, i) for k in (0, 1) for i in range(4)] if q < 3 else
                                 [(k, i) for i in range(4) for k in (0, 1)])
                        for k, i in order:
                            key, n, c0 = banks[i]
                            end_of_bank = q == 3 and k == 1
                            for xx in (0, 1):
                                ins = part_mm(psum[:, bank_of((key, n)), :], xx, xgT[:, 2 * q + k, :],
                                              wt[xx](k, c0, c0 + 512), last=end_of_bank)
                                if xx and end_of_bank:
                                    done(ins, (key, n))
                                elif (k, i) == (1, 3):
                                    ins.then_inc(expert_slot_free, 1)
                    b = fill(pe, ("ST", 0), it)
                    nc.tensor.transpose(b[:, 0:P], pick_gated[:, 0, :], ident).then_inc(expert_slot_free, 1)
                    done(nc.tensor.transpose(b[:, P:T], pick_gated[:, 1, :], ident), ("ST", 0))

                    def hidden_transposed(n):
                        pe.wait_ge(hidden_ready, 2 * it + (n + 1))
                        b = fill(pe, ("AT2", n), it)
                        for c in range(4):
                            ins = nc.tensor.transpose(b[:, c * P:(c + 1) * P], act_[n][:, c * P:(c + 1) * P], ident)
                        done(ins, ("AT2", n))

                    hidden_transposed(0)
                    after_evacuation(pe, ("AT2", 0), it)
                    for n in (0, 1):
                        fill(pe, ("OUT", n), it)
                    for q in (0, 1):
                        wt = [expert_slot(pe, it, 8 + 2 * q + xx, 4) for xx in (0, 1)]
                        if q:
                            after_evacuation(pe, ("AT2", 1), it)
                        order = [(k, n) for k in range(4) for n in (0, 1)] if q == 0 else [(k, n) for n in (0, 1) for k in range(4)]
                        for k, n in order:
                            if (q, k, n) == (0, 2, 0):
                                hidden_transposed(1)
                            for xx in (0, 1):
                                ins = part_mm(psum[:, bank_of(("OUT", n)), :], xx, actT[:, 4 * q + k, :],
                                              wt[xx](k, 512 * n, 512 * n + 512), q + k == 0, q + k == 4)
                                if xx and q and k == 3:
                                    done(ins, ("OUT", n))
                                elif (k, n) == (3, 1):
                                    ins.then_inc(expert_slot_free, 1)
                    after_evacuation(pe, ("ST", 0), it)
                    for n in (0, 1):
                        after_evacuation(pe, ("OUT", n), it)
                        for t in range(TT):
                            ins = sum_up(2 * t + n, spread_T[:, t * P:(t + 1) * P], out_sb[:, 512 * n:512 * n + 512])
                            if (n, t) == (0, 0):
                                ins.then_inc(expert_slot_free, 1)
                    ins.then_inc(combined, 1)

                over_pairs(pe, pair)

            def layer(l):
                def project(s):
                    wt = slot_ready(pe, s, l, KC)
                    for i in (2 * s, 2 * s + 1):
                        b = fill(pe, ("s", i), l)
                        at = (i % 2) * 256
                        for c in (0, 1):
                            for k in range(KC):
                                if i in ROW_SLICES:
                                    lhsT, rhs = hT[:, k, c * P:(c + 1) * P], wt(k, at, at + 256)
                                else:
                                    lhsT, rhs = wt(k, at + c * P, at + (c + 1) * P), hT[:, k, :]
                                ins = mm(b[:, c * T:(c + 1) * T], lhsT, rhs, k == 0, k == KC - 1)
                        done(ins, ("s", i))

                transposed("T", l, 1)
                for s in range(3):
                    project(s)
                after_evacuation(pe, ("s", 2), l)
                after_evacuation(pe, ("s", 3), l)
                for h in range(NH):
                    diagonal_scores("Z", l, kT, q_z, h)
                project(3)
                pe.wait_ge(rq_ready, l + 1)
                transposed_pair(("RQ", 0), l, rq)
                pe.wait_ge(rk_ready, l + 1)
                transposed_pair(("RK", 0), l, rk)
                project(4)
                after_evacuation(pe, ("RQ", 0), l)
                after_evacuation(pe, ("RK", 0), l)
                for h in range(NH):
                    diagonal_scores("RS", l, rkT, rq_z, h)
                project(5)
                pe.wait_ge(sb_soft, l + 1)
                for h in range(NH):
                    b = fill(pe, ("I", h), l)
                    mm(b[:, 0:T], suffix, soft[:, h, 0:T], True, False)
                    mm(b[:, P:T], ones, soft[:, h, T:DIAG], False, True)
                    done(mm(b[:, T:DIAG], suffix, soft[:, h, T:DIAG]), ("I", h))
                after_evacuation(pe, ("s", 7), l)
                b = fill(pe, ("RO", 0), l).rearrange("p (t h e) -> p t h e", t=TT, h=NH)
                for h in range(NH):
                    after_evacuation(pe, ("RS", h), l)
                    cut = slice(h * HD, (h + 1) * HD)
                    mm(b[:, 0, h, :], r_scores[:, h, 0:P], rv[:, 0, cut])
                    mm(b[:, 1, h, :], r_scores[:, h, P:T], rv[:, 0, cut], True, False)
                    ins = mm(b[:, 1, h, :], r_scores[:, h, T:DIAG], rv[:, 1, cut], False, True)
                done(ins, ("RO", 0))
                pe.wait_ge(sb_attn, l + 1)
                after_evacuation(pe, ("s", 4), l)
                for c in (0, 1):
                    b = fill(pe, ("SB", c), l)
                    for h in (2 * c, 2 * c + 1):
                        rows = slice((h % 2) * HD, (h % 2 + 1) * HD)
                        cut = slice(h * HD, (h + 1) * HD)
                        mm(b[rows, 0:T], v_sb[:, 0, cut], z[:, h, 0:T], True, False)
                        ins = mm(b[rows, P:T], v_sb[:, 1, cut], z[:, h, T:DIAG], False, True)
                    done(ins, ("SB", c))
                pe.wait_ge(conf_ready, l + 1)
                b = fill(pe, ("CM", 0), l)
                mm(b[:, 0:T], ones, conf[:, 0, :], True, False)
                done(mm(b[:, 0:T], ones, conf[:, 1, :], False, True), ("CM", 0))
                pe.wait_ge(conf_sq_ready, l + 1)
                b = fill(pe, ("CV", 0), l)
                mm(b[:, 0:T], ones, conf_sq[:, 0, :], True, False)
                done(mm(b[:, 0:T], ones, conf_sq[:, 1, :], False, True), ("CV", 0))
                pe.wait_ge(ret_ready, l + 1)
                transposed_pair(("RT", 0), l, ret)
                pe.wait_ge(sc_cat, l + 1)
                pe.wait_ge(conf_cat, l + 1)
                after_evacuation(pe, ("SB", 1), l)
                after_evacuation(pe, ("RT", 0), l)
                for i in range(4):
                    fill(pe, ("M", i), l)
                tokens_down("M", l, 6, catT, 0, 4, KC, False)
                tokens_down("M", l, 7, catT, 4, 4, KC, True)
                transposed("F", l, 2)
                for n, (slot, j) in enumerate(UNITS):
                    kind, g = FFN_SLOTS[slot]
                    pe.wait_ge(w_split, l * len(UNITS) + (n + 1))
                    wu = [unit_weights(n, v) for v in (0, 1)]
                    last = ends_item(n)
                    if kind == "up":
                        u, c = divmod(j, 2)
                        b = fill(pe, ("U", 2 * g + u), l) if c == 0 else psum[:, bank_of(("U", 2 * g + u)), :]
                        for k in range(KC):
                            for i, (a, v) in enumerate(PASSES):
                                ins = mm(b[:, c * T:(c + 1) * T], wu[a][:, k, :], hT_split[:, v, k, :], k + i == 0,
                                         k == KC - 1 and i == 2)
                        if last:
                            done(ins, ("U", 2 * g + u))
                    else:
                        kk = 4 * g + j
                        if j == 0:
                            pe.wait_ge(ff_ready, l * 11 + min(2 * g + 2, 11))
                        for i in range(4):
                            if kk == 0:
                                fill(pe, ("D", i), l)
                            t, half = divmod(i, 2)
                            for p_, (a, v) in enumerate(PASSES):
                                ins = mm(psum[:, bank_of(("D", i)), :], ffT_split[:, v, kk % 8, t * P:(t + 1) * P],
                                         wu[a][:, 0, half * 512:(half + 1) * 512], kk + p_ == 0, kk == FFC - 1 and p_ == 2)
                            if last:
                                done(ins, ("D", i))
                    if not last:
                        ins.then_inc(unit_used, 1)

            for b in range(8):
                pe.sem_inc(evacuated[b], 1)
            pe.wait_ge(const_loaded, 16)
            pe.wait_ge(zeros_ready, 4)
            loop_layers(pe, layer)
            second()


def pack_cols(inputs):
    def chunks(a):
        a = np.asarray(a)
        a = a.reshape(DEPTH, -1, a.shape[-1] // P, P)
        return a.transpose(0, 3, 1, 2).reshape(DEPTH, P, -1)

    names = ("norm_mix_pre", "conf_dw_w", "conf_dw_b", "conf_ln_g", "conf_ln_b", "sc_conv_w", "norm_ffn_pre",
             "ffn_conv_w")
    return np.ascontiguousarray(np.concatenate([chunks(inputs[n]) for n in names], axis=2))


def pack_cols2(inputs):
    ada = np.asarray(inputs["ada_b_2"])[0].reshape(6, D)[[0, 1, 3, 4]].reshape(-1)
    flat = np.concatenate([np.asarray(inputs["norm1_g_2"])[0], np.asarray(inputs["norm2_g_2"])[0], ada])
    return np.ascontiguousarray(flat.reshape(-1, P).T)


def pack_c(inputs):
    both = np.stack([np.asarray(inputs["c_2"])[0], np.asarray(inputs["c_ctx_2"])])
    return np.ascontiguousarray(both.reshape(2, KC, P).transpose(2, 1, 0).reshape(P, 2 * KC))


PACKED = ("norm_mix_pre", "norm_ffn_pre", "conf_dw_w", "conf_dw_b", "conf_ln_g", "conf_ln_b", "sc_conv_w", "ffn_conv_w",
          "c_2", "c_ctx_2", "norm1_g_2", "norm2_g_2")


def kernel(**inputs):
    import concourse.bacc as bacc
    from concourse.bass_utils import run_bass_kernel_spmd

    nc = bacc.Bacc("TRN2", target_bir_lowering=False, num_devices=1)
    arrays = {n: np.ascontiguousarray(a) for n, a in inputs.items() if n not in PACKED}
    arrays.update(const=shape_constants(), cols=pack_cols(inputs), const2=shape_constants2(), cols2=pack_cols2(inputs),
                  cT=pack_c(inputs))
    w = {n: nc.dram_tensor(f"{n}_dram", a.shape, mybir.dt.from_np(a.dtype), kind="ExternalInput").ap()
         for n, a in arrays.items()}
    out = nc.dram_tensor("out_dram", (T, D), F32, kind="ExternalOutput").ap()
    build_program(nc, w, out)
    result = run_bass_kernel_spmd(nc, [{f"{n}_dram": a for n, a in arrays.items()}], core_ids=[0])
    return np.asarray(result.results[0]["out_dram"]).reshape(inputs["x"].shape)
```

```python
from contextlib import ExitStack

import numpy as np

import concourse.bass as bass
from concourse import mybir

F32 = mybir.dt.float32
F32R = mybir.dt.float32r
ALU = mybir.AluOpType
ACT = mybir.ActivationFunctionType
AX = mybir.AxisListType.X

P = 128
T = 256
TT = T // P
D = 1024
KC = D // P
DEPTH = 2
GW = 256
HD = 64
NH = GW // HD
CONF_K = 31
SC_K = 3
FFN_K = 3
D_FF = 2816
FFC = D_FF // P
EPS = 1e-6
SCALE = HD ** -0.5

WORK = 21600
XHAT_AT = 2526
CAT_AT = XHAT_AT + 2 * 2048
HALF = 2048
ACT_STEPS = 9
DVE_STEPS = 127
ROW_SLICES = (4, 5, 6, 7, 8)
RING = 5
UNIT = 1024
DIAG = 384

COL_MIX_PRE = 0
COL_CONF_W = COL_MIX_PRE + KC
COL_CONF_B = COL_CONF_W + 2 * CONF_K
COL_CONF_LG = COL_CONF_B + 2
COL_CONF_LB = COL_CONF_LG + 2
COL_SC_W = COL_CONF_LB + 2
COL_FFN_PRE = COL_SC_W + 2 * SC_K
COL_FFN_W = COL_FFN_PRE + KC
N_COLS = COL_FFN_W + 2 * FFC * FFN_K
N_MIXROW = D + GW

CONSTS = {}
_at = 0
for _name, _n in (("ident", P), ("ones", P), ("suffix", P), ("sb_mask", DIAG), ("sb_neg", DIAG),
                  ("ret_decay", NH * DIAG), ("ret_cos", TT * GW), ("ret_sin", TT * GW)):
    CONSTS[_name] = (_at, _n)
    _at += _n
N_CONST = _at
SPARE = 3 * P


def shape_constants():
    c = np.zeros((P, N_CONST), np.float32)

    def put(name, a):
        at, n = CONSTS[name]
        c[:, at:at + n] = np.asarray(a, np.float32).reshape(P, n)

    i = np.arange(P)
    put("ident", np.eye(P))
    put("ones", np.ones((P, P)))
    put("suffix", i[:, None] >= i[None, :])
    strict = (i[:, None] < i[None, :]).astype(np.float32)
    mask = np.concatenate([strict, np.ones((P, P)), strict], axis=1)
    put("sb_mask", mask)
    put("sb_neg", np.where(mask > 0, 0.0, -1e30))
    log_gamma = np.log1p(-np.exp2(-5.0 - np.arange(NH)))
    diff = i[None, :] - i[:, None]
    decay = []
    for h in range(NH):
        diag = np.where(diff >= 0, np.exp(np.maximum(diff, 0) * log_gamma[h]), 0.0)
        full = np.exp((diff + P) * log_gamma[h])
        decay.append(np.concatenate([diag, full, diag], axis=1) * SCALE)
    put("ret_decay", np.stack(decay, axis=1))
    inv = (np.float32(10000.0) ** (-np.arange(0, HD, 2, dtype=np.float32) / np.float32(HD))).astype(np.float32)
    pos = (i[:, None] + P * np.arange(TT)[None, :]).astype(np.float32)
    ang = (pos[:, :, None] * inv[None, None, :]).astype(np.float32)
    cos, sin = np.cos(ang), np.sin(ang)
    put("ret_cos", np.tile(np.concatenate([cos, cos], -1)[:, :, None, :], (1, 1, NH, 1)))
    put("ret_sin", np.tile(np.concatenate([-sin, sin], -1)[:, :, None, :], (1, 1, NH, 1)))
    return c


LAYER_SLOTS = [("in", s) for s in range(6)] + [("out", s) for s in range(2)]
for _m in range(5):
    LAYER_SLOTS += [("up", g) for g in ((0, 1, 2) if _m == 0 else (2 * _m + 1, 2 * _m + 2))] + [("down", _m)]
LAYER_SLOTS += [("down", 5)]
assert 2 * len(LAYER_SLOTS) % RING == 0
LAYER_ROUNDS = 2 * len(LAYER_SLOTS) // RING

MIX_UNITS = 24
UNITS = [(n, j) for n, _slot in enumerate(LAYER_SLOTS) if _slot[0] != "out" for j in range(2 if _slot == ("down", 5) else 4)]
UNIT_BUFFERS = 3
assert len(UNITS) % UNIT_BUFFERS == 0


def item_of_layer_unit(n):
    slot, j = UNITS[n]
    kind, g = LAYER_SLOTS[slot]
    if kind == "down":
        return ("D", 3) if n == len(UNITS) - 1 else None
    return ({"in": "s", "up": "U"}[kind], 2 * g + j // 2) if j % 2 else None


PASSES = [(0, 0), (0, 1), (1, 0)]
UNITS_INSIDE = sum(item_of_layer_unit(n) is None for n in range(len(UNITS)))

LAYER_BANKS = [("T", i, i) for i in range(4)]
LAYER_BANKS += [("s", i, (4 + i) % 8) for i in range(6)]
LAYER_BANKS += [("Z", h, 2 + h) for h in range(4)]
LAYER_BANKS += [("s", 6, 6), ("s", 7, 7), ("RQ", 0, 0), ("RK", 0, 1), ("s", 8, 2), ("s", 9, 3)]
LAYER_BANKS += [("RS", h, 4 + h) for h in range(4)]
LAYER_BANKS += [("s", 10, 0), ("s", 11, 1)]
LAYER_BANKS += [("I", h, 2 + h) for h in range(4)]
LAYER_BANKS += [("RO", 0, 0), ("SB", 0, 6), ("SB", 1, 7)] + [("M", i, 4 + i) for i in range(4)]
LAYER_BANKS += [("CM", 0, 1), ("CV", 0, 2), ("RT", 0, 3)]
LAYER_BANKS += [("F", i, i) for i in range(4)]
LAYER_BANKS += [("U", g, (2 * (g // 2)) % 4 + g % 2) for g in range(6)]
LAYER_BANKS += [("D", i, 4 + i) for i in range(4)]
LAYER_BANKS += [("U", g, (2 * (g // 2)) % 4 + g % 2) for g in range(6, 22)]


NHM, DQK, DV = 4, 128, 256
ST = 2 * TT
S = ST * P
NHD, DHD = 8, 64
N_EXP, TOP_K = 32, 4
CAP = 64
PAIRS = N_EXP // 2
W_IN2_COLS = dict(mq=0, mk=512, mv=1024, gates=2048, mo=2064, dq=3088, dk=4112, dv=5136, pa=6160, pb=7184)
LAM_INIT = 0.2
LIMIT, ALPHA = 7.0, 1.702

CONSTS2 = {}
_at = 0
for _name, _n in (("rope_cos", T), ("rope_sin", T), ("partner", P), ("prefix", P), ("before", P), ("iota", CAP),
                  ("pick", 2), ("spread", P)):
    CONSTS2[_name] = (_at, _n)
    _at += _n
N_CONST2 = _at


def shape_constants2():
    c = np.zeros((P, N_CONST2), np.float32)

    def put(name, a):
        at, n = CONSTS2[name]
        c[:, at:at + n] = np.asarray(a, np.float32).reshape(P, n)

    i = np.arange(P)
    d = i % DHD
    nf = DHD // 4
    inv = (np.float32(10000.0) ** (-np.arange(nf, dtype=np.float32) / np.float32(nf))).astype(np.float32)
    tok = np.arange(T)
    pos = np.where((d < DHD // 2)[:, None], (tok // 64)[None, :], (tok % 64)[None, :]).astype(np.float32)
    ang = (pos * inv[d % nf][:, None]).astype(np.float32)
    first = (d % (2 * nf)) < nf
    put("rope_cos", np.cos(ang))
    put("rope_sin", np.where(first[:, None], -np.sin(ang), np.sin(ang)))
    partner = np.where(first, i + nf, i - nf)
    put("partner", partner[:, None] == i[None, :])
    put("prefix", i[:, None] <= i[None, :])
    put("before", i[:, None] < i[None, :])
    put("iota", np.tile(np.arange(CAP), (P, 1)))
    put("pick", (i % 32)[:, None] == np.arange(2)[None, :])
    put("spread", np.tile((i % 32 == 0)[:, None], (1, P)))
    return c


B2_SLOTS = [("ada", n) for n in range(4)] + [("mq", 0), ("ada", 4), ("ada", 5), ("mk", 0), ("ada", 6), ("ada", 7)]
B2_SLOTS += [("mv", 0), ("ada", 8), ("ada", 9), ("mv", 1), ("ada", 10), ("ada", 11), ("mo", 0), ("mo", 1)]
B2_SLOTS += [(k, g) for g in (0, 1) for k in ("dv", "dq", "dk")]
B2_SLOTS += [(k, g) for g in (0, 1) for k in ("pa", "pb", "wa", "wb")]
B2_SLOTS += [("wo", 0), ("wo", 1)]

COLUMN_SLOTS = ("mq", "mk", "dq", "dk", "pa", "pb")
ROW_TILES = {"mv": 2 * TT, "mo": TT, "dv": 2 * TT}
B2_UNITS = []
for _n, (_kind, _s) in enumerate(B2_SLOTS):
    if _kind == "dq":
        B2_UNITS += [(_n + i, j) for j in range(4) for i in (0, 1)]
    elif _kind in COLUMN_SLOTS and _kind != "dk" or _kind in ROW_TILES:
        B2_UNITS += [(_n, j) for j in range(4)]


def item_of_unit(n):
    slot, j = B2_UNITS[n]
    kind, s = B2_SLOTS[slot]
    if kind in ROW_TILES:
        return (kind, ROW_TILES[kind] * (s + 1) - 1) if j == 3 else None
    if kind in ("mk", "dq", "dk"):
        return kind, 4 * s + j
    return (kind, 2 * s + j // 2) if j % 2 else None


ITEM_UNIT = {item_of_unit(n): n for n in range(len(B2_UNITS)) if item_of_unit(n)}
for _kind, _tiles in ROW_TILES.items():
    for _s in (0, 1):
        for _i in range(_tiles):
            ITEM_UNIT[_kind, _tiles * _s + _i] = ITEM_UNIT[_kind, _tiles * (_s + 1) - 1]

B2_BANKS = []
B2_BANKS += [("ada", 0, 0), ("ada", 1, 1), ("mT", 0, 2), ("ada", 2, 0), ("ada", 3, 1)]
B2_BANKS += [("XT", i, i) for i in range(4)] + [("CT", i, 4 + i) for i in range(4)]
B2_BANKS += [("mq", 0, 0), ("mq", 1, 1), ("ada", 4, 6), ("ada", 5, 7)] + [("mk", h, 2 + h) for h in range(4)]
B2_BANKS += [("mg", 0, 6), ("mR", 4, 0), ("mR", 5, 1), ("ada", 6, 2), ("ada", 7, 3)]
B2_BANKS += [("mv", i, 4 + i) for i in range(4)]
B2_BANKS += [("F", 9, 0), ("GT", 0, 1), ("GT", 1, 2), ("mT", 1, 3), ("ada", 8, 0), ("ada", 9, 1)]
B2_BANKS += [("mv", 4 + i, 4 + i) for i in range(4)]
B2_BANKS += [("ada", 10, 2), ("ada", 11, 0)] + [("mo", i, 4 + i) for i in range(4)]
B2_BANKS += [("mR", 10, 1), ("mR", 11, 2), ("MR", 0, 3)]


def _heads_banks():
    out = []
    for h in range(NHM + 1):
        if h < NHM:
            out += [("MB", h, 7), ("QK", 2 * h, 0), ("QK", 2 * h + 1, 1)]
        if h >= 1:
            out += [("H", 4 * (h - 1) + i, 2 + i) for i in range(4)]
    return out


B2_BANKS += _heads_banks()
for _g in (0, 1):
    B2_BANKS += [("dv", 4 * _g + i, i) for i in range(4)]
    if _g == 0:
        B2_BANKS += [("AT", i, 4 + i) for i in range(4)]
    B2_BANKS += [("dq", 4 * _g, 4), ("dk", 4 * _g, 5), ("rot", 4 * _g, 4)]
    for _h in range(4 * _g, 4 * _g + 4):
        B2_BANKS += [("S", 4 * _h + i, i) for i in range(4)]
        B2_BANKS += [("dq", _h + 1, 4), ("dk", _h + 1, 5)] if _h % 4 < 3 else []
        B2_BANKS += [("PT", 2 * _h, 7), ("PT", 2 * _h + 1, 6)]
        B2_BANKS += [("rot", _h + 1, 4)] if _h % 4 < 3 else []
        B2_BANKS += [("O", _h, 5)]
for _g in (0, 1):
    B2_BANKS += [("pa", 2 * _g, 4), ("pa", 2 * _g + 1, 5), ("pb", 2 * _g, 6), ("pb", 2 * _g + 1, 7)]
    B2_BANKS += [("BT", i, i) for i in range(4)] if _g == 0 else []
    B2_BANKS += [("wa", 2 * _g, 0), ("wa", 2 * _g + 1, 1), ("wb", 2 * _g, 2), ("wb", 2 * _g + 1, 3)]
B2_BANKS += [("Y", i, 4 + i) for i in range(4)]
B2_BANKS += [("R", i, i) for i in range(4)]
B2_BANKS += [("L", 0, 4), ("PC", 0, 5), ("CN", 0, 6), ("gT", 0, 7)]
B2_BANKS += [("YM", i, i) for i in range(4)]
MOE_BANKS = [("G", 0, 4), ("G", 1, 5), ("GLU", 0, 6), ("LIN", 0, 7), ("GLU", 1, 4), ("LIN", 1, 5),
             ("ST", 0, 6), ("AT2", 0, 7), ("OUT", 0, 4), ("OUT", 1, 5), ("AT2", 1, 6)]
PAIR_SLOTS = [("w1", x, q) for q in range(4) for x in (0, 1)] + [("w2", x, q) for q in range(2) for x in (0, 1)]
PAIR_RING = (5, 6, 7, 8, 9, 10, 11, 3, 4, 0, 1, 2)


def bank_rounds(items):
    used, where = [0] * 8, {}
    for kind, i, b in items:
        where[kind, i] = (b, used[b])
        used[b] += 1
    return where, used


LAYER_WHERE, LAYER_FILLS = bank_rounds(LAYER_BANKS)
B2_WHERE, B2_FILLS = bank_rounds(B2_BANKS)
MOE_WHERE, MOE_FILLS = bank_rounds(MOE_BANKS)


def earlier_fills(key, l):
    if key in MOE_WHERE:
        b, n = MOE_WHERE[key]
        return b, l * MOE_FILLS[b] + (DEPTH * LAYER_FILLS[b] + B2_FILLS[b] + n)
    if key in B2_WHERE:
        b, n = B2_WHERE[key]
        return b, DEPTH * LAYER_FILLS[b] + n
    b, n = LAYER_WHERE[key]
    return b, l * LAYER_FILLS[b] + n


def build_program(nc, w, out):
    with ExitStack() as ctx:
        def sb(name, n, p=P):
            return ctx.enter_context(nc.sbuf_tensor(name, [p, n], F32))

        def sem(name):
            return ctx.enter_context(nc.semaphore(name))

        psum = ctx.enter_context(nc.psum_tensor("psum", [P, 8, 512], F32))
        with (nc.sbuf_tensor("split_weights", [P, UNIT_BUFFERS * 2 * UNIT + 2 * KC * 16], F32R) as split_w,
              nc.sbuf_tensor("split_rows", [P, 2 * (KC + 8) * T], F32R) as split_x):
            pass
        late = sb("late", UNIT_BUFFERS * 2 * UNIT + 2 * KC * 16 + 2 * (KC + 8) * T)
        ring = sb("ring", RING * HALF)
        const = sb("const", N_CONST)
        x_row = sb("x_row", TT * D)
        stats = sb("stats", 64)
        work = sb("work", WORK)
        offset = [0]

        def part(n, *shape):
            at = offset[0]
            offset[0] += n
            assert offset[0] <= WORK, offset
            v = work[:, at:at + n]
            if shape:
                names = "abcd"[:len(shape)]
                v = v.rearrange(f"p ({' '.join(names)}) -> p {' '.join(names)}", **dict(zip(names, shape)))
            return v

        def cst(name):
            at, n = CONSTS[name]
            return const[:, at:at + n]

        ident, ones, suffix = cst("ident"), cst("ones"), cst("suffix")
        sb_mask4 = cst("sb_mask").unsqueeze(1).broadcast_to([P, NH, DIAG])
        sb_neg4 = cst("sb_neg").unsqueeze(1).broadcast_to([P, NH, DIAG])
        ret_decay = cst("ret_decay").rearrange("p (h n) -> p h n", h=NH)
        x = x_row[:, :].rearrange("p (t d) -> p t d", t=TT)
        sumsq, rms, rinv = stats[:, 0:2], stats[:, 2:4], stats[:, 4:6]
        ret_mu, ret_var, ret_std, ret_rinv = (stats[:, 8 + 8 * i:16 + 8 * i] for i in range(4))

        cols = part(N_COLS + N_COLS % 2)
        mix_row = part(N_MIXROW)
        ffn_row = part(D)
        assert offset[0] == XHAT_AT
        xhat = part(TT * D, TT, D)
        part(CAT_AT - XHAT_AT - TT * D)
        assert offset[0] == CAT_AT
        catT = part(KC * T, KC, T)
        q_z = part(NH * T, NH, T)
        rq_z = part(NH * T, NH, T)
        conf_pad = part(2 * (T + 30), 2, T + 30)
        sc_pad = part(2 * (T + 2), 2, T + 2)
        branch_at = offset[0]
        kT = part(2 * T, 2, T)
        v_sb = part(TT * GW, TT, GW)
        z = part(NH * DIAG, NH, DIAG)
        soft = part(NH * DIAG, NH, DIAG)
        rq = part(TT * GW, TT, GW)
        rk = part(TT * GW, TT, GW)
        swapped = part(TT * GW)
        rkT = part(2 * T, 2, T)
        rv = part(TT * GW, TT, GW)
        rg = part(TT * GW, TT, GW)
        conf_gate = part(2 * T, 2, T)
        conf = part(2 * T, 2, T)
        conf_sq = part(2 * T, 2, T)
        sc_b = part(2 * T, 2, T)
        sc_c = part(2 * T, 2, T)
        r_scores = xhat.rearrange("p t d -> p (t d)")[:, 0:NH * DIAG].rearrange("p (h n) -> p h n", h=NH)
        ret = conf_sq
        offset[0] = branch_at
        taps = part(2 * 4 * T, 2, 4, T)
        hT_split = split_x[:, 0:2 * KC * T].rearrange("p (s k t) -> p s k t", s=2, k=KC)
        ffT_split = split_x[:, 2 * KC * T:].rearrange("p (s k t) -> p s k t", s=2, k=8)

        extra_at = [CAT_AT + 1024]

        def extra(n, *shape):
            at = extra_at[0]
            extra_at[0] += n
            assert extra_at[0] <= CAT_AT + 1024 + 4096
            return shaped(work[:, at:at + n], shape)

        def shaped(v, shape):
            if not shape:
                return v
            names = "abcd"[:len(shape)]
            return v.rearrange(f"p ({' '.join(names)}) -> p {' '.join(names)}", **dict(zip(names, shape)))

        def at(start, n, *shape):
            assert start + n <= WORK
            return shaped(work[:, start:start + n], shape)

        ctx_row = extra(TT * D, TT, D)
        const2 = extra(N_CONST2)
        cols2 = extra(2 * KC + 4 * KC)
        gate_w = extra(KC * 16, KC, 16)
        gate_b = extra(16)
        lam_row = extra(4 * DHD, 4, DHD)
        router_b = extra(N_EXP)

        def cst2(name):
            a, n = CONSTS2[name]
            return const2[:, a:a + n]

        flatten = lambda v: v.rearrange("p a b -> p (a b)")
        low, mid = 0, XHAT_AT + TT * D
        ada_rows = at(CAT_AT, 1024, 2, 512)
        uT_split = split_x[:, :].rearrange("p (s k t) -> p s k t", s=2, k=KC)
        u_rows = at(low, 4 * 512, 4, 512)
        gate_w_split = split_w[:, UNIT_BUFFERS * 2 * UNIT:].rearrange("p (s k n) -> p s k n", s=2, k=KC)
        high = CAT_AT + 1024 + 4096
        g_rows = at(WORK - 2048, 2048, 2, D)
        top = WORK - 2048
        m_v = at(high, ST * NHM * 258, ST, NHM, 258)
        m_kT = at(high + 4128, NHM * S, NHM, S)
        m_qT = at(high + 6176, NHM * T, NHM, T)
        cummax = [[const[0:NHM, SPARE + 384 * (2 * d + i):SPARE + 384 * (2 * d + i + 1)] for i in (0, 1)] for d in (0, 1)]
        assert high + 7200 <= top and high + 7680 <= top and branch_at + FFC * T + 2048 <= top
        o_row = at(mid, TT * D, TT, D)
        decay = [at(low, 2 * ST * T, 2, ST * T), at(XHAT_AT, 2 * ST * T, 2, ST * T)]
        h_row = ctx_row
        norm_row = at(CAT_AT, D)
        a_outT = at(mid, KC * T, KC, T)
        d_kT = at(high, 4 * S, 4, S)
        d_v = at(high + 2048, ST * 512, ST, 512)
        d_q = at(high + 4096, 8 * T, 8, T)
        raw = at(high + 6144, 1024, 2, 512)
        turned = at(high + 7168, 512)
        aT = shaped(const[:, SPARE + 1536:SPARE + 2560], (2, 512))
        probs = at(low, 2048, 2, 2, S)
        b_row = xhat
        squares = at(low, 2 * D)
        b_outT = at(high, KC * T, KC, T)
        gate_a, gate_bb = at(low, 1024), at(low + 1024, 1024)
        yT = at(high + 2048, KC * T, KC, T)
        b1_rows = at(high + 4096, 2 * D)
        b2_rows = at(high + 6144, D)
        router_w = at(high + 7168, KC * N_EXP, KC, N_EXP)
        final_row = const[:, SPARE + 1536:SPARE + 2560]
        u2T = at(CAT_AT + 1024, KC * T, KC, T)
        xgT = at(mid, KC * P, KC, P)
        pick = at(mid + 1024, TT * P, TT, P)
        pick_gated = at(mid + 1280, TT * P, TT, P)
        spread_T = at(mid + 1536, T)
        assert mid + 1792 <= CAT_AT + 1024
        glu, sig, lin, act_ = ([at(CAT_AT + 1024 + 512 * (4 * e + i), 512) for e in (0, 1)] for i in range(4))
        actT = at(low, KC * P, KC, P)
        pick_e = at(low + 1024, P)
        gT = at(low + 1152, T)
        out_sb = at(high, D)
        router_at = [SPARE]

        def routed(n, *shape):
            a = router_at[0]
            router_at[0] += n
            assert router_at[0] <= SPARE + 1536
            return shaped(const[:, a:a + n], shape)

        n_wide = N_EXP + 4
        logits, others, exps = (routed(TT * n_wide, TT, n_wide) for _ in range(3))
        top8 = routed(TT * 8, TT, 8)
        neg_top, gate_sum, gate_inv = routed(TT), routed(TT), routed(TT)
        chosen, gate_row = routed(TT * N_EXP, TT, N_EXP), routed(TT * N_EXP, TT, N_EXP)
        pair_gate, pair_slot = routed(TT * N_EXP), routed(TT * N_EXP)
        most, n_pass = routed(1), routed(1)
        passes = ctx.enter_context(nc.sbuf_tensor("passes", [P, 1], mybir.dt.int32))

        small = sb("small", 944)
        small_at = [0]

        def tiny(n, *shape):
            a = small_at[0]
            small_at[0] += n
            assert small_at[0] <= 944
            return shaped(small[:, a:a + n], shape)

        modT = tiny(64, 32, 2)
        scale1, shift1 = tiny(16, 2, KC), tiny(16, 2, KC)
        scale2 = tiny(KC)
        gates = tiny(64, ST, 16)
        f_neg, f_abs, f_min, log_f = (tiny(32, ST * 2, 4) for _ in range(4))
        g_sub = tiny(32, ST, 8)
        ctx_max = tiny(2)
        m_neg = tiny(16)
        den, den2 = tiny(16), tiny(16)
        h_sq, h_rms, h_inv = tiny(8), tiny(8), tiny(8)
        lam_prod = tiny(128, 2, DHD)
        lam_sum, lam_exp, neg_lam = tiny(2), tiny(2), tiny(1)
        row_max, neg_max, row_sum, row_inv, map_scale = (tiny(4, 2, 2) for _ in range(5))
        b_sq, b_rms, b_inv = tiny(16), tiny(16), tiny(16)
        iota = tiny(CAP)
        cT = tiny(2 * KC, KC, 2)
        siluc = tiny(KC * 32, KC, 32)

        filled = [sem(f"bank{b}_filled") for b in range(8)]
        evacuated = [sem(f"bank{b}_evacuated") for b in range(8)]
        half_loaded = [sem(f"half_slot{s}_loaded") for s in range(12)]
        hT_high_ready, w_high_ready, w_split, unit_used, product_ready, ff_high_ready, c_loaded = (
            sem(n) for n in ("hT_high_ready", "weights_high_ready", "weights_split", "unit_used", "ff_product_ready",
                             "ff_high_ready", "c_loaded"))
        slot_free = sem("slot_free")
        const_loaded, x_loaded, mix_par_loaded, ffn_par_loaded = (
            sem(n) for n in ("const_loaded", "x_loaded", "mix_par_loaded", "ffn_par_loaded"))
        zeros_ready, tables_loaded = sem("zeros_ready"), sem("tables_loaded")
        x_ready = sem("x_ready")
        act_step, dve_step = sem("act_step"), sem("dve_step")
        rms_ready, xhat_tile_ready, xhat_ready = (sem(n) for n in ("rms_ready", "xhat_tile_ready", "xhat_ready"))
        x_tile_ready, head_rms_ready = sem("x_tile_ready"), sem("head_rms_ready")
        sb_abs, sb_log, sb_soft, sb_arg, sb_attn = (
            sem(n) for n in ("sb_abs_ready", "sb_log_ready", "sb_soft_ready", "sb_arg_ready", "sb_attn_ready"))
        rq_ready, rk_ready, ret_var_ready, ret_std_ready, ret_ready = (
            sem(n) for n in ("rq_ready", "rk_ready", "ret_var_ready", "ret_std_ready", "ret_ready"))
        conf_ready, conf_sq_ready, conf_normed, conf_cat = (
            sem(n) for n in ("conf_conv_ready", "conf_sq_ready", "conf_normed", "conf_cat_ready"))
        sc_cat = sem("sc_cat_ready")
        tap_ready, silu_ready, ff_ready = (sem(n) for n in ("first_tap_ready", "silu_ready", "ff_ready"))
        out_stored = sem("out_stored")
        names = ("early_loaded ctx_loaded g_bias_loaded norm_row_loaded late_loaded siluc_ready scale1_ready ctx_hat_ready "
                 "gate_abs_ready gate_log_ready gate_ready cummax_ready m_neg_ready decay_exp_ready "
                 "h_ready h_normed lam_sum_ready lam_exp_ready qk_ready row_max_ready "
                 "attn_ready b_normed y_ready").split()
        (early_loaded, ctx_loaded, g_bias_loaded, norm_row_loaded, late_loaded, siluc_ready, scale1_ready, ctx_hat_ready,
         gate_abs_ready, gate_log_ready, gate_ready, cummax_ready, m_neg_ready, decay_exp_ready,
         h_ready, h_normed, lam_sum_ready, lam_exp_ready, qk_ready, row_max_ready,
         attn_ready, b_normed, y_ready) = (sem(n) for n in names)
        pairs_step, mask_ready, exp_ready, gates_ready, passes_ready = (
            sem(n) for n in ("pairs_step", "chosen_ready", "exp_ready", "expert_gates_ready", "passes_ready"))
        b1_zeroed, picks_ready, sig_ready, hidden_ready, combined, out_ready = (
            sem(n) for n in ("b1_rows_zeroed", "picks_ready", "glu_sigmoid_ready", "hidden_ready", "pair_combined",
                             "out_ready"))
        expert_slot_free, expert_load_claimed = sem("expert_slot_free"), sem("expert_load_claimed")
        L2 = DEPTH
        half_rounds = [DEPTH * LAYER_ROUNDS + len(range(s, 2 * len(B2_SLOTS), RING)) for s in range(RING)] + [0] * 7
        u_high_ready, u_ready, gate_w_high, gate_w_ready = (
            sem(n) for n in ("u_high_ready", "u_ready", "gate_weights_high_ready", "gate_weights_split"))

        def bank_of(key):
            return earlier_fills(key, 0)[0]

        def fill(pe, key, l):
            b, n = earlier_fills(key, l)
            pe.wait_ge(evacuated[b], n + 1)
            return psum[:, b, :]

        def take(eng, key, l):
            b, n = earlier_fills(key, l)
            eng.wait_ge(filled[b], n + 1)
            return psum[:, b, :]

        def after_evacuation(eng, key, l):
            b, n = earlier_fills(key, l)
            eng.wait_ge(evacuated[b], n + 2)

        def half_place(s):
            return ring[:, s * HALF:(s + 1) * HALF] if s < RING else late[:, (s - RING) * HALF:(s - RING + 1) * HALF]

        def half_ready(eng, h, l):
            eng.wait_ge(half_loaded[h % RING], 16 * (l * LAYER_ROUNDS + (h // RING + 1)))
            return half_place(h % RING)

        def slot_ready(pe, n, l, n_k):
            halves = [half_ready(pe, 2 * n + h, l).rearrange("p (k n) -> p k n", k=n_k // 2) for h in (0, 1)]
            return lambda k, c0, c1: halves[k // (n_k // 2)][:, k % (n_k // 2), c0:c1]

        def after_unit(eng, n, l):
            item = item_of_layer_unit(n)
            if item:
                take(eng, item, l)
            else:
                eng.wait_ge(unit_used, l * UNITS_INSIDE + sum(item_of_layer_unit(i) is None for i in range(n + 1)))

        def unit_weights(n, v):
            slot, j = UNITS[n]
            kind, g = LAYER_SLOTS[slot]
            rows = kind == "in" and 2 * g + j // 2 in ROW_SLICES
            n_k = 1 if kind == "down" else 4 if rows else KC
            if v is not None:
                at = (2 * (n % UNIT_BUFFERS) + v) * UNIT
                return split_w[:, at:at + UNIT].rearrange("p (k n) -> p k n", k=n_k)
            n_units = sum(s == slot for s, _ in UNITS)
            h = 2 * slot + j // (n_units // 2)
            raw = half_place(h % RING)
            if n_k == KC:
                return raw.rearrange("p (k n) -> p k n", k=KC)[:, :, (j % 2) * P:(j % 2 + 1) * P], h
            at = j % (n_units // 2) * UNIT
            return raw[:, at:at + UNIT].rearrange("p (k n) -> p k n", k=n_k), h

        def after_unit2(eng, n):
            item = item_of_unit(n)
            if item:
                take(eng, item, L2)
            else:
                eng.wait_ge(unit_used, DEPTH * UNITS_INSIDE + sum(item_of_unit(i) is None for i in range(n + 1)))

        def unit_half2(n):
            slot, j = B2_UNITS[n]
            return 2 * slot + j // 2

        def unit_weights2(n, v):
            slot, j = B2_UNITS[n]
            columns = B2_SLOTS[slot][0] in COLUMN_SLOTS
            if v is not None:
                at_ = (2 * (n % UNIT_BUFFERS) + v) * UNIT
                return split_w[:, at_:at_ + UNIT].rearrange("p (k n) -> p k n", k=KC if columns else 2)
            raw = half_place(unit_half2(n) % RING)
            if columns:
                return raw.rearrange("p (k n) -> p k n", k=KC)[:, :, (j % 2) * P:(j % 2 + 1) * P]
            return raw.rearrange("p (k n) -> p k n", k=4)[:, 2 * (j % 2):2 * (j % 2) + 2, :]

        def units_ahead(split, units):
            n_split = [0]

            def until(n):
                while n_split[0] <= min(n, len(units) - 1):
                    split(n_split[0])
                    n_split[0] += 1

            return until

        def next_units(h):
            return ITEM_UNIT["dk", h + 1] if h % 4 < 3 else ITEM_UNIT["dk", h] + UNIT_BUFFERS

        def unit2(kind, s, j):
            return B2_UNITS.index((B2_SLOTS.index((kind, s)), j))

        block = ctx.enter_context(nc.Block())

        def slot_used(eng, l, n):
            kind, s = B2_SLOTS[n] if l == L2 else LAYER_SLOTS[n]
            last_item = {"ada": s, "wa": 2 * s + 1, "wb": 2 * s + 1}
            if kind in last_item:
                take(eng, (kind, last_item[kind]), l)
            elif kind == "wo":
                take(eng, ("Y", 3), l)
            elif (kind, s) == ("out", 1):
                take(eng, ("M", 3), l)
            else:
                eng.wait_ge(slot_free, l + 1)

        def half_used(eng, l, h):
            n = h // 2
            if l == L2 and h in [unit_half2(i) for i in range(len(B2_UNITS))]:
                last = max(i for i in range(len(B2_UNITS)) if unit_half2(i) == h)
                eng.wait_ge(w_split, DEPTH * len(UNITS) + last + 1)
            elif l == L2 or LAYER_SLOTS[n][0] == "out":
                slot_used(eng, l, n)
            else:
                units = [i for i in range(len(UNITS)) if unit_weights(i, None)[1] == h]
                eng.wait_ge(w_split, l * len(UNITS) + units[-1] + 1)

        def last_unit(kind, g):
            return max(n for n, (slot, _) in enumerate(UNITS) if LAYER_SLOTS[slot] == (kind, g))

        def ffn_stages(split, convolve, finish):
            n, pending, whole = MIX_UNITS, None, None
            for slot in range(8, len(LAYER_SLOTS)):
                kind, g = LAYER_SLOTS[slot]
                for i in range(sum(s_ == slot for s_, _ in UNITS)):
                    split(n)
                    n += 1
                    if i == 0 and whole is not None:
                        finish(whole)
                        whole = None
                    if i in (1, 3) and pending is not None:
                        convolve(pending, i // 2)
                        if i == 3:
                            pending, whole = None, pending
                if kind == "up":
                    assert pending is None
                    pending = g

        def expert_slot(pe, it, n, n_k):
            halves = []
            for h in (0, 1):
                s = PAIR_RING[(2 * n + h) % 12]
                pe.wait_ge(half_loaded[s], 16 * (2 * it) + 16 * (half_rounds[s] + n // 6 + 1))
                halves.append(half_place(s).rearrange("p (k n) -> p k n", k=n_k // 2))
            return lambda k, c0, c1: halves[k // (n_k // 2)][:, k % (n_k // 2), c0:c1]

        def over_pairs(eng, pair):
            with eng.Fori(0, PAIRS) as j:
                pair(j, j)
            eng.wait_ge(passes_ready, 1)
            n = eng.value_load(passes[0:1, 0:1], min_val=1, max_val=T // CAP)
            with eng.If(n > 1), eng.Fori(1, n) as r:
                with eng.Fori(0, PAIRS) as j:
                    pair(r * PAIRS + j, j)
            return n

        def load_mixer_parameters(eng, l):
            eng.dma_start(cols[:, 0:COL_FFN_PRE], w["cols"][l][:, 0:COL_FFN_PRE]).then_inc(mix_par_loaded, 16)
            eng.dma_start(mix_row[:, 0:D], w["norm_mix_post"][l:l + 1, :].partition_broadcast(P)).then_inc(mix_par_loaded, 16)
            eng.dma_start(mix_row[:, D:], w["ret_norm_g"][l:l + 1, :].partition_broadcast(P)).then_inc(mix_par_loaded, 16)

        def load_ffn_parameters(eng, l):
            eng.dma_start(cols[:, COL_FFN_PRE:N_COLS], w["cols"][l][:, COL_FFN_PRE:N_COLS]).then_inc(ffn_par_loaded, 16)
            eng.dma_start(ffn_row, w["norm_ffn_post"][l:l + 1, :].partition_broadcast(P)).then_inc(ffn_par_loaded, 16)

        def loop_layers(eng, layer):
            with eng.Fori(0, DEPTH) as l:
                layer(l)

        @block.sync
        def _(sp):
            def load_slot(l, n):
                kind, s = B2_SLOTS[n] if l == L2 else LAYER_SLOTS[n]
                chunks = lambda a: a.rearrange("(k p) n -> p k n", p=P)
                if kind == "up":
                    src = chunks(w["ffn_up"][l])
                    two = [src[:, :, u * D_FF + s * 256:u * D_FF + (s + 1) * 256] for u in (0, 1)]
                elif kind in ("out", "down", "wo"):
                    src = chunks({"out": w["w_out"], "down": w["ffn_down"], "wo": w["w_out_2"]}[kind][l % L2])
                    half = min(4, src.shape[1] - 4 * s) // 2
                    two = [src[:, 4 * s + h * half:4 * s + (h + 1) * half, :] for h in (0, 1)]
                else:
                    name, c0 = {"in": ("w_in", 0), "ada": ("ada_w_2", 0), "wa": ("w_branch_a_2", 0),
                                "wb": ("w_branch_b_2", 0)}.get(kind) or ("w_in_2", W_IN2_COLS[kind])
                    c0 += 512 * s
                    src = chunks(w[name][l % L2])
                    two = ([src[:, :, c0 + h * 256:c0 + (h + 1) * 256] for h in (0, 1)] if kind in COLUMN_SLOTS + ("in",) else
                           [src[:, h * 4:h * 4 + 4, c0:c0 + 512] for h in (0, 1)])
                for h in (0, 1):
                    g = 2 * n + h
                    place = g % RING
                    if g >= RING:
                        half_used(sp, l, g - RING)
                    elif l:
                        half_used(sp, l - 1, 2 * len(LAYER_SLOTS) - RING + g)
                    n_k, n_col = two[h].shape[1:]
                    sp.dma_start(half_place(place)[:, 0:n_k * n_col].rearrange("p (k n) -> p k n", k=n_k), two[h]
                                 ).then_inc(half_loaded[place], 16)

            sp.dma_start(x, w["x"].rearrange("b (t p) d -> p (b t) d", p=P)).then_inc(x_loaded, 16)
            for l in range(DEPTH):
                for n in range(len(LAYER_SLOTS)):
                    load_slot(l, n)
                    if n == 13 and l + 1 < DEPTH:
                        sp.wait_ge(x_ready, 2 * l + 2)
                        load_mixer_parameters(sp, l + 1)
                    if n == RING and l:
                        sp.wait_ge(x_ready, 2 * l + 1)
                        load_ffn_parameters(sp, l)
            for n in range(len(B2_SLOTS)):
                load_slot(L2, n)

            def pair(it, j):
                for n, (kind, xx, q) in enumerate(PAIR_SLOTS):
                    n_k = 1 if kind == "w1" else 2
                    src = w["exp_w1_2" if kind == "w1" else "exp_w2_2"][0, 2 * j + xx].rearrange("(k p) n -> p k n", p=P)
                    for h in (0, 1):
                        s = PAIR_RING[(2 * n + h) % 12]
                        if h == 0:
                            sp.wait_ge(expert_slot_free, 12 * it + (n + 1))
                            sp.sem_inc(expert_load_claimed, 1)
                        k0 = n_k * (2 * q + h)
                        sp.dma_start(half_place(s).rearrange("p (k n) -> p k n", k=n_k), src[:, k0:k0 + n_k, :]
                                     ).then_inc(half_loaded[s], 16)

            over_pairs(sp, pair)
            for t in range(TT):
                sp.wait_ge(out_ready, t + 1)
                sp.dma_start(out[t * P:(t + 1) * P, :], xhat[:, t, :]).then_inc(out_stored, 16)
            sp.wait_ge(out_stored, 32)

        @block.gpsimd
        def _(pool):
            nc.gpsimd.memset(flatten(siluc), 0.0).then_inc(zeros_ready, 1)
            for v in (conf_pad[:, :, 0:30], sc_pad[:, :, 0:2]):
                nc.gpsimd.memset(v, 0.0).then_inc(zeros_ready, 1)
            pool.wait_ge(x_ready, 2 * DEPTH)
            for dst, src in ((gate_w, w["w_in_2"][0].rearrange("(k p) n -> p k n", p=P)[:, :, 2048:2064]),
                             (const2, w["const2"]), (cols2, w["cols2"]),
                             (gate_b, w["mlstm_gate_b_2"].partition_broadcast(P)),
                             (flatten(lam_row), w["diff_lambda_2"].rearrange("l a b -> l (a b)").partition_broadcast(P)),
                             (router_b, w["router_b_2"].partition_broadcast(P))):
                pool.dma_start(dst, src).then_inc(early_loaded, 16)
            pool.dma_start(ctx_row, w["ctx_2"].rearrange("b (t p) d -> p (b t) d", p=P)).then_inc(ctx_loaded, 16)
            for i, c0 in enumerate((2 * D, 5 * D)):
                pool.dma_start(g_rows[:, i, :], w["ada_b_2"][:, c0:c0 + D].partition_broadcast(P)).then_inc(g_bias_loaded, 16)
            take(pool, ("mR", 11), L2)
            pool.dma_start(norm_row, w["mlstm_norm_g_2"].rearrange("l a b -> l (a b)").partition_broadcast(P)
                           ).then_inc(norm_row_loaded, 16)
            pool.wait_ge(h_normed, 1)
            pool.dma_start(norm_row, w["diff_norm_g_2"].rearrange("l a b -> l (a b)").partition_broadcast(P)
                           ).then_inc(norm_row_loaded, 16)
            take(pool, ("O", NHD - 1), L2)
            nc.gpsimd.memset(b1_rows, 0.0).then_inc(b1_zeroed, 1)
            pool.wait_ge(b1_zeroed, 1)
            for dst, src in ((b1_rows[0:N_EXP, :], w["exp_b1_2"][0]), (b2_rows[0:N_EXP, :], w["exp_b2_2"][0]),
                             (router_w, w["router_w_2"][0].rearrange("(k p) e -> p k e", p=P)),
                             (final_row, w["final_norm_g_2"].partition_broadcast(P))):
                pool.dma_start(dst, src).then_inc(late_loaded, 16)

        @block.scalar
        def _(act):
            n_step = [0]

            def step(ins, l):
                n_step[0] += 1
                ins.then_inc(act_step, 1)
                act.wait_ge(act_step, l * ACT_STEPS + n_step[0])

            def flat(v):
                return v.rearrange("p a b -> p (a b)")

            def rms_of(rows, l, before, squares_out=xhat):
                for t in range(TT):
                    before(t)
                    step(nc.scalar.activation(squares_out[:, t, :], rows[t], ACT.Square, accum_out=sumsq[:, t:t + 1]), l)
                    nc.scalar.activation(rms[:, t:t + 1], sumsq[:, t:t + 1], ACT.Sqrt, bias=EPS, scale=1.0 / D
                                         ).then_inc(rms_ready, 1)

            def rms_of_x(l, n):
                rms_of([x[:, t, :] for t in range(TT)], l, lambda t: act.wait_ge(x_ready if t else x_tile_ready, n))

            def rms_of_banks(l, key):
                rms_of([psum[:, 4 + 2 * t:6 + 2 * t, :].rearrange("p b n -> p (b n)") for t in range(TT)], l,
                       lambda t: [take(act, (key, 2 * t + i), l) for i in (0, 1)])

            def evac(key, l, out_, in_, func=ACT.Copy, **kw):
                nc.scalar.activation(out_, in_, func, **kw).then_inc(evacuated[bank_of(key)], 1)

            def high_rows(key, l, n, col):
                for i in range(4):
                    b = take(act, (key, i), l)
                    for c in (0, 1):
                        k = 2 * i + c
                        ins = nc.scalar.activation(hT_split[:, 0, k, :], b[:, c * T:(c + 1) * T], ACT.Copy,
                                                   scale=cols[:, col + k:col + k + 1])
                    ins.then_inc(hT_high_ready, 1)

            def halves(key, l, dst, scale):
                b = take(act, key, l).rearrange("p (c t) -> p c t", c=2)
                nc.scalar.activation(dst[0:64, 0:NH:2, :], b[0:64], ACT.Copy, scale=scale)
                evac(key, l, dst[64:128, 1:NH:2, :], b[64:128], scale=scale)

            def layer(l):
                n_step[0] = 0
                def split(n):
                    if n >= UNIT_BUFFERS:
                        after_unit(act, n - UNIT_BUFFERS, l)
                    raw, h = unit_weights(n, None)
                    half_ready(act, h, l)
                    nc.scalar.activation(unit_weights(n, 0), raw, ACT.Copy).then_inc(w_high_ready, 1)

                split_until = units_ahead(split, UNITS)
                rms_of_x(l, 2 * l + 1)
                split_until(UNIT_BUFFERS - 1)
                act.wait_ge(mix_par_loaded, 48 * l + 48)
                high_rows("T", l, 0, COL_MIX_PRE)

                split_until(5)
                evac(("s", 1), l, flat(conf_gate), take(act, ("s", 1), l), ACT.Sigmoid)
                split_until(7)
                halves(("s", 2), l, q_z, SCALE)
                split_until(9)
                evac(("s", 3), l, flat(kT), take(act, ("s", 3), l))
                split_until(11)
                evac(("s", 4), l, flat(v_sb), take(act, ("s", 4), l))
                split_until(13)
                for h in range(NH):
                    evac(("Z", h), l, z[:, h, :], take(act, ("Z", h), l)[:, 0:DIAG])
                split_until(17)
                evac(("s", 7), l, flat(rv), take(act, ("s", 7), l))
                act.wait_ge(sb_abs, l + 1)
                step(nc.scalar.activation(soft, soft, ACT.Exp, scale=-1.0), l)
                nc.scalar.activation(soft, soft, ACT.Ln, bias=1.0).then_inc(sb_log, 1)
                split_until(18)
                halves(("RQ", 0), l, rq_z, 1.0)
                evac(("RK", 0), l, flat(rkT), take(act, ("RK", 0), l))
                split_until(19)
                evac(("s", 8), l, flat(rg), take(act, ("s", 8), l), ACT.Silu)
                split_until(21)
                evac(("s", 9), l, flat(sc_b), take(act, ("s", 9), l))
                split_until(23)
                evac(("s", 10), l, flat(sc_c), take(act, ("s", 10), l))
                act.wait_ge(sb_arg, l + 1)
                nc.scalar.activation(z, z, ACT.Exp).then_inc(sb_attn, 1)
                for c in (0, 1):
                    evac(("SB", c), l, catT[:, 2 + c, :], take(act, ("SB", c), l)[:, 0:T])
                after_evacuation(act, ("CM", 0), l)
                nc.scalar.activation(conf_sq, conf, ACT.Square).then_inc(conf_sq_ready, 1)
                evac(("CV", 0), l, conf_gate[:, 0, :], take(act, ("CV", 0), l)[:, 0:T], ACT.Sqrt,
                     bias=EPS, scale=1.0 / GW)
                act.wait_ge(ret_var_ready, l + 1)
                nc.scalar.activation(ret_std, ret_var, ACT.Sqrt, bias=EPS, scale=1.0 / HD).then_inc(ret_std_ready, 1)
                act.wait_ge(conf_normed, l + 1)
                for c in (0, 1):
                    ins = nc.scalar.activation(catT[:, c, :], conf[:, c, :], ACT.Silu,
                                               bias=cols[:, COL_CONF_LB + c:COL_CONF_LB + c + 1],
                                               scale=cols[:, COL_CONF_LG + c:COL_CONF_LG + c + 1])
                ins.then_inc(conf_cat, 1)
                evac(("RT", 0), l, flat(catT[:, 4:6, :]), take(act, ("RT", 0), l))
                split_until(MIX_UNITS + UNIT_BUFFERS - 1)
                rms_of_banks(l, "M")
                rms_of_x(l, 2 * l + 2)
                act.wait_ge(ffn_par_loaded, 32 * l + 32)
                high_rows("F", l, 4, COL_FFN_PRE)

                def first_tap(g, u):
                    if g >= 2 and u == 0:
                        act.wait_ge(ff_ready, l * 11 + (g - 1))
                    b = take(act, ("U", 2 * g + u), l)
                    for c in (0, 1):
                        at = COL_FFN_W + (2 * FFC) * 2 + u * FFC + 2 * g + c
                        ins = nc.scalar.activation(taps[:, g % 2, 2 * u + c, :], b[:, c * T:(c + 1) * T],
                                                   ACT.Copy, scale=cols[:, at:at + 1])
                    ins.then_inc(tap_ready, 1)
                    if u == 1:
                        after_evacuation(act, ("U", 2 * g), l)
                        nc.scalar.activation(taps[:, g % 2, 0:2, :], taps[:, g % 2, 0:2, :], ACT.Silu).then_inc(silu_ready, 1)

                def high_part(g):
                    act.wait_ge(product_ready, l * 11 + (g + 1))
                    if g >= 4:
                        after_unit(act, last_unit("down", (g - 4) // 2), l)
                    nc.scalar.activation(ffT_split[:, 0, 2 * (g % 4):2 * (g % 4) + 2, :], taps[:, g % 2, 0:2, :], ACT.Copy
                                         ).then_inc(ff_high_ready, 1)

                ffn_stages(split_until, first_tap, high_part)
                rms_of_banks(l, "D")
                assert n_step[0] == ACT_STEPS, n_step

            def second():
                n_step[0] = 0
                l = L2
                act.wait_ge(c_loaded, 16)
                act.wait_ge(zeros_ready, 4)
                nc.scalar.activation(siluc[:, :, 0:2], cT, ACT.Silu).then_inc(siluc_ready, 1)
                def split(n):
                    if n >= UNIT_BUFFERS:
                        after_unit2(act, n - UNIT_BUFFERS)
                    half_ready(act, unit_half2(n), l)
                    nc.scalar.activation(unit_weights2(n, 0), unit_weights2(n, None), ACT.Copy).then_inc(w_high_ready, 1)

                split_until = units_ahead(split, B2_UNITS)

                def projected(key):
                    split_until(ITEM_UNIT[key] + 2)
                    return take(act, key, l)

                rms_of_x(l, 2 * L2 + 1)
                act.wait_ge(early_loaded, 96)
                nc.scalar.activation(gate_w_split[:, 0], gate_w, ACT.Copy).then_inc(gate_w_high, 1)
                def ada_rows_out(*ns):
                    for n in ns:
                        evac(("ada", n), l, ada_rows[:, n % 2, :], take(act, ("ada", n), l))

                act.wait_ge(ctx_loaded, 16)
                act.wait_ge(xhat_ready, 2 * L2 + 1)
                rms_of([ctx_row[:, t, :] for t in range(TT)], l, lambda t: None, flatten(u_rows).rearrange("p (t d) -> p t d", t=TT))
                ada_rows_out(0, 1, 2, 3)
                act.wait_ge(scale1_ready, 1)
                split_until(UNIT_BUFFERS - 1)
                for q in range(8):
                    key, v, t0, i = ("XT", 0, T, q) if q < 4 else ("CT", 1, 0, q - 4)
                    if i % 2 == 0:
                        b = take(act, (key, i), l)
                        if q >= 4:
                            act.wait_ge(u_ready, q - 3)
                        for c in (0, 1):
                            k = 2 * i + c
                            ins = nc.scalar.activation(u_rows[:, i, c * T:(c + 1) * T], b[:, c * T:(c + 1) * T], ACT.Identity,
                                                       scale=scale1[:, v, k:k + 1], bias=shift1[:, v, k:k + 1])
                        ins.then_inc(evacuated[bank_of((key, i))], 1)
                    after_evacuation(act, (key, i), l)
                    nc.scalar.activation(uT_split[:, 0, 2 * i:2 * i + 2, t0:t0 + T],
                                         u_rows[:, i, :].rearrange("p (c t) -> p c t", c=2), ACT.Copy).then_inc(u_high_ready, 1)
                for i in (0, 1):
                    evac(("mq", i), l, flat(m_qT[:, 2 * i:2 * i + 2, :]), projected(("mq", i)), scale=DQK ** -0.5)
                ada_rows_out(4, 5)
                for h in range(NHM):
                    evac(("mk", h), l, m_kT[:, h, :], projected(("mk", h)))
                ada_rows_out(6, 7)
                act.wait_ge(gate_abs_ready, 1)
                step(nc.scalar.activation(f_abs, f_abs, ACT.Exp, scale=-1.0), l)
                nc.scalar.activation(f_abs, f_abs, ACT.Ln, bias=1.0).then_inc(gate_log_ready, 1)
                for i in (0, 1):
                    evac(("mv", i), l, m_v[:, i, 0:2, 0:DV], projected(("mv", i)).rearrange("p (h e) -> p h e", h=2))
                for i in (2, 3, 4, 5, 6, 7):
                    evac(("mv", i), l, m_v[:, i % 4, 2 * (i // 4):2 * (i // 4) + 2, 0:DV],
                         projected(("mv", i)).rearrange("p (h e) -> p h e", h=2))
                    if i in (3, 7):
                        ada_rows_out(8, 9) if i == 3 else ada_rows_out(10, 11)
                for i in range(4):
                    evac(("mo", i), l, o_row[:, i % 2, 512 * (i // 2):512 * (i // 2 + 1)], projected(("mo", i)), ACT.Sigmoid)
                split_until(unit2("dv", 0, 2))
                act.wait_ge(m_neg_ready, 1)
                step(nc.scalar.activation(m_neg, m_neg, ACT.Exp), l)
                for h in range(NHM):
                    after_evacuation(act, ("MB", h), l)
                    nc.scalar.activation(flat(decay[h % 2]), flat(decay[h % 2]), ACT.Exp, scale=-1.0).then_inc(decay_exp_ready, 1)
                act.wait_ge(h_ready, NHM)
                for t in range(TT):
                    for h in range(NHM):
                        ins = nc.scalar.activation(flat(decay[0])[:, (t * NHM + h) * DV:(t * NHM + h + 1) * DV], h_row[:, t, h * DV:(h + 1) * DV], ACT.Square,
                                                   accum_out=h_sq[:, t * NHM + h:t * NHM + h + 1])
                step(ins, l)
                nc.scalar.activation(h_rms, h_sq, ACT.Sqrt, bias=EPS, scale=1.0 / DV).then_inc(head_rms_ready, 1)
                act.wait_ge(lam_sum_ready, 1)
                nc.scalar.activation(lam_exp, lam_sum, ACT.Exp).then_inc(lam_exp_ready, 1)

                def values(g):
                    for i in range(4 * g, 4 * g + 4):
                        evac(("dv", i), l, d_v[:, i % 4, :], projected(("dv", i)))

                def raws(h):
                    evac(("dq", h), l, raw[:, h % 2, 0:T], projected(("dq", h))[:, 0:T])
                    b = projected(("dk", h))
                    nc.scalar.activation(d_kT[:, h % 4, 0:T], b[:, 0:T], ACT.Copy)
                    evac(("dk", h), l, raw[:, h % 2, T:S], b[:, T:S])

                def softmax(h):
                    for t in range(TT):
                        act.wait_ge(row_max_ready, 2 * h + t + 1)
                        for m in (0, 1):
                            b = psum[:, bank_of(("S", 4 * h + 2 * t + m)), :]
                            ins = nc.scalar.activation(probs[:, t, m, :], b, ACT.Exp, bias=neg_max[:, t, m:m + 1],
                                                       scale=DHD ** -0.5, accum_out=row_sum[:, t, m:m + 1])
                            ins.then_inc(evacuated[bank_of(("S", 4 * h + 2 * t + m))], 1)

                def out_of(h):
                    for t in range(TT):
                        evac(("PT", 2 * h + t), l, aT[:, t, :], take(act, ("PT", 2 * h + t), l))

                def head_rows(h):
                    evac(("O", h), l, b_row[:, :, h * P:(h + 1) * P],
                         take(act, ("O", h), l)[:, 0:T].rearrange("p (t e) -> p t e", t=TT))

                for h in range(NHD):
                    if h % 4 == 0:
                        values(h // 4)
                        if h == 0:
                            for i in range(4):
                                evac(("AT", i), l, flat(a_outT[:, 2 * i:2 * i + 2, :]), take(act, ("AT", i), l))
                        raws(h)
                    split_until(next_units(h))
                    softmax(h)
                    if h % 4 < 3:
                        raws(h + 1)
                    out_of(h)
                    head_rows(h)
                after_evacuation(act, ("O", NHD - 1), l)
                for t in range(TT):
                    for h in range(NHD):
                        ins = nc.scalar.activation(squares[:, (t * NHD + h) * P:(t * NHD + h + 1) * P], b_row[:, t, h * P:(h + 1) * P], ACT.Square,
                                                   accum_out=b_sq[:, t * NHD + h:t * NHD + h + 1])
                step(ins, l)
                nc.scalar.activation(b_rms, b_sq, ACT.Sqrt, bias=EPS, scale=1.0 / P).then_inc(head_rms_ready, 1)
                for g in (0, 1):
                    if g:
                        for i in range(4):
                            evac(("BT", i), l, flat(b_outT[:, 2 * i:2 * i + 2, :]), take(act, ("BT", i), l))
                    for key, dst in (("pa", gate_a), ("pb", gate_bb)):
                        for i in (0, 1):
                            if g:
                                after_evacuation(act, ("wa", i), l) if key == "pa" else act.wait_ge(y_ready, i + 1)
                            evac((key, 2 * g + i), l, dst[:, 512 * i:512 * i + 512], projected((key, 2 * g + i)), ACT.Sigmoid)
                rms_of_x(l, 2 * L2 + 2)
                for i in (0, 2):
                    b = take(act, ("R", i), l)
                    for c in (0, 1):
                        k = 2 * i + c
                        ins = nc.scalar.activation(u2T[:, k, :], b[:, c * T:(c + 1) * T], ACT.Identity,
                                                   scale=scale2[:, k:k + 1], bias=modT[:, 2 * KC + k, 0:1])
                    ins.then_inc(evacuated[bank_of(("R", i))], 1)
                act.wait_ge(mask_ready, 1)
                for t in range(TT):
                    ins = nc.scalar.activation(exps[:, t, 0:N_EXP], logits[:, t, 0:N_EXP], ACT.Exp, bias=neg_top[:, t:t + 1])
                ins.then_inc(exp_ready, 1)
                evac(("gT", 0), l, gT[0:N_EXP, :], take(act, ("gT", 0), l)[0:N_EXP, 0:T])

                def pair(it, j):
                    b = take(act, ("G", 0), it)
                    for k in range(4):
                        ins = nc.scalar.activation(xgT[:, k, :], b[:, k * P:(k + 1) * P], ACT.Identity,
                                                   scale=scale2[:, k:k + 1], bias=modT[:, 2 * KC + k, 0:1])
                    ins.then_inc(evacuated[bank_of(("G", 0))], 1)
                    for n in (0, 1):
                        after_evacuation(act, ("GLU", n), it)
                        nc.scalar.activation(sig[n], glu[n], ACT.Sigmoid, scale=ALPHA).then_inc(sig_ready, 1)
                    evac(("ST", 0), it, spread_T, take(act, ("ST", 0), it)[:, 0:T])
                    evac(("AT2", 0), it, flat(actT[:, 0:4, :]), take(act, ("AT2", 0), it))
                    for n in (0, 1):
                        evac(("OUT", n), it, out_sb[:, 512 * n:512 * n + 512], take(act, ("OUT", n), it))

                over_pairs(act, pair)
                rms_of_x(l, 2 * L2 + 3)

            act.dma_start(const[:, 0:SPARE], w["const"][:, 0:SPARE]).then_inc(const_loaded, 16)
            load_mixer_parameters(act, 0)
            act.dma_start(const[:, SPARE:], w["const"][:, SPARE:]).then_inc(tables_loaded, 16)
            act.dma_start(flatten(cT), w["cT"]).then_inc(c_loaded, 16)
            load_ffn_parameters(act, 0)
            loop_layers(act, layer)
            second()

        @block.vector
        def _(dve):
            n_step = [0]

            def step(ins, l, wait=True):
                n_step[0] += 1
                ins.then_inc(dve_step, 1)
                if wait:
                    dve.wait_ge(dve_step, l * DVE_STEPS + n_step[0])

            def inverse_rms(l, i, t):
                dve.wait_ge(rms_ready, 8 * l + 2 * i + t + 1)
                step(nc.vector.reciprocal(rinv[:, t:t + 1], rms[:, t:t + 1]), l)

            def normalise(l, i, n):
                for t in range(TT):
                    dve.wait_ge(x_ready if t else x_tile_ready, n)
                    inverse_rms(l, i, t)
                    nc.vector.tensor_scalar(xhat[:, t, :], x[:, t, :], rinv[:, t:t + 1], None, ALU.mult
                                            ).then_inc(xhat_ready if t else xhat_tile_ready, 1)

            def add_to_x(t):
                nc.vector.tensor_tensor(x[:, t, :], x[:, t, :], xhat[:, t, :], ALU.add
                                        ).then_inc(x_ready if t else x_tile_ready, 1)

            def add_normed(l, i, keys, gain):
                for t in range(TT):
                    inverse_rms(l, i, t)
                    for n in (0, 1):
                        b = bank_of(keys[2 * t + n])
                        cut = slice(512 * n, 512 * n + 512)
                        ins = nc.vector.scalar_tensor_tensor(out=xhat[:, t, cut], in0=psum[:, b, :],
                                                             scalar=rinv[:, t:t + 1], in1=gain[:, cut],
                                                             op0=ALU.mult, op1=ALU.mult)
                        ins.then_inc(evacuated[b], 1)
                    after_evacuation(dve, keys[2 * t + 1], l)
                    add_to_x(t)

            def low_rows(key, l, n, col):
                for i in range(4):
                    dve.wait_ge(hT_high_ready, 8 * l + (n + i + 1))
                    b = psum[:, bank_of((key, i)), :]
                    for c in (0, 1):
                        k = 2 * i + c
                        ins = nc.vector.scalar_tensor_tensor(out=hT_split[:, 1, k, :], in0=b[:, c * T:(c + 1) * T],
                                                             scalar=cols[:, col + k:col + k + 1],
                                                             in1=hT_split[:, 0, k, :], op0=ALU.mult, op1=ALU.subtract)
                    ins.then_inc(evacuated[bank_of((key, i))], 1)

            def rotate(key, l, dst, ready):
                b = take(dve, key, l)
                d = dst.rearrange("p a b -> p (a b)")
                halves = lambda v: v.rearrange("p (g e) -> p g e", e=HD)
                bs, sn, sw = halves(b), halves(cst("ret_sin")), halves(swapped)
                nc.vector.tensor_tensor(d, b, cst("ret_cos"), ALU.mult)
                nc.vector.tensor_tensor(sw[:, :, 0:32], bs[:, :, 32:64], sn[:, :, 0:32], ALU.mult)
                nc.vector.tensor_tensor(sw[:, :, 32:64], bs[:, :, 0:32], sn[:, :, 32:64], ALU.mult
                                        ).then_inc(evacuated[bank_of(key)], 1)
                after_evacuation(dve, key, l)
                nc.vector.tensor_tensor(d, d, swapped, ALU.add).then_inc(ready, 1)

            def layer(l):
                n_step[0] = 0
                def split(n):
                    dve.wait_ge(w_high_ready, l * len(UNITS) + (n + 1))
                    nc.vector.tensor_tensor(unit_weights(n, 1), unit_weights(n, None)[0], unit_weights(n, 0), ALU.subtract
                                            ).then_inc(w_split, 1)

                split_until = units_ahead(split, UNITS)
                normalise(l, 0, 2 * l + 1)
                split_until(UNIT_BUFFERS - 1)
                dve.wait_ge(mix_par_loaded, 48 * l + 48)
                low_rows("T", l, 0, COL_MIX_PRE)

                split_until(5)
                b = take(dve, ("s", 0), l).rearrange("p (c t) -> p c t", c=2)
                after_evacuation(dve, ("s", 1), l)
                nc.vector.tensor_tensor(conf_pad[:, :, 30:30 + T], b, conf_gate, ALU.mult
                                        ).then_inc(evacuated[bank_of(("s", 0))], 1)
                after_evacuation(dve, ("s", 0), l)

                def conf_taps(lo, hi):
                    for k in range(lo, hi):
                        for c in (0, 1):
                            wk = cols[:, COL_CONF_W + 2 * k + c:COL_CONF_W + 2 * k + c + 1]
                            src = conf_pad[:, c, k:k + T]
                            if k == 0:
                                ins = nc.vector.tensor_scalar(conf[:, c, :], src, wk,
                                                              cols[:, COL_CONF_B + c:COL_CONF_B + c + 1],
                                                              ALU.mult, ALU.add)
                            else:
                                dve.wait_ge(dve_step, l * DVE_STEPS + n_step[0] - 1)
                                ins = nc.vector.scalar_tensor_tensor(out=conf[:, c, :], in0=src, scalar=wk,
                                                                     in1=conf[:, c, :], op0=ALU.mult, op1=ALU.add)
                            if k == CONF_K - 1 and c == 1:
                                ins.then_inc(conf_ready, 1)
                            else:
                                step(ins, l, wait=False)

                for first, last, n in ((0, 3, 7), (3, 6, 9), (6, 10, 11)):
                    conf_taps(first, last)
                    split_until(n)
                dve.wait_ge(tables_loaded, 16)
                rotate(("s", 5), l, rq, rq_ready)
                split_until(13)
                for h in range(NH):
                    after_evacuation(dve, ("Z", h), l)
                nc.vector.scalar_tensor_tensor(out=soft, in0=z, scalar=-1.0, in1=z, op0=ALU.mult, op1=ALU.max
                                               ).then_inc(sb_abs, 1)
                dve.wait_ge(rq_ready, l + 1)
                split_until(15)
                rotate(("s", 6), l, rk, rk_ready)
                conf_taps(10, 12)
                split_until(17)
                conf_taps(12, 16)
                split_until(18)
                dve.wait_ge(sb_log, l + 1)
                step(nc.vector.scalar_tensor_tensor(out=soft, in0=z, scalar=0.0, in1=soft,
                                                    op0=ALU.max, op1=ALU.add), l)
                nc.vector.tensor_tensor(soft, soft, sb_mask4, ALU.mult).then_inc(sb_soft, 1)
                split_until(19)
                for h in range(NH):
                    b = take(dve, ("RS", h), l)
                    nc.vector.tensor_tensor(r_scores[:, h, :], b[:, 0:DIAG], ret_decay[:, h, :], ALU.mult
                                            ).then_inc(evacuated[bank_of(("RS", h))], 1)
                split_until(21)
                conf_taps(16, 20)
                split_until(23)
                for h in range(NH):
                    b = take(dve, ("I", h), l)
                    nc.vector.tensor_tensor(z[:, h, :], z[:, h, :], b[:, 0:DIAG], ALU.subtract
                                            ).then_inc(evacuated[bank_of(("I", h))], 1)
                after_evacuation(dve, ("I", 3), l)
                nc.vector.tensor_tensor(z, z, sb_neg4, ALU.add).then_inc(sb_arg, 1)
                conf_taps(20, CONF_K)
                b = take(dve, ("s", 11), l).rearrange("p (c t) -> p c t", c=2)
                after_evacuation(dve, ("s", 10), l)
                nc.vector.tensor_tensor(sc_pad[:, :, 2:2 + T], b, sc_c, ALU.mult
                                        ).then_inc(evacuated[bank_of(("s", 11))], 1)
                after_evacuation(dve, ("s", 11), l)
                for k in range(SC_K):
                    for c in (0, 1):
                        wk = cols[:, COL_SC_W + 2 * k + c:COL_SC_W + 2 * k + c + 1]
                        src = sc_pad[:, c, k:k + T]
                        if k == 0:
                            step(nc.vector.tensor_scalar(sc_c[:, c, :], src, wk, None, ALU.mult), l, wait=False)
                        else:
                            dve.wait_ge(dve_step, l * DVE_STEPS + n_step[0] - 1)
                            step(nc.vector.scalar_tensor_tensor(out=sc_c[:, c, :], in0=src, scalar=wk,
                                                                in1=sc_c[:, c, :], op0=ALU.mult, op1=ALU.add),
                                 l, wait=k == SC_K - 1 and c == 1)
                after_evacuation(dve, ("s", 9), l)
                nc.vector.tensor_tensor(catT[:, 6:8, :], sc_c, sc_b, ALU.mult).then_inc(sc_cat, 1)
                b = take(dve, ("CM", 0), l)
                for c in (0, 1):
                    ins = nc.vector.scalar_tensor_tensor(out=conf[:, c, :], in0=b[:, 0:T], scalar=-1.0 / GW,
                                                         in1=conf[:, c, :], op0=ALU.mult, op1=ALU.add)
                ins.then_inc(evacuated[bank_of(("CM", 0))], 1)
                b = take(dve, ("RO", 0), l).rearrange("p (g e) -> p g e", e=HD)
                retg = ret.rearrange("p a b -> p (a b)").rearrange("p (g e) -> p g e", e=HD)
                sqg = swapped.rearrange("p (g e) -> p g e", e=HD)
                wide = lambda v: v.unsqueeze(2).broadcast_to([P, 8, HD])
                step(nc.vector.tensor_reduce(ret_mu, b, AX, ALU.add), l)
                step(nc.vector.tensor_scalar(ret_mu, ret_mu, 1.0 / HD, None, ALU.mult), l)
                take(dve, ("CV", 0), l)
                nc.vector.tensor_tensor(retg, b, wide(ret_mu), ALU.subtract).then_inc(evacuated[bank_of(("RO", 0))], 1)
                after_evacuation(dve, ("RO", 0), l)
                step(nc.vector.tensor_tensor(sqg, retg, retg, ALU.mult), l)
                nc.vector.tensor_reduce(ret_var, sqg, AX, ALU.add).then_inc(ret_var_ready, 1)
                after_evacuation(dve, ("CV", 0), l)
                step(nc.vector.reciprocal(conf_gate[:, 1, :], conf_gate[:, 0, :]), l)
                nc.vector.tensor_tensor(conf, conf, conf_gate[:, 1:2, :].broadcast_to([P, 2, T]), ALU.mult
                                        ).then_inc(conf_normed, 1)
                dve.wait_ge(ret_std_ready, l + 1)
                step(nc.vector.reciprocal(ret_rinv, ret_std), l)
                step(nc.vector.tensor_tensor(retg, retg, wide(ret_rinv), ALU.mult), l)
                gain = mix_row[:, D:].unsqueeze(1).broadcast_to([P, TT, GW])
                step(nc.vector.tensor_tensor(ret, ret, gain, ALU.mult), l)
                after_evacuation(dve, ("s", 8), l)
                nc.vector.tensor_tensor(ret, ret, rg, ALU.mult).then_inc(ret_ready, 1)
                split_until(MIX_UNITS + UNIT_BUFFERS - 1)
                add_normed(l, 1, [("M", i) for i in range(4)], mix_row)
                normalise(l, 2, 2 * l + 2)
                dve.wait_ge(ffn_par_loaded, 32 * l + 32)
                low_rows("F", l, 4, COL_FFN_PRE)

                def later_taps(g, u):
                    b = take(dve, ("U", 2 * g + u), l)
                    dve.wait_ge(tap_ready, l * 22 + (2 * g + u + 1))
                    for k in (1, 2):
                        for c in (0, 1):
                            at = COL_FFN_W + (2 * FFC) * (2 - k) + u * FFC + 2 * g + c
                            o = taps[:, g % 2, 2 * u + c, k:T]
                            ins = nc.vector.scalar_tensor_tensor(
                                out=o, in0=b[:, c * T:(c + 1) * T - k], scalar=cols[:, at:at + 1], in1=o,
                                op0=ALU.mult, op1=ALU.add)
                            if k == 1:
                                step(ins, l, wait=c == 1)
                    ins.then_inc(evacuated[bank_of(("U", 2 * g + u))], 1)
                    if u == 1:
                        after_evacuation(dve, ("U", 2 * g + 1), l)
                        dve.wait_ge(silu_ready, l * 11 + (g + 1))
                        nc.vector.tensor_tensor(taps[:, g % 2, 0:2, :], taps[:, g % 2, 0:2, :], taps[:, g % 2, 2:4, :],
                                                ALU.mult).then_inc(product_ready, 1)

                def low_part(g):
                    dve.wait_ge(ff_high_ready, l * 11 + (g + 1))
                    nc.vector.tensor_tensor(ffT_split[:, 1, 2 * (g % 4):2 * (g % 4) + 2, :], taps[:, g % 2, 0:2, :],
                                            ffT_split[:, 0, 2 * (g % 4):2 * (g % 4) + 2, :], ALU.subtract).then_inc(ff_ready, 1)

                ffn_stages(split_until, later_taps, low_part)
                add_normed(l, 3, [("D", i) for i in range(4)], ffn_row)
                assert n_step[0] == DVE_STEPS, n_step

            def second():
                n_step[0] = 0
                l = L2
                norm_g = cols2[:, 0:2 * KC].rearrange("p (a k) -> p a k", a=2)
                ada_b = cols2[:, 2 * KC:6 * KC].unsqueeze(2).broadcast_to([P, 4 * KC, 2])
                dve.wait_ge(early_loaded, 96)
                step(nc.vector.tensor_copy(iota, cst2("iota")), l, wait=False)
                dve.wait_ge(gate_w_high, 1)
                nc.vector.tensor_tensor(gate_w_split[:, 1], gate_w, gate_w_split[:, 0], ALU.subtract).then_inc(gate_w_ready, 1)

                def split(n):
                    dve.wait_ge(w_high_ready, DEPTH * len(UNITS) + n + 1)
                    nc.vector.tensor_tensor(unit_weights2(n, 1), unit_weights2(n, None), unit_weights2(n, 0), ALU.subtract
                                            ).then_inc(w_split, 1)

                split_until = units_ahead(split, B2_UNITS)
                pairs = lam_row.rearrange("p (a b) e -> p a b e", b=2)
                step(nc.vector.tensor_tensor(lam_prod, pairs[:, :, 0, :], pairs[:, :, 1, :], ALU.mult), l)
                nc.vector.tensor_reduce(lam_sum, lam_prod, AX, ALU.add).then_inc(lam_sum_ready, 1)
                dve.wait_ge(g_bias_loaded, 32)

                def spread_rows(n):
                    i = 0 if n < 6 else 1
                    cut = slice(512 * (n % 2), 512 * (n % 2) + 512)
                    b = take(dve, ("mR", n), l)
                    nc.vector.tensor_tensor(g_rows[:, i, cut], g_rows[:, i, cut], b, ALU.add
                                            ).then_inc(evacuated[bank_of(("mR", n))], 1)

                def mod_columns(i):
                    b = take(dve, ("mT", i), l)[:, 0:32].rearrange("p (k v) -> p k v", v=2)
                    nc.vector.tensor_tensor(modT[:, 16 * i:16 * i + 16, :], b, ada_b[:, 16 * i:16 * i + 16, :], ALU.add
                                            ).then_inc(evacuated[bank_of(("mT", i))], 1)
                    after_evacuation(dve, ("mT", i), l)

                normalise(l, 0, 2 * L2 + 1)
                dve.wait_ge(xhat_ready, 2 * L2 + 1)
                for t in range(TT):
                    inverse_rms(l, 1, t)
                    ins = nc.vector.tensor_scalar(ctx_row[:, t, :], ctx_row[:, t, :], rinv[:, t:t + 1], None, ALU.mult)
                ins.then_inc(ctx_hat_ready, 1)
                mod_columns(0)
                for v in (0, 1):
                    step(nc.vector.tensor_copy(shift1[:, v, :], modT[:, 0:KC, v]), l, wait=False)
                    ins = nc.vector.scalar_tensor_tensor(out=scale1[:, v, :], in0=modT[:, KC:2 * KC, v], scalar=1.0,
                                                         in1=norm_g[:, 0, :], op0=ALU.add, op1=ALU.mult)
                    ins.then_inc(scale1_ready, 1) if v else step(ins, l, wait=False)
                dve.wait_ge(scale1_ready, 1)
                split_until(UNIT_BUFFERS - 1)
                for q in range(8):
                    key, v, t0, i = ("XT", 0, T, q) if q < 4 else ("CT", 1, 0, q - 4)
                    if i % 2:
                        b = take(dve, (key, i), l)
                        if q >= 4:
                            dve.wait_ge(u_ready, q - 3)
                        for c in (0, 1):
                            k = 2 * i + c
                            ins = nc.vector.tensor_scalar(u_rows[:, i, c * T:(c + 1) * T], b[:, c * T:(c + 1) * T],
                                                          scale1[:, v, k:k + 1], shift1[:, v, k:k + 1], ALU.mult, ALU.add)
                        ins.then_inc(evacuated[bank_of((key, i))], 1)
                    dve.wait_ge(u_high_ready, q + 1)
                    hi, lo = (uT_split[:, a, 2 * i:2 * i + 2, t0:t0 + T] for a in (0, 1))
                    nc.vector.tensor_tensor(lo, u_rows[:, i, :].rearrange("p (c t) -> p c t", c=2), hi, ALU.subtract
                                            ).then_inc(u_ready, 1)
                split_until(unit2("mv", 0, 1))
                ones_col = m_v[:, :, :, DV:DV + 1]
                step(nc.vector.memset(ones_col, 1.0), l, wait=False)
                for d in (0, 1):
                    for i in (0, 1):
                        step(nc.vector.memset(cummax[d][i], 0.0), l, wait=False)
                b = take(dve, ("mg", 0), l)[:, 0:ST * 16].rearrange("p (s n) -> p s n", n=16)
                nc.vector.tensor_tensor(gates, b, gate_b.unsqueeze(1).broadcast_to([P, ST, 16]), ALU.add
                                        ).then_inc(evacuated[bank_of(("mg", 0))], 1)
                after_evacuation(dve, ("mg", 0), l)
                by_dir = gates.rearrange("p s (d g h) -> p (s d) g h", d=2, g=2)
                in_gate, f_gate = by_dir[:, :, 0, :], by_dir[:, :, 1, :]
                step(nc.vector.tensor_scalar(f_neg, f_gate, -1.0, None, ALU.mult), l, wait=False)
                step(nc.vector.tensor_scalar(f_min, f_gate, 0.0, None, ALU.min), l)
                nc.vector.tensor_tensor(f_abs, f_gate, f_neg, ALU.max).then_inc(gate_abs_ready, 1)
                spread_rows(4)
                spread_rows(5)
                dve.wait_ge(gate_log_ready, 1)
                nc.vector.tensor_tensor(log_f, f_min, f_abs, ALU.subtract).then_inc(gate_ready, 1)
                split_until(unit2("mv", 1, 1))
                b = take(dve, ("F", 9), l)
                f_sum = b[:, 0:32].rearrange("p (s h) -> p s h", h=4)
                step(nc.vector.tensor_copy(f_neg[:, 0:4, :], f_sum[:, 4:8, :]), l, wait=False)
                nc.vector.tensor_tensor(g_sub.rearrange("p s (d h) -> p (s d) h", d=2), in_gate, f_sum, ALU.subtract
                                        ).then_inc(evacuated[bank_of(("F", 9))], 1)
                for d in (0, 1):
                    b = take(dve, ("GT", d), l)[0:NHM, :]
                    step(nc.vector.tensor_reduce(ctx_max[0:NHM, d:d + 1], b[:, 0:T], AX, ALU.max), l)
                    step(nc.vector.tensor_scalar(ctx_max[0:NHM, d:d + 1], ctx_max[0:NHM, d:d + 1], 0.0, None, ALU.max), l)
                    at0 = P * (1 - d)
                    nc.vector.tensor_scalar(cummax[d][0][:, at0:at0 + T], b[:, T:S], ctx_max[0:NHM, d:d + 1], None,
                                            ALU.max).then_inc(evacuated[bank_of(("GT", d))], 1)
                    after_evacuation(dve, ("GT", d), l)
                for i in range(8):
                    for d in (0, 1):
                        src, dst = cummax[d][i % 2], cummax[d][(i + 1) % 2]
                        at0, shift = P * (1 - d), (1 << i) * (2 * d - 1)
                        ins = nc.vector.tensor_tensor(dst[:, at0:at0 + T], src[:, at0:at0 + T],
                                                      src[:, at0 + shift:at0 + shift + T], ALU.max)
                        if i == 7 and d == 1:
                            ins.then_inc(cummax_ready, 1)
                        else:
                            step(ins, l, wait=d == 1)
                    if i % 2:
                        split_until(unit2("mv", 1, 1) + (i + 1) // 2)
                mod_columns(1)
                step(nc.vector.scalar_tensor_tensor(out=scale2, in0=modT[:, 3 * KC:4 * KC, 0], scalar=1.0,
                                                    in1=norm_g[:, 1, :], op0=ALU.add, op1=ALU.mult), l, wait=False)
                split_until(unit2("mo", 1, 3))
                spread_rows(10)
                spread_rows(11)
                split_until(unit2("dv", 0, 2))
                b = take(dve, ("MR", 0), l)[:, 0:16].rearrange("p (s h) -> p s h", h=4)
                mn = m_neg.rearrange("p (s h) -> p s h", h=4)
                nc.vector.scalar_tensor_tensor(out=mn, in0=b, scalar=-1.0, in1=f_neg[:, 0:4, :],
                                               op0=ALU.mult, op1=ALU.subtract).then_inc(evacuated[bank_of(("MR", 0))], 1)
                after_evacuation(dve, ("MR", 0), l)
                nc.vector.tensor_scalar(m_neg, m_neg, 88.0, None, ALU.min).then_inc(m_neg_ready, 1)

                def decay_args(h):
                    b = take(dve, ("MB", h), l)
                    if h >= 2:
                        take(dve, ("H", 4 * (h - 2) + 3), l)
                    for d in (0, 1):
                        for st in range(ST):
                            g = g_sub[:, st, 4 * d + h:4 * d + h + 1]
                            ins = nc.vector.tensor_scalar(decay[h % 2][:, d, st * T:(st + 1) * T], b[:, d * T:(d + 1) * T],
                                                          g, 0.0, ALU.subtract, ALU.max)
                            if d == 0 or st < ST - 1:
                                step(ins, l, wait=False)
                    ins.then_inc(evacuated[bank_of(("MB", h))], 1)

                def weigh(h):
                    dve.wait_ge(decay_exp_ready, h + 1)
                    for d, tri in ((0, cst2("prefix")), (1, suffix)):
                        for t in range(TT):
                            v = decay[h % 2][:, d, (TT + t) * T + t * P:(TT + t) * T + (t + 1) * P]
                            step(nc.vector.tensor_tensor(v, v, tri, ALU.mult), l, wait=d == 1 and t == 1)
                    for q in (0, 1):
                        b = take(dve, ("QK", 2 * h + q), l)
                        for d in (0, 1):
                            v = decay[h % 2][:, d, 512 * q:512 * q + 512]
                            ins = nc.vector.tensor_tensor(v, v, b, ALU.mult)
                            if d == 0:
                                step(ins, l, wait=False)
                        ins.then_inc(evacuated[bank_of(("QK", 2 * h + q))], 1)

                def outputs(h):
                    for d in (0, 1):
                        for t in range(TT):
                            b = take(dve, ("H", 4 * h + 2 * d + t), l)
                            i = 2 * d + t
                            step(nc.vector.tensor_scalar(den[:, i:i + 1], b[:, DV:DV + 1], -1.0, None, ALU.mult), l)
                            step(nc.vector.tensor_tensor(den[:, i:i + 1], den[:, i:i + 1], b[:, DV:DV + 1], ALU.max), l)
                            e = m_neg[:, 4 * (2 * t + d) + h:4 * (2 * t + d) + h + 1]
                            step(nc.vector.tensor_tensor(den[:, i:i + 1], den[:, i:i + 1], e, ALU.max), l)
                            step(nc.vector.reciprocal(den2[:, i:i + 1], den[:, i:i + 1]), l)
                            o = h_row[:, t, h * DV:(h + 1) * DV]
                            if d == 0:
                                ins = nc.vector.tensor_scalar(o, b[:, 0:DV], den2[:, i:i + 1], None, ALU.mult)
                            else:
                                after_evacuation(dve, ("H", 4 * h + t), l)
                                ins = nc.vector.scalar_tensor_tensor(out=o, in0=b[:, 0:DV], scalar=den2[:, i:i + 1],
                                                                     in1=o, op0=ALU.mult, op1=ALU.add)
                            ins.then_inc(evacuated[bank_of(("H", 4 * h + i))], 1)
                    after_evacuation(dve, ("H", 4 * h + 3), l)
                    dve.sem_inc(h_ready, 1)

                decay_args(0)
                weigh(0)
                for h in range(1, NHM + 1):
                    if h < NHM:
                        decay_args(h)
                    if h < NHM:
                        weigh(h)
                    outputs(h - 1)
                dve.wait_ge(head_rms_ready, 1)
                dve.wait_ge(norm_row_loaded, 16)
                step(nc.vector.reciprocal(h_inv, h_rms), l)
                for t in range(TT):
                    for h in range(NHM):
                        v = h_row[:, t, h * DV:(h + 1) * DV]
                        i = t * NHM + h
                        step(nc.vector.scalar_tensor_tensor(out=v, in0=v, scalar=h_inv[:, i:i + 1],
                                                            in1=norm_row[:, h * DV:(h + 1) * DV],
                                                            op0=ALU.mult, op1=ALU.mult), l, wait=i == 2 * NHM - 1)
                after_evacuation(dve, ("mo", 3), l)
                nc.vector.tensor_tensor(h_row, h_row, o_row, ALU.mult).then_inc(h_normed, 1)
                split_until(unit2("dk", 0, 0))
                dve.wait_ge(lam_exp_ready, 1)
                step(nc.vector.tensor_tensor(neg_lam, lam_exp[:, 1:2], lam_exp[:, 0:1], ALU.subtract), l)
                step(nc.vector.tensor_scalar(neg_lam, neg_lam, -LAM_INIT, None, ALU.add), l)
                for h in range(4):
                    step(nc.vector.memset(d_q[0:64, 2 * h + 1, :], 0.0), l, wait=False)
                    step(nc.vector.memset(d_q[64:128, 2 * h, :], 0.0), l, wait=False)
                cos2 = cst2("rope_cos").unsqueeze(1).broadcast_to([P, 2, T])
                sin2 = cst2("rope_sin").unsqueeze(1).broadcast_to([P, 2, T])

                def rope(h):
                    b = take(dve, ("rot", h), l)
                    r = raw[:, h % 2, :]
                    two = lambda v: v.rearrange("p (a t) -> p a t", a=2)
                    step(nc.vector.tensor_tensor(two(r), two(r), cos2, ALU.mult), l, wait=False)
                    if h:
                        dve.wait_ge(qk_ready, h)
                    nc.vector.tensor_tensor(two(turned), two(b), sin2, ALU.mult).then_inc(evacuated[bank_of(("rot", h))], 1)
                    after_evacuation(dve, ("rot", h), l)
                    if h >= 4:
                        take(dve, ("S", 4 * (h - 4) + 3), l)
                    for m in (0, 1):
                        rows = slice(64 * m, 64 * m + 64)
                        step(nc.vector.tensor_tensor(d_q[rows, 2 * (h % 4) + m, :], r[rows, 0:T], turned[rows, 0:T], ALU.add),
                             l, wait=False)
                    nc.vector.tensor_tensor(d_kT[:, h % 4, T:S], r[:, T:S], turned[:, T:S], ALU.add).then_inc(qk_ready, 1)

                def maxima(h):
                    for t in range(TT):
                        for m in (0, 1):
                            b = take(dve, ("S", 4 * h + 2 * t + m), l)
                            step(nc.vector.tensor_reduce(row_max[:, t, m:m + 1], b, AX, ALU.max), l, wait=m == 1)
                        nc.vector.tensor_scalar(neg_max[:, t, :], row_max[:, t, :], -DHD ** -0.5, None, ALU.mult
                                                ).then_inc(row_max_ready, 1)

                def difference(h):
                    for t in range(TT):
                        after_evacuation(dve, ("S", 4 * h + 2 * t), l)
                        after_evacuation(dve, ("S", 4 * h + 2 * t + 1), l)
                        step(nc.vector.reciprocal(row_inv[:, t, :], row_sum[:, t, :]), l)
                        step(nc.vector.tensor_tensor(map_scale[:, t, 0:1], row_inv[:, t, 1:2], neg_lam, ALU.mult), l)
                        p1 = probs[:, t, 1, :]
                        step(nc.vector.tensor_scalar(p1, p1, map_scale[:, t, 0:1], None, ALU.mult), l)
                        p0 = probs[:, t, 0, :]
                        nc.vector.scalar_tensor_tensor(out=p0, in0=p0, scalar=row_inv[:, t, 0:1], in1=p1,
                                                       op0=ALU.mult, op1=ALU.add).then_inc(attn_ready, 1)

                for h in range(NHD):
                    if h % 4 == 0:
                        rope(h)
                    split_until(next_units(h))
                    maxima(h)
                    difference(h)
                    if h % 4 < 3:
                        rope(h + 1)
                    elif h < NHD - 1:
                        split_until(ITEM_UNIT["dk", h + 1])
                dve.wait_ge(head_rms_ready, 2)
                dve.wait_ge(norm_row_loaded, 32)
                step(nc.vector.reciprocal(b_inv, b_rms), l)
                step(nc.vector.tensor_scalar(b_inv, b_inv, 1.0 - LAM_INIT, None, ALU.mult), l)
                for t in range(TT):
                    for h in range(NHD):
                        v = b_row[:, t, h * P:(h + 1) * P]
                        i = t * NHD + h
                        ins = nc.vector.scalar_tensor_tensor(out=v, in0=v, scalar=b_inv[:, i:i + 1],
                                                             in1=norm_row[:, h * P:(h + 1) * P], op0=ALU.mult, op1=ALU.mult)
                        if i < 2 * NHD - 1:
                            step(ins, l, wait=False)
                ins.then_inc(b_normed, 1)
                split_until(ITEM_UNIT["pb", 1] + 2)
                for g in (0, 1):
                    if g:
                        split_until(len(B2_UNITS) - 1)
                    for i in (0, 1):
                        cut = slice(512 * i, 512 * i + 512)
                        y = flatten(yT[:, 4 * g + 2 * i:4 * g + 2 * i + 2, :])
                        b = take(dve, ("wa", 2 * g + i), l)
                        after_evacuation(dve, ("pa", 2 * g + i), l)
                        nc.vector.tensor_tensor(y, b, gate_a[:, cut], ALU.mult
                                                ).then_inc(evacuated[bank_of(("wa", 2 * g + i))], 1)
                        b = take(dve, ("wb", 2 * g + i), l)
                        after_evacuation(dve, ("pb", 2 * g + i), l)
                        nc.vector.tensor_tensor(gate_bb[:, cut], b, gate_bb[:, cut], ALU.mult
                                                ).then_inc(evacuated[bank_of(("wb", 2 * g + i))], 1)
                        after_evacuation(dve, ("wa", 2 * g + i), l)
                        after_evacuation(dve, ("wb", 2 * g + i), l)
                        nc.vector.tensor_tensor(y, y, gate_bb[:, cut], ALU.add).then_inc(y_ready, 1)
                assert len(B2_UNITS) == unit2("pb", 1, 3) + 1
                for i in range(4):
                    t, half = divmod(i, 2)
                    cut = slice(512 * half, 512 * half + 512)
                    b = take(dve, ("Y", i), l)
                    nc.vector.tensor_tensor(xhat[:, t, cut], b, g_rows[:, 0, cut], ALU.mult
                                            ).then_inc(evacuated[bank_of(("Y", i))], 1)
                    if half:
                        after_evacuation(dve, ("Y", i), l)
                        add_to_x(t)
                normalise(l, 2, 2 * L2 + 2)
                for i in (1, 3):
                    b = take(dve, ("R", i), l)
                    for c in (0, 1):
                        k = 2 * i + c
                        ins = nc.vector.tensor_scalar(u2T[:, k, :], b[:, c * T:(c + 1) * T], scale2[:, k:k + 1],
                                                      modT[:, 2 * KC + k, 0:1], ALU.mult, ALU.add)
                    ins.then_inc(evacuated[bank_of(("R", i))], 1)
                below = -3e38
                step(nc.vector.memset(logits[:, :, N_EXP:], below), l, wait=False)
                b = take(dve, ("L", 0), l)[:, 0:TT * N_EXP].rearrange("p (t e) -> p t e", t=TT)
                nc.vector.tensor_tensor(logits[:, :, 0:N_EXP], b, router_b.unsqueeze(1).broadcast_to([P, TT, N_EXP]), ALU.add
                                        ).then_inc(evacuated[bank_of(("L", 0))], 1)
                after_evacuation(dve, ("L", 0), l)
                for t in range(TT):
                    step(nc.vector.max(top8[:, t, :], logits[:, t, 0:N_EXP]), l, wait=t == 1)
                step(nc.vector.tensor_scalar(neg_top, top8[:, :, 0], -1.0, None, ALU.mult), l, wait=False)
                step(nc.vector.memset(top8[:, :, TOP_K:], below), l)
                for t in range(TT):
                    step(nc.vector.match_replace(others[:, t, :], top8[:, t, :], logits[:, t, :], below), l, wait=t == 1)
                nc.vector.tensor_tensor(chosen, logits[:, :, 0:N_EXP], others[:, :, 0:N_EXP], ALU.not_equal
                                        ).then_inc(mask_ready, 1)
                dve.wait_ge(exp_ready, 1)
                step(nc.vector.tensor_tensor(gate_row, exps[:, :, 0:N_EXP], chosen, ALU.mult), l)
                step(nc.vector.tensor_reduce(gate_sum, gate_row, AX, ALU.add), l)
                step(nc.vector.reciprocal(gate_inv, gate_sum), l)
                nc.vector.tensor_tensor(gate_row, gate_row, gate_inv.unsqueeze(2).broadcast_to([P, TT, N_EXP]), ALU.mult
                                        ).then_inc(gates_ready, 1)
                by_pair = lambda v: v.rearrange("p (j t x) -> p t j x", j=PAIRS, t=TT)
                pairs = lambda v: v.rearrange("p (j x) -> p j x", x=2)
                dve.wait_ge(gates_ready, 1)
                b = take(dve, ("PC", 0), l)
                for t in range(TT):
                    step(nc.vector.tensor_copy(by_pair(pair_gate)[:, t], pairs(gate_row[:, t, :])), l, wait=False)
                    ins = nc.vector.scalar_tensor_tensor(out=by_pair(pair_slot)[:, t], in0=pairs(b[:, t * N_EXP:(t + 1) * N_EXP]),
                                                         scalar=1.0, in1=pairs(chosen[:, t, :]), op0=ALU.add, op1=ALU.mult)
                    if t == 0:
                        step(ins, l, wait=False)
                ins.then_inc(evacuated[bank_of(("PC", 0))], 1)
                after_evacuation(dve, ("PC", 0), l)
                step(nc.vector.tensor_scalar(pair_slot, pair_slot, -1.0, None, ALU.add), l)
                b = take(dve, ("CN", 0), l)
                nc.vector.tensor_reduce(most, b[:, 0:N_EXP], AX, ALU.max).then_inc(evacuated[bank_of(("CN", 0))], 1)
                after_evacuation(dve, ("CN", 0), l)
                step(nc.vector.tensor_scalar(n_pass, most, float(CAP), 1.0, ALU.is_gt, ALU.add), l)
                for k in range(2, T // CAP):
                    step(nc.vector.scalar_tensor_tensor(out=n_pass, in0=most, scalar=float(k * CAP), in1=n_pass,
                                                        op0=ALU.is_gt, op1=ALU.add), l)
                nc.vector.tensor_copy(passes[:, :], n_pass).then_inc(passes_ready, 1)
                slots4 = iota.unsqueeze(1).broadcast_to([P, 4, CAP])

                def pair(it, j):
                    n_pair_step = [0]

                    def pair_step(ins):
                        n_pair_step[0] += 1
                        ins.then_inc(pairs_step, 1)
                        dve.wait_ge(pairs_step, 5 * it + n_pair_step[0])

                    four = pair_slot[:, bass.ds(4 * j, 4)]
                    to_slots = lambda v: v.rearrange("p t (x s) -> p (t x) s", x=2)
                    pair_step(nc.vector.tensor_tensor(to_slots(pick), slots4, four.unsqueeze(2).broadcast_to([P, 4, CAP]),
                                                      ALU.is_equal))
                    nc.vector.tensor_copy(pick_e.rearrange("p (x s) -> p x s", x=2),
                                          ident[:, bass.ds(2 * j, 2)].unsqueeze(2).broadcast_to([P, 2, CAP]))
                    pair_step(nc.vector.tensor_scalar(four, four, -float(CAP), None, ALU.add))
                    nc.vector.tensor_tensor(to_slots(pick_gated), to_slots(pick),
                                            pair_gate[:, bass.ds(4 * j, 4)].unsqueeze(2).broadcast_to([P, 4, CAP]),
                                            ALU.mult).then_inc(picks_ready, 1)
                    b = take(dve, ("G", 1), it)
                    for k in range(4):
                        ins = nc.vector.tensor_scalar(xgT[:, 4 + k, :], b[:, k * P:(k + 1) * P], scale2[:, 4 + k:5 + k],
                                                      modT[:, 2 * KC + 4 + k, 0:1], ALU.mult, ALU.add)
                    ins.then_inc(evacuated[bank_of(("G", 1))], 1)
                    for n in (0, 1):
                        nc.vector.tensor_scalar(glu[n], take(dve, ("GLU", n), it), LIMIT, None, ALU.min
                                                ).then_inc(evacuated[bank_of(("GLU", n))], 1)
                        nc.vector.tensor_scalar(lin[n], take(dve, ("LIN", n), it), LIMIT, -LIMIT, ALU.min, ALU.max
                                                ).then_inc(evacuated[bank_of(("LIN", n))], 1)
                        after_evacuation(dve, ("LIN", n), it)
                        pair_step(nc.vector.scalar_tensor_tensor(out=lin[n], in0=lin[n], scalar=1.0, in1=glu[n],
                                                                 op0=ALU.add, op1=ALU.mult))
                        dve.wait_ge(sig_ready, 2 * it + (n + 1))
                        nc.vector.tensor_tensor(act_[n], lin[n], sig[n], ALU.mult).then_inc(hidden_ready, 1)
                    nc.vector.tensor_copy(flatten(actT[:, 4:8, :]), take(dve, ("AT2", 1), it)
                                          ).then_inc(evacuated[bank_of(("AT2", 1))], 1)
                    dve.sem_inc(pairs_step, 1)

                n = over_pairs(dve, pair)
                dve.wait_ge(late_loaded, 64)
                dve.wait_ge(combined, n * PAIRS)
                for i in range(4):
                    t, half = divmod(i, 2)
                    cut = slice(512 * half, 512 * half + 512)
                    step(nc.vector.tensor_tensor(xhat[:, t, cut], psum[:, i, :], g_rows[:, 1, cut], ALU.mult), l, wait=half == 1)
                    if half:
                        add_to_x(t)
                for t in range(TT):
                    dve.wait_ge(x_ready if t else x_tile_ready, 2 * L2 + 3)
                    inverse_rms(l, 3, t)
                    nc.vector.scalar_tensor_tensor(out=xhat[:, t, :], in0=x[:, t, :], scalar=rinv[:, t:t + 1], in1=final_row,
                                                   op0=ALU.mult, op1=ALU.mult).then_inc(out_ready, 1)

            for v in (q_z, rq_z):
                nc.vector.memset(v[0:64, 1:NH:2, :], 0.0)
                ins = nc.vector.memset(v[64:128, 0:NH:2, :], 0.0)
            ins.then_inc(zeros_ready, 1)
            dve.wait_ge(const_loaded, 16)
            dve.wait_ge(zeros_ready, 4)
            dve.wait_ge(x_loaded, 16)
            dve.sem_inc(x_tile_ready, 1)
            dve.sem_inc(x_ready, 1)
            loop_layers(dve, layer)
            second()

        @block.tensor
        def _(pe):
            def mm(out_, lhsT, rhs, first=True, last=True):
                return nc.tensor.matmul(out_, lhsT, rhs, start=first, stop=last)

            def done(ins, key):
                ins.then_inc(filled[bank_of(key)], 1)

            def transposed(key0, l, n, rows=xhat, wait=True):
                for t in range(TT):
                    if n:
                        pe.wait_ge(xhat_ready if t else xhat_tile_ready, 2 * l + n)
                    for i in range(4):
                        b = psum[:, bank_of((key0, i)), :] if t else fill(pe, (key0, i), l)
                        for c in (0, 1):
                            k = 2 * i + c
                            ins = nc.tensor.transpose(b[:, c * T + t * P:c * T + (t + 1) * P],
                                                      rows[:, t, k * P:(k + 1) * P], ident)
                        if t:
                            done(ins, (key0, i))
                for i in range(4 if wait else 0):
                    after_evacuation(pe, (key0, i), l)

            def transposed_pair(key, l, rows):
                b = fill(pe, key, l)
                for c in (0, 1):
                    for t in range(TT):
                        ins = nc.tensor.transpose(b[:, c * T + t * P:c * T + (t + 1) * P],
                                                  rows[:, t, c * P:(c + 1) * P], ident)
                done(ins, key)

            def diagonal_scores(key, l, keysT, queries, h):
                b = fill(pe, (key, h), l)
                mm(b[:, 0:T], keysT[:, h // 2, 0:P], queries[:, h, :])
                done(mm(b[:, T:DIAG], keysT[:, h // 2, P:T], queries[:, h, P:T]), (key, h))

            def tokens_down(key, l, n, lhs, ks, first, last, free):
                wt = slot_ready(pe, n, l, 4)
                for i in range(4):
                    t, half = divmod(i, 2)
                    for kk in ks:
                        ins = mm(psum[:, bank_of((key, i)), :], lhs[:, kk, t * P:(t + 1) * P],
                                 wt(kk % 4, half * 512, (half + 1) * 512), first and kk == ks[0], last and kk == ks[-1])
                    if last:
                        done(ins, (key, i))
                if free:
                    ins.then_inc(free, 1)

            def second():
                l = L2
                n_slot = [0]

                def skip_slot(kind, s):
                    assert B2_SLOTS[n_slot[0]] == (kind, s)
                    n_slot[0] += 1

                def next_slot(kind, s):
                    assert B2_SLOTS[n_slot[0]] == (kind, s)
                    n_slot[0] += 1
                    return slot_ready(pe, n_slot[0] - 1, l, KC)

                n_unit = [0]

                def next_unit(kind, s, j):
                    n = n_unit[0]
                    assert B2_SLOTS[B2_UNITS[n][0]] == (kind, s) and B2_UNITS[n][1] == j, (n, kind, s, j)
                    n_unit[0] += 1
                    pe.wait_ge(w_split, DEPTH * len(UNITS) + n + 1)
                    return unit_weights2(n, 0), unit_weights2(n, 1)

                def column_unit(b, kind, s, j, t0):
                    wu = next_unit(kind, s, j)
                    for k in range(KC):
                        for i, (a, v) in enumerate(PASSES):
                            ins = mm(b, wu[a][:, k, :], uT_split[:, v, k, t0:S], k + i == 0, k == KC - 1 and i == 2)
                    item = item_of_unit(n_unit[0] - 1)
                    ins.then_inc(filled[bank_of(item)] if item else unit_used, 1)

                def summed(b, lhs, rhs, n_k=KC):
                    for k in range(n_k):
                        ins = mm(b, lhs(k), rhs(k), k == 0, k == n_k - 1)
                    return ins

                pe.wait_ge(siluc_ready, 1)

                def ada_follow(n):
                    if n == 0:
                        pe.wait_ge(early_loaded, 96)
                    after_evacuation(pe, ("ada", n), l)
                    rows = ada_rows[:, n % 2, :]
                    if n in (4, 5, 10, 11):
                        b = fill(pe, ("mR", n), l)
                        done(mm(b, cst2("spread"), rows), ("mR", n))
                    else:
                        i, j = (0, n) if n < 4 else (1, n - 6)
                        b = psum[:, bank_of(("mT", i)), :]
                        if j == 0:
                            fill(pe, ("mT", i), l)
                        for c in range(4):
                            at_ = 8 * j + 2 * c
                            ins = mm(b[:, at_:at_ + 2], rows[:, c * P:(c + 1) * P], cst2("pick"))
                        if j == 3:
                            done(ins, ("mT", i))

                def ada(*ns):
                    for n in ns:
                        wt = next_slot("ada", n)
                        b = fill(pe, ("ada", n), l)
                        for k in range(KC):
                            q = k % 4
                            ins = mm(b[32 * q:32 * q + 32, :], siluc[:, k, :], wt(k, 0, 512), k < 4, k >= 4)
                        done(ins, ("ada", n))

                ada(0, 1)
                ada_follow(0)
                ada(2)
                ada_follow(1)
                ada(3)
                ada_follow(2)
                ada_follow(3)
                transposed("XT", l, 1, wait=False)
                pe.wait_ge(ctx_hat_ready, 1)
                transposed("CT", l, 0, ctx_row, wait=False)
                pe.wait_ge(u_ready, 4)
                skip_slot("mq", 0)
                for i in (0, 1):
                    b = fill(pe, ("mq", i), l)
                    for c in (0, 1):
                        column_unit(b[:, c * T:(c + 1) * T], "mq", 0, 2 * i + c, T)
                ada(4, 5)
                pe.wait_ge(u_ready, 8)
                skip_slot("mk", 0)
                for h in range(NHM):
                    column_unit(fill(pe, ("mk", h), l), "mk", 0, h, 0)
                pe.wait_ge(gate_w_ready, 1)
                b = fill(pe, ("mg", 0), l)
                for st in range(ST):
                    for k in range(KC):
                        for i, (a, v) in enumerate(PASSES):
                            ins = mm(b[:, 16 * st:16 * st + 16], uT_split[:, v, k, st * P:(st + 1) * P],
                                     gate_w_split[:, a, k, :], k + i == 0, k == KC - 1 and i == 2)
                done(ins, ("mg", 0))

                def token_rows(key, s, tiles):
                    skip_slot(key, s)
                    for j in range(4):
                        wu = next_unit(key, s, j)
                        for i, st in enumerate(tiles):
                            item = (key, len(tiles) * s + i)
                            b = fill(pe, item, l) if j == 0 else psum[:, bank_of(item), :]
                            for k in (0, 1):
                                for q, (a, v) in enumerate(PASSES):
                                    ins = mm(b, uT_split[:, v, 2 * j + k, st * P:(st + 1) * P], wu[a][:, k, :],
                                             j + k + q == 0, j == 3 and k == 1 and q == 2)
                            if j == 3:
                                done(ins, item)
                        if j < 3:
                            ins.then_inc(unit_used, 1)

                ada_follow(4)
                ada_follow(5)
                ada(6, 7)
                token_rows("mv", 0, range(ST))
                pe.wait_ge(gate_ready, 1)
                b = fill(pe, ("F", 9), l)
                prefix = cst2("prefix")
                for st in range(ST):
                    terms = [(s_, ones) for s_ in range(st)] + [(st, prefix)]
                    for n, (s_, tri) in enumerate(terms):
                        mm(b[:, 8 * st:8 * st + 4], tri, log_f[:, 2 * s_, :], n == 0, n == len(terms) - 1)
                    whole = [0, 1] if st >= TT else []
                    later = [s_ for s_ in range(st + 1, TT if st < TT else ST)]
                    terms = [(s_, ones) for s_ in whole + later] + [(st, suffix)]
                    for n, (s_, tri) in enumerate(terms):
                        ins = mm(b[:, 8 * st + 4:8 * st + 8], tri, log_f[:, 2 * s_ + 1, :], n == 0,
                                 n == len(terms) - 1)
                done(ins, ("F", 9))
                after_evacuation(pe, ("F", 9), l)
                for d in (0, 1):
                    b = fill(pe, ("GT", d), l)
                    for st in range(ST):
                        ins = nc.tensor.transpose(b[0:NHM, st * P:(st + 1) * P], g_sub[:, st, 4 * d:4 * d + 4], ident)
                    done(ins, ("GT", d))
                ada_follow(6)
                ada_follow(7)
                ada(8, 9)
                token_rows("mv", 1, range(ST))
                ada_follow(8)
                ada_follow(9)
                ada(10, 11)
                token_rows("mo", 0, (2, 3))
                token_rows("mo", 1, (2, 3))
                ada_follow(10)
                ada_follow(11)
                pe.wait_ge(cummax_ready, 1)
                b = fill(pe, ("MR", 0), l)
                for t in range(TT):
                    for d in (0, 1):
                        i = 2 * t + d
                        at_ = P * (1 - d) + t * P
                        ins = nc.tensor.transpose(b[:, 4 * i:4 * i + 4], cummax[d][0][:, at_:at_ + P], ident[0:NHM, 0:NHM])
                done(ins, ("MR", 0))
                for i in (0, 1):
                    after_evacuation(pe, ("mq", i), l)

                def m_scores(h):
                    b = fill(pe, ("MB", h), l)
                    pick_h = ident[0:NHM, h:h + 1].broadcast_to([NHM, P])
                    for d in (0, 1):
                        ins = mm(b[:, d * T:(d + 1) * T], pick_h, cummax[d][0][:, P * (1 - d):P * (1 - d) + T])
                    done(ins, ("MB", h))
                    after_evacuation(pe, ("mk", h), l)
                    for q in (0, 1):
                        b = fill(pe, ("QK", 2 * h + q), l)
                        for c in (0, 1):
                            st = 2 * q + c
                            ins = mm(b[:, c * T:(c + 1) * T], m_kT[:, h, st * P:(st + 1) * P], m_qT[:, h, :])
                        done(ins, ("QK", 2 * h + q))

                def m_outputs(h):
                    after_evacuation(pe, ("QK", 2 * h + 1), l)
                    for d in (0, 1):
                        for t in range(TT):
                            tiles = [0, 1, 2, 3]
                            if (d, t) == (0, 0):
                                tiles = [0, 1, 2]
                            if (d, t) == (1, 1):
                                tiles = [0, 1, 3]
                            b = fill(pe, ("H", 4 * h + 2 * d + t), l)
                            for n, st in enumerate(tiles):
                                ins = mm(b[:, 0:DV + 1], decay[h % 2][:, d, st * T + t * P:st * T + (t + 1) * P],
                                         m_v[:, st, h, 0:DV + 1], n == 0, n == len(tiles) - 1)
                            done(ins, ("H", 4 * h + 2 * d + t))

                for i in range(8):
                    after_evacuation(pe, ("mv", i), l)
                for h in range(NHM + 1):
                    if h < NHM:
                        m_scores(h)
                    if h:
                        m_outputs(h - 1)
                for g in (0, 1):
                    token_rows("dv", g, range(ST))
                    if g == 0:
                        pe.wait_ge(h_normed, 1)
                        transposed("AT", l, 0, h_row)
                    skip_slot("dq", g)
                    skip_slot("dk", g)

                    def project_head(h):
                        column_unit(fill(pe, ("dq", h), l)[:, 0:T], "dq", g, h % 4, T)
                        column_unit(fill(pe, ("dk", h), l), "dk", g, h % 4, 0)

                    def partners(h):
                        after_evacuation(pe, ("dq", h), l)
                        after_evacuation(pe, ("dk", h), l)
                        b = fill(pe, ("rot", h), l)
                        done(mm(b, cst2("partner"), raw[:, h % 2, :]), ("rot", h))

                    project_head(4 * g)
                    partners(4 * g)
                    for h in range(4 * g, 4 * g + 4):
                        pe.wait_ge(qk_ready, h + 1)
                        for i in range(4):
                            t, m = divmod(i, 2)
                            b = fill(pe, ("S", 4 * h + i), l)
                            done(mm(b, d_q[:, 2 * (h % 4) + m, t * P:(t + 1) * P], d_kT[:, h % 4, :]), ("S", 4 * h + i))
                        if h % 4 < 3:
                            project_head(h + 1)
                        for t in range(TT):
                            pe.wait_ge(attn_ready, 2 * h + t + 1)
                            b = fill(pe, ("PT", 2 * h + t), l)
                            for st in range(ST):
                                ins = nc.tensor.transpose(b[:, st * P:(st + 1) * P], probs[:, t, 0, st * P:(st + 1) * P], ident)
                            done(ins, ("PT", 2 * h + t))
                        if h % 4 == 0:
                            for i in range(4):
                                after_evacuation(pe, ("dv", 4 * g + i), l)
                        if h % 4 < 3:
                            partners(h + 1)
                        b = fill(pe, ("O", h), l)
                        for t in range(TT):
                            after_evacuation(pe, ("PT", 2 * h + t), l)
                            for st in range(ST):
                                ins = mm(b[:, t * P:(t + 1) * P], aT[:, t, st * P:(st + 1) * P],
                                         d_v[:, st, (h % 4) * P:(h % 4 + 1) * P], st == 0, st == ST - 1)
                        done(ins, ("O", h))
                for i in range(4):
                    after_evacuation(pe, ("AT", i), l)
                for g in (0, 1):
                    for key in ("pa", "pb", "wa", "wb"):
                        if (g, key) == (0, "wa"):
                            pe.wait_ge(b_normed, 1)
                            transposed("BT", l, 0, b_row)
                        if key in COLUMN_SLOTS:
                            skip_slot(key, g)
                            for i in (0, 1):
                                b = fill(pe, (key, 2 * g + i), l)
                                for c in (0, 1):
                                    column_unit(b[:, c * T:(c + 1) * T], key, g, 2 * i + c, T)
                        else:
                            wt, src = next_slot(key, g), a_outT if key == "wa" else b_outT
                            for i in (0, 1):
                                b = fill(pe, (key, 2 * g + i), l)
                                for c in (0, 1):
                                    ins = summed(b[:, c * T:(c + 1) * T],
                                                 lambda k: wt(k, (2 * i + c) * P, (2 * i + c + 1) * P),
                                                 lambda k: src[:, k, :])
                                done(ins, (key, 2 * g + i))
                        if (g, key) in ((1, "pb"), (1, "wb")):
                            take(pe, (key, 3), l)
                            pe.sem_inc(expert_slot_free, 3 if key == "pb" else 1)
                pe.wait_ge(y_ready, 4)
                for i in range(4):
                    fill(pe, ("Y", i), l)
                for s_ in (0, 1):
                    tokens_down("Y", l, n_slot[0] + s_, yT, range(4 * s_, 4 * s_ + 4), s_ == 0, s_ == 1,
                                None if s_ else expert_slot_free)
                take(pe, ("Y", 3), l)
                pe.sem_inc(expert_slot_free, 1)
                transposed("R", l, 2)
                pe.wait_ge(late_loaded, 64)
                b = fill(pe, ("L", 0), l)
                for t in range(TT):
                    ins = summed(b[:, t * N_EXP:(t + 1) * N_EXP], lambda k: u2T[:, k, t * P:(t + 1) * P],
                                 lambda k: router_w[:, k, :])
                done(ins, ("L", 0))
                pe.wait_ge(mask_ready, 1)
                b = fill(pe, ("PC", 0), l)
                before = cst2("before")
                mm(b[:, 0:N_EXP], before, chosen[:, 0, :])
                mm(b[:, N_EXP:2 * N_EXP], ones, chosen[:, 0, :], True, False)
                done(mm(b[:, N_EXP:2 * N_EXP], before, chosen[:, 1, :], False, True), ("PC", 0))
                b = fill(pe, ("CN", 0), l)
                mm(b[:, 0:N_EXP], ones, chosen[:, 0, :], True, False)
                done(mm(b[:, 0:N_EXP], ones, chosen[:, 1, :], False, True), ("CN", 0))
                pe.wait_ge(gates_ready, 1)
                b = fill(pe, ("gT", 0), l)
                for t in range(TT):
                    ins = nc.tensor.transpose(b[0:N_EXP, t * P:(t + 1) * P], gate_row[:, t, :], ident)
                done(ins, ("gT", 0))
                after_evacuation(pe, ("gT", 0), l)

                def sum_up(i, lhsT, rhs, first=False):
                    return nc.tensor.matmul(psum[:, i, :], lhsT, rhs, start=first, stop=True, skip_group_check=True)

                for i in range(4):
                    t, n = divmod(i, 2)
                    fill(pe, ("YM", i), l)
                    sum_up(i, gT[0:N_EXP, t * P:(t + 1) * P], b2_rows[0:N_EXP, 512 * n:512 * n + 512], True)

                def part_mm(b, xx, lhs, rhs, first=False, last=False):
                    rows = slice(CAP * xx, CAP * (xx + 1))
                    return nc.tensor.matmul(b[rows, :], lhs[:, rows], rhs, start=first, stop=last, skip_group_check=True)

                def pair(it, j):
                    pe.wait_ge(picks_ready, it + 1)
                    for g in (0, 1):
                        b = fill(pe, ("G", g), it)
                        for c in range(4):
                            k = 4 * g + c
                            for t in range(TT):
                                ins = mm(b[:, c * P:(c + 1) * P], xhat[:, t, k * P:(k + 1) * P], pick[:, t, :], t == 0, t == 1)
                        done(ins, ("G", g))
                    banks = [("GLU", 0, 0), ("LIN", 0, D), ("GLU", 1, 512), ("LIN", 1, D + 512)]
                    for key, n, c0 in banks:
                        b = fill(pe, (key, n), it)
                        nc.tensor.matmul(b, pick_e, b1_rows[:, c0:c0 + 512], start=True, stop=False, skip_group_check=True)
                    after_evacuation(pe, ("G", 0), it)
                    for q in range(4):
                        if q == 2:
                            after_evacuation(pe, ("G", 1), it)
                        wt = [expert_slot(pe, it, 2 * q + xx, 2) for xx in (0, 1)]
                        order = ([(k, i) for k in (0, 1) for i in range(4)] if q < 3 else
                                 [(k, i) for i in range(4) for k in (0, 1)])
                        for k, i in order:
                            key, n, c0 = banks[i]
                            end_of_bank = q == 3 and k == 1
                            for xx in (0, 1):
                                ins = part_mm(psum[:, bank_of((key, n)), :], xx, xgT[:, 2 * q + k, :],
                                              wt[xx](k, c0, c0 + 512), last=end_of_bank)
                                if xx and end_of_bank:
                                    done(ins, (key, n))
                                elif (k, i) == (1, 3):
                                    ins.then_inc(expert_slot_free, 1)
                    b = fill(pe, ("ST", 0), it)
                    nc.tensor.transpose(b[:, 0:P], pick_gated[:, 0, :], ident).then_inc(expert_slot_free, 1)
                    done(nc.tensor.transpose(b[:, P:T], pick_gated[:, 1, :], ident), ("ST", 0))

                    def hidden_transposed(n):
                        pe.wait_ge(hidden_ready, 2 * it + (n + 1))
                        b = fill(pe, ("AT2", n), it)
                        for c in range(4):
                            ins = nc.tensor.transpose(b[:, c * P:(c + 1) * P], act_[n][:, c * P:(c + 1) * P], ident)
                        done(ins, ("AT2", n))

                    hidden_transposed(0)
                    after_evacuation(pe, ("AT2", 0), it)
                    for n in (0, 1):
                        fill(pe, ("OUT", n), it)
                    for q in (0, 1):
                        wt = [expert_slot(pe, it, 8 + 2 * q + xx, 4) for xx in (0, 1)]
                        if q:
                            after_evacuation(pe, ("AT2", 1), it)
                        order = [(k, n) for k in range(4) for n in (0, 1)] if q == 0 else [(k, n) for n in (0, 1) for k in range(4)]
                        for k, n in order:
                            if (q, k, n) == (0, 2, 0):
                                hidden_transposed(1)
                            for xx in (0, 1):
                                ins = part_mm(psum[:, bank_of(("OUT", n)), :], xx, actT[:, 4 * q + k, :],
                                              wt[xx](k, 512 * n, 512 * n + 512), q + k == 0, q + k == 4)
                                if xx and q and k == 3:
                                    done(ins, ("OUT", n))
                                elif (k, n) == (3, 1):
                                    ins.then_inc(expert_slot_free, 1)
                    after_evacuation(pe, ("ST", 0), it)
                    for n in (0, 1):
                        after_evacuation(pe, ("OUT", n), it)
                        for t in range(TT):
                            ins = sum_up(2 * t + n, spread_T[:, t * P:(t + 1) * P], out_sb[:, 512 * n:512 * n + 512])
                            if (n, t) == (0, 0):
                                ins.then_inc(expert_slot_free, 1)
                    ins.then_inc(combined, 1)

                over_pairs(pe, pair)

            def layer(l):
                def column_unit(b, wu):
                    for k in range(KC):
                        for i, (a, v) in enumerate(PASSES):
                            ins = mm(b, wu[a][:, k, :], hT_split[:, v, k, :], k + i == 0, k == KC - 1 and i == 2)
                    return ins

                def project(s):
                    for i in (2 * s, 2 * s + 1):
                        b = fill(pe, ("s", i), l)
                        for j in (0, 1):
                            n = 2 * i + j
                            pe.wait_ge(w_split, l * len(UNITS) + (n + 1))
                            wu = [unit_weights(n, v) for v in (0, 1)]
                            if i not in ROW_SLICES:
                                ins = column_unit(b[:, j * T:(j + 1) * T], wu)
                            else:
                                for c in (0, 1):
                                    for k in range(4):
                                        for q, (a, v) in enumerate(PASSES):
                                            ins = nc.tensor.matmul(
                                                b[:, c * T:(c + 1) * T], hT_split[:, v, 4 * j + k, c * P:(c + 1) * P],
                                                wu[a][:, k, :], start=j + c + k + q == 0, stop=j == 1 and k == 3 and q == 2,
                                                skip_group_check=True)
                            ins.then_inc(filled[bank_of(("s", i))] if j else unit_used, 1)

                transposed("T", l, 1)
                for s in range(3):
                    project(s)
                after_evacuation(pe, ("s", 2), l)
                after_evacuation(pe, ("s", 3), l)
                for h in range(NH):
                    diagonal_scores("Z", l, kT, q_z, h)
                project(3)
                pe.wait_ge(rq_ready, l + 1)
                transposed_pair(("RQ", 0), l, rq)
                pe.wait_ge(rk_ready, l + 1)
                transposed_pair(("RK", 0), l, rk)
                project(4)
                after_evacuation(pe, ("RQ", 0), l)
                after_evacuation(pe, ("RK", 0), l)
                for h in range(NH):
                    diagonal_scores("RS", l, rkT, rq_z, h)
                project(5)
                pe.wait_ge(sb_soft, l + 1)
                for h in range(NH):
                    b = fill(pe, ("I", h), l)
                    mm(b[:, 0:T], suffix, soft[:, h, 0:T], True, False)
                    mm(b[:, P:T], ones, soft[:, h, T:DIAG], False, True)
                    done(mm(b[:, T:DIAG], suffix, soft[:, h, T:DIAG]), ("I", h))
                after_evacuation(pe, ("s", 7), l)
                b = fill(pe, ("RO", 0), l).rearrange("p (t h e) -> p t h e", t=TT, h=NH)
                for h in range(NH):
                    after_evacuation(pe, ("RS", h), l)
                    cut = slice(h * HD, (h + 1) * HD)
                    mm(b[:, 0, h, :], r_scores[:, h, 0:P], rv[:, 0, cut])
                    mm(b[:, 1, h, :], r_scores[:, h, P:T], rv[:, 0, cut], True, False)
                    ins = mm(b[:, 1, h, :], r_scores[:, h, T:DIAG], rv[:, 1, cut], False, True)
                done(ins, ("RO", 0))
                pe.wait_ge(sb_attn, l + 1)
                after_evacuation(pe, ("s", 4), l)
                for c in (0, 1):
                    b = fill(pe, ("SB", c), l)
                    for h in (2 * c, 2 * c + 1):
                        rows = slice((h % 2) * HD, (h % 2 + 1) * HD)
                        cut = slice(h * HD, (h + 1) * HD)
                        mm(b[rows, 0:T], v_sb[:, 0, cut], z[:, h, 0:T], True, False)
                        ins = mm(b[rows, P:T], v_sb[:, 1, cut], z[:, h, T:DIAG], False, True)
                    done(ins, ("SB", c))
                for c in (0, 1):
                    after_evacuation(pe, ("SB", c), l)
                for i in range(4):
                    fill(pe, ("M", i), l)
                tokens_down("M", l, 6, catT, (2, 3), True, False, None)
                pe.wait_ge(conf_ready, l + 1)
                b = fill(pe, ("CM", 0), l)
                mm(b[:, 0:T], ones, conf[:, 0, :], True, False)
                done(mm(b[:, 0:T], ones, conf[:, 1, :], False, True), ("CM", 0))
                pe.wait_ge(conf_sq_ready, l + 1)
                b = fill(pe, ("CV", 0), l)
                mm(b[:, 0:T], ones, conf_sq[:, 0, :], True, False)
                done(mm(b[:, 0:T], ones, conf_sq[:, 1, :], False, True), ("CV", 0))
                pe.wait_ge(sc_cat, l + 1)
                tokens_down("M", l, 7, catT, (6, 7), False, False, None)
                pe.wait_ge(ret_ready, l + 1)
                transposed_pair(("RT", 0), l, ret)
                pe.wait_ge(conf_cat, l + 1)
                tokens_down("M", l, 6, catT, (0, 1), False, False, slot_free)
                after_evacuation(pe, ("RT", 0), l)
                tokens_down("M", l, 7, catT, (4, 5), False, True, None)
                transposed("F", l, 2)
                for n in range(MIX_UNITS, len(UNITS)):
                    slot, j = UNITS[n]
                    kind, g = LAYER_SLOTS[slot]
                    pe.wait_ge(w_split, l * len(UNITS) + (n + 1))
                    wu = [unit_weights(n, v) for v in (0, 1)]
                    last = item_of_layer_unit(n) is not None
                    if kind == "up":
                        u, c = divmod(j, 2)
                        b = fill(pe, ("U", 2 * g + u), l) if c == 0 else psum[:, bank_of(("U", 2 * g + u)), :]
                        ins = column_unit(b[:, c * T:(c + 1) * T], wu)
                        if last:
                            done(ins, ("U", 2 * g + u))
                    else:
                        kk = 4 * g + j
                        if j == 0:
                            pe.wait_ge(ff_ready, l * 11 + min(2 * g + 2, 11))
                        for i in range(4):
                            if kk == 0:
                                fill(pe, ("D", i), l)
                            t, half = divmod(i, 2)
                            for p_, (a, v) in enumerate(PASSES):
                                ins = mm(psum[:, bank_of(("D", i)), :], ffT_split[:, v, kk % 8, t * P:(t + 1) * P],
                                         wu[a][:, 0, half * 512:(half + 1) * 512], kk + p_ == 0, kk == FFC - 1 and p_ == 2)
                            if last:
                                done(ins, ("D", i))
                    if not last:
                        ins.then_inc(unit_used, 1)

            for b in range(8):
                pe.sem_inc(evacuated[b], 1)
            pe.wait_ge(const_loaded, 16)
            pe.wait_ge(zeros_ready, 4)
            loop_layers(pe, layer)
            second()


def pack_cols(inputs):
    def chunks(a):
        a = np.asarray(a)
        a = a.reshape(DEPTH, -1, a.shape[-1] // P, P)
        return a.transpose(0, 3, 1, 2).reshape(DEPTH, P, -1)

    names = ("norm_mix_pre", "conf_dw_w", "conf_dw_b", "conf_ln_g", "conf_ln_b", "sc_conv_w", "norm_ffn_pre",
             "ffn_conv_w")
    return np.ascontiguousarray(np.concatenate([chunks(inputs[n]) for n in names], axis=2))


def pack_cols2(inputs):
    ada = np.asarray(inputs["ada_b_2"])[0].reshape(6, D)[[0, 1, 3, 4]].reshape(-1)
    flat = np.concatenate([np.asarray(inputs["norm1_g_2"])[0], np.asarray(inputs["norm2_g_2"])[0], ada])
    return np.ascontiguousarray(flat.reshape(-1, P).T)


def pack_c(inputs):
    both = np.stack([np.asarray(inputs["c_2"])[0], np.asarray(inputs["c_ctx_2"])])
    return np.ascontiguousarray(both.reshape(2, KC, P).transpose(2, 1, 0).reshape(P, 2 * KC))


PACKED = ("norm_mix_pre", "norm_ffn_pre", "conf_dw_w", "conf_dw_b", "conf_ln_g", "conf_ln_b", "sc_conv_w", "ffn_conv_w",
          "c_2", "c_ctx_2", "norm1_g_2", "norm2_g_2")


def kernel(**inputs):
    import concourse.bacc as bacc
    from concourse.bass_utils import run_bass_kernel_spmd

    nc = bacc.Bacc("TRN2", target_bir_lowering=False, num_devices=1)
    arrays = {n: np.ascontiguousarray(a) for n, a in inputs.items() if n not in PACKED}
    arrays.update(const=shape_constants(), cols=pack_cols(inputs), const2=shape_constants2(), cols2=pack_cols2(inputs),
                  cT=pack_c(inputs))
    w = {n: nc.dram_tensor(f"{n}_dram", a.shape, mybir.dt.from_np(a.dtype), kind="ExternalInput").ap()
         for n, a in arrays.items()}
    out = nc.dram_tensor("out_dram", (T, D), F32, kind="ExternalOutput").ap()
    build_program(nc, w, out)
    result = run_bass_kernel_spmd(nc, [{f"{n}_dram": a for n, a in arrays.items()}], core_ids=[0])
    return np.asarray(result.results[0]["out_dram"]).reshape(inputs["x"].shape)
```
